# Optimizing a Trainium2 kernel written in Bass

```python
import jax, jax.numpy as jnp
from jax import lax
import numpy as np

D_MODEL = 1024
BATCH = 1
SEQ = 2048
DEPTH = 1

MIX_WIDTH = D_MODEL
HGRN_WIDTH = D_MODEL // 2
HGRN_EXPAND = 128
HGRN_HEADS = HGRN_WIDTH // HGRN_EXPAND
HGRN_DV = HGRN_WIDTH // HGRN_HEADS
HGRN_CHUNK = 64
FOX_WIDTH = MIX_WIDTH - HGRN_WIDTH
FOX_HEAD_DIM = 64
FOX_HEADS = FOX_WIDTH // FOX_HEAD_DIM
Q_BLOCK = 128
D_FF = 4 * D_MODEL
NORM_EPS = 1e-6
SPLIT_SIZES = (HGRN_WIDTH, HGRN_WIDTH, HGRN_WIDTH, HGRN_WIDTH,
               FOX_WIDTH, FOX_WIDTH, FOX_WIDTH, FOX_HEADS)
IN_COLS = sum(SPLIT_SIZES)
SPLIT_POINTS = tuple(int(v) for v in np.cumsum(SPLIT_SIZES)[:-1])

kernel_name = "hymba_hgrn2_fox_hybrid"

def rms_norm(x, w):
    xf = x.astype(jnp.float32)
    y = xf * lax.rsqrt(jnp.mean(xf * xf, axis=-1, keepdims=True) + NORM_EPS)
    return (y * w.astype(jnp.float32)).astype(x.dtype)

def layer_lower_bounds(lower_bounds):
    p = jax.nn.softmax(lower_bounds.astype(jnp.float32), axis=0)
    c = jnp.cumsum(p, axis=0)
    return c - c[0:1]

def hgrn2_mixer(q, f_pre, i_in, g, lb, norm_w):
    B, S, _ = q.shape
    nc = S // HGRN_CHUNK
    f = lb + (1.0 - lb) * jax.nn.sigmoid(f_pre.astype(jnp.float32))
    log_f = jnp.log(f)
    k = 1.0 - f
    qf = q.astype(jnp.float32) * (HGRN_EXPAND ** -0.5)
    vf = i_in.astype(jnp.float32)

    def to_chunks(t, d):
        t = t.reshape(B, nc, HGRN_CHUNK, HGRN_HEADS, d)
        return jnp.transpose(t, (1, 0, 3, 2, 4))

    qc = to_chunks(qf, HGRN_EXPAND)
    kc = to_chunks(k, HGRN_EXPAND)
    vc = to_chunks(vf, HGRN_DV)
    lfc = to_chunks(log_f, HGRN_EXPAND)
    causal = jnp.tril(jnp.ones((HGRN_CHUNK, HGRN_CHUNK), dtype=bool))

    def step(state, inp):
        qb, kb, vb, lfb = inp
        b = jnp.cumsum(lfb, axis=2)
        inter = jnp.einsum('bhtk,bhkv->bhtv', qb * jnp.exp(b), state)
        diff = b[:, :, :, None, :] - b[:, :, None, :, :]
        decay = jnp.exp(jnp.where(causal[None, None, :, :, None], diff, -jnp.inf))
        a = jnp.einsum('bhtk,bhsk,bhtsk->bhts', qb, kb, decay)
        intra = jnp.einsum('bhts,bhsv->bhtv', a, vb)
        b_last = b[:, :, -1:, :]
        new_state = (jnp.exp(b_last[:, :, 0, :])[..., None] * state
                     + jnp.einsum('bhsk,bhsv->bhkv', kb * jnp.exp(b_last - b), vb))
        return new_state, inter + intra

    s0 = jnp.zeros((B, HGRN_HEADS, HGRN_EXPAND, HGRN_DV), jnp.float32)
    _, o = lax.scan(step, s0, (qc, kc, vc, lfc))
    o = jnp.transpose(o, (1, 0, 3, 2, 4)).reshape(B, S, HGRN_HEADS, HGRN_DV)
    o = rms_norm(o, norm_w)
    gate = jax.nn.silu(g.astype(jnp.float32)).reshape(B, S, HGRN_HEADS, HGRN_DV)
    return (o * gate).reshape(B, S, HGRN_WIDTH).astype(q.dtype)

def fox_mixer(q, k, v, f_logit, f_bias, q_norm_w, k_norm_w):
    B, S, _ = q.shape

    def heads(t):
        return jnp.transpose(t.reshape(B, S, FOX_HEADS, FOX_HEAD_DIM), (0, 2, 1, 3)).astype(jnp.float32)

    qh = rms_norm(heads(q), q_norm_w) * (FOX_HEAD_DIM ** -0.5)
    kh = rms_norm(heads(k), k_norm_w)
    vh = heads(v)
    log_f = jax.nn.log_sigmoid(f_logit.astype(jnp.float32) + f_bias.astype(jnp.float32))
    c = jnp.cumsum(jnp.transpose(log_f, (0, 2, 1)), axis=-1)
    kpos = jnp.arange(S)

    def block(bi):
        start = bi * Q_BLOCK
        qb = lax.dynamic_slice_in_dim(qh, start, Q_BLOCK, axis=2)
        cb = lax.dynamic_slice_in_dim(c, start, Q_BLOCK, axis=2)
        s = jnp.einsum('bhqd,bhkd->bhqk', qb, kh) + (cb[..., :, None] - c[..., None, :])
        qpos = start + jnp.arange(Q_BLOCK)
        mask = kpos[None, :] <= qpos[:, None]
        p = jax.nn.softmax(jnp.where(mask[None, None], s, -jnp.inf), axis=-1)
        return jnp.einsum('bhqk,bhkd->bhqd', p, vh)

    o = lax.map(block, jnp.arange(S // Q_BLOCK))
    o = jnp.transpose(o, (1, 0, 3, 2, 4)).reshape(B, S, FOX_WIDTH)
    return o.astype(q.dtype)

def setup_inputs(seed: int = 0) -> dict:
    key = jax.random.key(seed)
    ks = jax.random.split(key, 12)
    f32 = jnp.float32
    x = jax.random.normal(ks[0], (BATCH, SEQ, D_MODEL), f32)
    lower_bounds = 0.1 * jax.random.normal(ks[1], (DEPTH, HGRN_WIDTH), f32)
    norm1_w = 1.0 + 0.02 * jax.random.normal(ks[2], (DEPTH, D_MODEL), f32)
    w_in = jax.random.normal(ks[3], (DEPTH, D_MODEL, IN_COLS), f32) * D_MODEL ** -0.5
    fox_f_bias = jax.random.uniform(ks[4], (DEPTH, FOX_HEADS), f32, minval=0.0, maxval=3.0)
    q_norm_w = 1.0 + 0.02 * jax.random.normal(ks[5], (DEPTH, FOX_HEAD_DIM), f32)
    k_norm_w = 1.0 + 0.02 * jax.random.normal(ks[6], (DEPTH, FOX_HEAD_DIM), f32)
    hgrn_norm_w = 1.0 + 0.02 * jax.random.normal(ks[7], (DEPTH, HGRN_DV), f32)
    w_out = jax.random.normal(ks[8], (DEPTH, MIX_WIDTH, D_MODEL), f32) * MIX_WIDTH ** -0.5
    norm2_w = 1.0 + 0.02 * jax.random.normal(ks[9], (DEPTH, D_MODEL), f32)
    w_up = jax.random.normal(ks[10], (DEPTH, D_MODEL, D_FF), f32) * D_MODEL ** -0.5
    w_down = jax.random.normal(ks[11], (DEPTH, D_FF, D_MODEL), f32) * D_FF ** -0.5
    return {"x": x, "lower_bounds": lower_bounds, "norm1_w": norm1_w, "w_in": w_in,
            "fox_f_bias": fox_f_bias, "q_norm_w": q_norm_w, "k_norm_w": k_norm_w,
            "hgrn_norm_w": hgrn_norm_w, "w_out": w_out, "norm2_w": norm2_w,
            "w_up": w_up, "w_down": w_down}

def reference(x, lower_bounds, norm1_w, w_in, fox_f_bias, q_norm_w, k_norm_w,
              hgrn_norm_w, w_out, norm2_w, w_up, w_down):
    lbs = layer_lower_bounds(lower_bounds)
    for l in range(DEPTH):
        h = rms_norm(x, norm1_w[l])
        proj = jnp.einsum('bsd,dc->bsc', h, w_in[l])
        hq, hf, hi, hg, fq, fk, fv, ff = jnp.split(proj, SPLIT_POINTS, axis=-1)
        o_a = hgrn2_mixer(hq, hf, hi, hg, lbs[l], hgrn_norm_w[l])
        o_b = fox_mixer(fq, fk, fv, ff, fox_f_bias[l], q_norm_w[l], k_norm_w[l])
        mix = jnp.concatenate([o_a, o_b], axis=-1)
        x = x + jnp.einsum('bsc,cd->bsd', mix, w_out[l])
        h2 = rms_norm(x, norm2_w[l])
        u = jax.nn.relu(jnp.einsum('bsd,df->bsf', h2, w_up[l]))
        x = x + jnp.einsum('bsf,fd->bsd', u * u, w_down[l])
    return x


_drawn_inputs = setup_inputs


def setup_inputs(seed=0):
    import zlib

    import numpy as np

    out = dict(_drawn_inputs(seed))
    spreads = {}
    factors = {'q_norm_w': 8.0, 'k_norm_w': 8.0, 'hgrn_norm_w': 6.681, 'norm2_w': 3.372}
    for name, (base, spread) in spreads.items():
        noise = np.random.default_rng([zlib.crc32(name.encode()), seed]).standard_normal(out[name].shape)
        drawn = base * np.exp(spread * noise) if base else spread * noise
        out[name] = __import__('jax').numpy.asarray(drawn.astype(out[name].dtype))
    for name, factor in factors.items():
        out[name] = (out[name] * factor).astype(out[name].dtype)
    return out
```

```python
from contextlib import ExitStack

import concourse.bass as bass
from concourse import mybir

F32 = mybir.dt.float32
F32R = mybir.dt.float32r
ALU = mybir.AluOpType
ACT = mybir.ActivationFunctionType
AX = mybir.AxisListType

P = 128
BANK = 512
S = 2048
DM = 1024
DT = DM // P
TT = S // P
HH = 4
FH = 8
FD = 64
DFF = 4 * DM
EPS = 1e-6
NT = 5
V_, FQ_, FK_, FV_, G_ = range(NT)


class Ring:

    def __init__(self, slots):
        self.slots = slots

    def slot(self, n):
        return n % self.slots

    def landed(self, n):
        return 16 * (n // self.slots + 1)


def wait_alone(eng, sem, value, passed):
    eng.wait_ge(sem, value)
    eng.sem_inc(passed, 1)


def three_pass(nc, out, l_hi, l_lo, r_hi, r_lo, first, last):
    nc.tensor.matmul(out, l_hi, r_hi, start=first, stop=False)
    nc.tensor.matmul(out, l_hi, r_lo, start=False, stop=False)
    return nc.tensor.matmul(out, l_lo, r_hi, start=False, stop=last)


def constants(nc, ctx, inp):
    def sb(name, shape, dt=F32):
        return ctx.enter_context(nc.sbuf_tensor(name, shape, dt))

    c = {
        "ident": sb("ident", [P, P]),
        "neg_half": sb("neg_half", [P, FH]),
        "eps_dm": sb("eps_dm", [P, 1]),
        "eps_fd": sb("eps_fd", [P, FH]),
        "eps_p": sb("eps_p", [P, 1]),
        "lb": sb("lb", [P, HH]),
        "one_minus_lb": sb("one_minus_lb", [P, HH]),
        "ff_logit": sb("ff_logit", [P, TT, FH]),
        "hgrn_w": sb("hgrn_w", [P, P]),
        "qk_w": sb("qk_w", [P, 2, FD]),
    }
    small_in = ctx.enter_context(nc.semaphore("small_in"))
    pool_step = ctx.enter_context(nc.semaphore("const_pool_step"))
    act_step = ctx.enter_context(nc.semaphore("const_act_step"))
    lb_step = ctx.enter_context(nc.semaphore("const_lb_step"))
    lb_work = sb("lb_work", [P, 3, HH])
    with nc.Block() as block:
        @block.sync
        def _(sp):
            with nc.allow_non_contiguous_dma(reason="512 values"):
                sp.dma_start(c["lb"][:], inp["lower_bounds"].rearrange("l (h p) -> p (l h)", p=P)).then_inc(small_in, 16)
            sp.dma_start(c["hgrn_w"][:], bcast(inp["hgrn_norm_w"], P)).then_inc(small_in, 16)
            sp.dma_start(c["qk_w"][:, 0, :], bcast(inp["q_norm_w"], FD)).then_inc(small_in, 16)
            sp.dma_start(c["qk_w"][:, 1, :], bcast(inp["k_norm_w"], FD)).then_inc(small_in, 16)
            sp.wait_ge(small_in, 64)

        @block.gpsimd
        def _(pool):
            nc.gpsimd.memset(c["neg_half"][:], -0.5)
            nc.gpsimd.memset(c["eps_dm"][:], DM * EPS)
            nc.gpsimd.memset(c["eps_fd"][:], FD * EPS)
            nc.gpsimd.memset(c["eps_p"][:], P * EPS)
            nc.gpsimd.memset(c["ident"][:], 0.0).then_inc(pool_step, 1)
            pool.wait_ge(pool_step, 1)
            nc.gpsimd.affine_select(out=c["ident"][:], in_=c["ident"][:], compare_op=ALU.not_equal, fill=1.0,
                                    base=0, pattern=[[-1, P]], channel_multiplier=1).then_inc(pool_step, 1)
            pool.wait_ge(pool_step, 2)

        @block.vector
        def _(dve):
            dve.wait_ge(small_in, 64)
            nc.vector.tensor_tensor(lb_work[:, 0, :], c["lb"][:], c["lb"][:], ALU.subtract).then_inc(lb_step, 1)
            nc.vector.tensor_scalar(c["qk_w"][:, 0, :], c["qk_w"][:, 0, :], -1.0, None, ALU.mult)
            nc.vector.tensor_scalar(c["qk_w"][:, 1, :], c["qk_w"][:, 1, :], float(FD) ** 0.5, None, ALU.mult)
            nc.vector.tensor_scalar(c["hgrn_w"][:], c["hgrn_w"][:], float(P) ** 0.5, None, ALU.mult)
            dve.wait_ge(act_step, 1)
            nc.vector.reciprocal(lb_work[:, 2, :], lb_work[:, 1, :]).then_inc(lb_step, 1)
            dve.wait_ge(lb_step, 2)
            nc.vector.tensor_tensor(lb_work[:, 0, :], lb_work[:, 1, :], lb_work[:, 2, :], ALU.mult).then_inc(lb_step, 1)
            dve.wait_ge(lb_step, 3)
            nc.vector.tensor_tensor(c["lb"][:], lb_work[:, 0, :], lb_work[:, 0, :], ALU.subtract).then_inc(lb_step, 1)
            dve.wait_ge(lb_step, 4)
            nc.vector.tensor_scalar(c["one_minus_lb"][:], c["lb"][:], -1.0, 1.0, ALU.mult, ALU.add).then_inc(lb_step, 1)
            dve.wait_ge(lb_step, 5)

        @block.scalar
        def _(act):
            act.wait_ge(lb_step, 1)
            nc.scalar.activation(lb_work[:, 1, :], lb_work[:, 0, :], ACT.Exp).then_inc(act_step, 1)
            act.wait_ge(act_step, 1)
    return c


def bcast(row, n):
    return bass.AP(tensor=row.tensor, offset=row.offset, ap=[[0, P], [1, n]])


def project(nc, ctx, c, inp, tok_out, ch_out):
    NW = 16
    NRAW = 2
    CH = 7
    COLS = [1024, 2048, 2560, 3072, 1536, 0, 512]
    FF = 3584
    raw_ring, x_ring = Ring(NRAW), Ring(2)

    def sem(name):
        return ctx.enter_context(nc.semaphore("p_" + name))

    x_in = [sem(f"x_in{k}") for k in range(2)]
    raw_in = [sem(f"raw_in{k}") for k in range(NRAW)]
    stored = [sem(f"stored{k}") for k in range(4)]
    w1_in, ff_in, squared, rstd_step, scaled, tp_ready = (sem(n) for n in ("w1_in", "ff_in", "squared", "rstd_step", "scaled", "tp_ready"))
    ht_hi_done, ht_lo_done, w_hi_done, w_lo_done, w_used = (sem(n) for n in ("ht_hi", "ht_lo", "w_hi", "w_lo", "w_used"))
    ffw_hi_done, ffw_lo_done, w1_scaled = sem("ffw_hi"), sem("ffw_lo"), sem("w1_scaled")
    acc_ready, banks_free, act_out, summed, qk_rstd, dve_step = (
        sem(n) for n in ("acc_ready", "banks_free", "act_out", "summed", "qk_rstd", "dve_step"))
    with ExitStack() as own:
        def sb(name, shape, dt=F32):
            return own.enter_context(nc.sbuf_tensor("p_" + name, shape, dt))

        ht_hi, ht_lo = sb("ht_hi", [P, DT, S], F32R), sb("ht_lo", [P, DT, S], F32R)
        w_hi, w_lo = sb("w_hi", [P, NW, BANK], F32R), sb("w_lo", [P, NW, BANK], F32R)
        raw = sb("raw", [P, NRAW, BANK])
        stage = sb("stage", [P, 4, BANK])
        xt = sb("xt", [P, 2, DM])
        w1 = sb("w1", [P, DM])
        work = sb("work", [P, BANK])
        ff_raw, ff_hi, ff_lo = sb("ff_raw", [P, DT, FH]), sb("ff_hi", [P, DT, FH], F32R), sb("ff_lo", [P, DT, FH], F32R)
        ss, rstd = sb("ss", [P, 2, 2]), sb("rstd", [P, 2])
        qss, qrs = sb("qss", [P, 2, FH]), sb("qrs", [P, 2, FH])
        acc = own.enter_context(nc.psum_tensor("p_acc", [P, 4, BANK], F32))
        tp = own.enter_context(nc.psum_tensor("p_tp", [P, 4, BANK], F32))
        tpv = tp[:].rearrange("p (u b) (d t) -> p u (b d) t", u=2, t=P)
        x_tiles = inp["x"].rearrange("b (t p) d -> (b t) p d", p=P)
        w_in = inp["w_in"].rearrange("l (d p) n -> p (l d) n", p=P)
        block = own.enter_context(nc.Block())

        def each_group(eng, body):
            with eng.Fori(0, 3) as i:
                for j in range(4):
                    body(i, j, False)
            for j in range(4):
                body(3, j, True)

        def late_pieces(ch, j):
            if ch + 1 >= CH:
                return []
            m = 8 * (ch + 1)
            return {0: [m, m + 1], 1: [m + 2, m + 3], 2: [m + 4, m + 5], 3: [], 4: [m + 6, m + 7]}[j]

        @block.sync
        def _(sp):
            def load_x(t, slot):
                sp.dma_start(xt[:, slot, :], x_tiles[t]).then_inc(x_in[slot], 16)

            def load_piece(m):
                ch, d = divmod(m, 8)
                if m >= NRAW:
                    sp.wait_ge(w_lo_done, m - NRAW + 1)
                sp.dma_start(raw[:, m % NRAW, :], w_in[:, d, COLS[ch]:COLS[ch] + BANK]).then_inc(raw_in[m % NRAW], 16)

            load_x(0, 0)
            sp.dma_start(w1[:], bcast(inp["norm1_w"], DM)).then_inc(w1_in, 16)
            load_x(1, 1)
            for m in range(8):
                load_piece(m)
            sp.dma_start(ff_raw[:], w_in[:, :, FF:FF + FH]).then_inc(ff_in, 16)
            for ch in range(CH):
                def body(i, j, last):
                    if ch == 0 and not (last and j >= 2):
                        sp.wait_ge(tp_ready, 4 * i + j + 1)
                        load_x(4 * i + j + 2, j % 2)
                    for m in (late_pieces(ch, j) if last else []):
                        load_piece(m)
                    sp.wait_ge(banks_free, 4 + 16 * ch + 4 * i + j + 1)
                    if ch < NT:
                        dst = tok_out[ch, 4 * i + j]
                    else:
                        dst = ch_out[ch - NT, i, :, j * BANK:(j + 1) * BANK]
                    sp.dma_start(dst, stage[:, j, :]).then_inc(stored[j], 16)
                each_group(sp, body)
                for m in late_pieces(ch, 4):
                    load_piece(m)
            for j in range(4):
                sp.wait_ge(stored[j], 16 * 4 * CH)

        @block.gpsimd
        def _(pool):
            steps = [0]

            def tile_rstd(t, slot):
                pool.wait_ge(squared, 2 * t + 2)
                nc.gpsimd.tensor_tensor(rstd[:, slot:slot + 1], ss[:, slot, 0:1], ss[:, slot, 1:2],
                                        ALU.add).then_inc(rstd_step, 1)
                pool.wait_ge(rstd_step, 3 * t + 1)
                nc.gpsimd.tensor_tensor(rstd[:, slot:slot + 1], rstd[:, slot:slot + 1], c["eps_dm"][:],
                                        ALU.add).then_inc(rstd_step, 1)
                pool.wait_ge(rstd_step, 3 * t + 2)
                nc.gpsimd.tensor_tensor(rstd[:, slot:slot + 1], rstd[:, slot:slot + 1], c["neg_half"][:, 0:1],
                                        ALU.pow).then_inc(rstd_step, 1)

            def cut_lo(m):
                s = m % NW
                pool.wait_ge(w_hi_done, m + 1)
                nc.gpsimd.tensor_tensor(w_lo[:, s, :], raw[:, m % NRAW, :], w_hi[:, s, :].bitcast(F32),
                                        ALU.subtract).then_inc(w_lo_done, 1)

            tile_rstd(0, 0)
            tile_rstd(1, 1)
            for m in range(8):
                cut_lo(m)
            pool.wait_ge(ffw_hi_done, 1)
            nc.gpsimd.tensor_tensor(ff_lo[:], ff_raw[:], ff_hi[:].bitcast(F32), ALU.subtract).then_inc(ffw_lo_done, 1)
            for ch in range(CH):
                def body(i, j, last):
                    if ch == 0 and not (last and j >= 2):
                        tile_rstd(4 * i + j + 2, j % 2)
                    if ch in (FQ_, FK_):
                        n = 16 * (ch - 1) + 4 * i + j
                        pool.wait_ge(summed, n + 1)
                        nc.gpsimd.tensor_tensor(qrs[:, j % 2, :], qss[:, j % 2, :], c["eps_fd"][:],
                                                ALU.add).then_inc(qk_rstd, 1)
                        pool.wait_ge(qk_rstd, 2 * n + 1)
                        nc.gpsimd.tensor_tensor(qrs[:, j % 2, :], qrs[:, j % 2, :], c["neg_half"][:],
                                                ALU.pow).then_inc(qk_rstd, 1)
                    for m in (late_pieces(ch, j) if last else []):
                        cut_lo(m)
                each_group(pool, body)
                for m in late_pieces(ch, 4):
                    cut_lo(m)

        @block.scalar
        def _(act):
            def square_tile(i, j):
                act.wait_ge(x_in[j % 2], 16 * (2 * i + j // 2 + 1))
                for half in range(2):
                    act.wait_ge(squared, 2 * (4 * i + j) + half)
                    nc.scalar.activation(work[:], xt[:, j % 2, half * BANK:(half + 1) * BANK], ACT.Square,
                                         accum_out=ss[:, j % 2, half:half + 1]).then_inc(squared, 1)

            def tile_hi(t, slot):
                act.wait_ge(tp_ready, t + 1)
                nc.scalar.copy(ht_hi[:, :, bass.ds(t * P, P)], tpv[:, slot]).then_inc(ht_hi_done, 1)

            def cut_hi(m):
                act.wait_ge(raw_in[m % NRAW], raw_ring.landed(m))
                if m >= NW:
                    ch, d = divmod(m - NW, DT)
                    if d == DT - 1:
                        act.wait_ge(acc_ready, 16 * (ch + 1))
                    else:
                        act.wait_ge(w_used, (DT - 1) * ch + d + 1)
                nc.scalar.copy(w_hi[:, m % NW, :], raw[:, m % NRAW, :]).then_inc(w_hi_done, 1)

            square_tile(0, 0)
            square_tile(0, 1)
            tile_hi(0, 0)
            for m in range(8):
                cut_hi(m)
            act.wait_ge(ff_in, 16)
            nc.scalar.copy(ff_hi[:], ff_raw[:]).then_inc(ffw_hi_done, 1)
            for ch in range(CH):
                def body(i, j, last):
                    n = 16 * ch + 4 * i + j
                    if ch == 0:
                        if not (last and j == 3):
                            tile_hi(4 * i + j + 1, (j + 1) % 2)
                        if not (last and j >= 2):
                            square_tile(i + (j + 2) // 4, (j + 2) % 4)
                    for m in (late_pieces(ch, j) if last else []):
                        cut_hi(m)
                    k = {FQ_: 0, FK_: 1, G_: 2, CH - 1: 3}.get(ch)
                    if k is not None:
                        act.wait_ge(acc_ready, n + 1)
                        act.wait_ge(banks_free, 4 + n)
                        nc.scalar.activation(work[:], acc[:, j, :],
                                             ACT.Square if ch in (FQ_, FK_) else ACT.Sigmoid).then_inc(act_out, 1)
                each_group(act, body)
                for m in late_pieces(ch, 4):
                    cut_hi(m)

        @block.vector
        def _(dve):
            def scale_tile(t, slot):
                dve.wait_ge(rstd_step, 3 * t + 3)
                nc.vector.scalar_tensor_tensor(xt[:, slot, :], xt[:, slot, :], rstd[:, slot:slot + 1], w1[:],
                                               ALU.mult, ALU.mult).then_inc(scaled, 1)

            def tile_lo(t, slot):
                dve.wait_ge(ht_hi_done, t + 1)
                nc.vector.tensor_tensor(ht_lo[:, :, bass.ds(t * P, P)], tpv[:, slot],
                                        ht_hi[:, :, bass.ds(t * P, P)].bitcast(F32), ALU.subtract).then_inc(ht_lo_done, 1)

            dve.sem_inc(banks_free, 4)
            dve.wait_ge(w1_in, 16)
            nc.vector.tensor_scalar(w1[:], w1[:], float(DM) ** 0.5, None, ALU.mult).then_inc(w1_scaled, 1)
            dve.wait_ge(w1_scaled, 1)
            scale_tile(0, 0)
            scale_tile(1, 1)
            tile_lo(0, 0)
            for ch in range(CH):
                def body(i, j, last):
                    n = 16 * ch + 4 * i + j
                    if ch == 0:
                        if not (last and j == 3):
                            tile_lo(4 * i + j + 1, (j + 1) % 2)
                        if not (last and j >= 2):
                            scale_tile(4 * i + j + 2, j % 2)
                    dve.wait_ge(acc_ready, n + 1)
                    src, dst = acc[:, j, :], stage[:, j, :]
                    if ch in (FQ_, FK_):
                        k = n - 16 * FQ_
                        dve.wait_ge(act_out, k + 1)
                        nc.vector.tensor_reduce(qss[:, j % 2, :], work[:].rearrange("p (h e) -> p h e", h=FH),
                                                AX.X, ALU.add).then_inc(summed, 1)
                    dve.wait_ge(stored[j], 16 * (4 * ch + i))
                    if ch in (V_, FV_):
                        if ch == FV_:
                            nc.vector.tensor_copy(c["ff_logit"][:, 4 * i + j, :], tp[:, j, 0:FH])
                        nc.vector.tensor_copy(dst, src).then_inc(banks_free, 1)
                    elif ch in (FQ_, FK_):
                        heads = dst.rearrange("p (h e) -> p h e", h=FH)
                        nc.vector.tensor_tensor(heads, src.rearrange("p (h e) -> p h e", h=FH),
                                                c["qk_w"][:, ch - FQ_:ch - FQ_ + 1, :].broadcast_to([P, FH, FD]),
                                                ALU.mult).then_inc(dve_step, 1)
                        dve.wait_ge(dve_step, k + 1)
                        dve.wait_ge(qk_rstd, 2 * k + 2)
                        nc.vector.tensor_tensor(heads, heads, qrs[:, j % 2, :].unsqueeze(2).broadcast_to([P, FH, FD]),
                                                ALU.mult).then_inc(banks_free, 1)
                    elif ch == G_:
                        k = n - 32
                        dve.wait_ge(act_out, 32 + n - 16 * G_ + 1)
                        nc.vector.tensor_tensor(dst, src, work[:], ALU.mult).then_inc(dve_step, 1)
                        dve.wait_ge(dve_step, 32 + n - 16 * G_ + 1)
                        nc.vector.tensor_tensor(dst.rearrange("p (h e) -> p h e", h=HH),
                                                dst.rearrange("p (h e) -> p h e", h=HH),
                                                c["hgrn_w"][:].unsqueeze(1).broadcast_to([P, HH, P]),
                                                ALU.mult).then_inc(banks_free, 1)
                    elif ch == NT:
                        nc.vector.tensor_scalar(dst, src, float(P) ** -0.5, None, ALU.mult).then_inc(banks_free, 1)
                    else:
                        dve.wait_ge(act_out, 48 + n - 16 * (CH - 1) + 1)
                        nc.vector.tensor_scalar(dst, work[:], c["one_minus_lb"][:, bass.ds(i, 1)],
                                                c["lb"][:, bass.ds(i, 1)], ALU.mult, ALU.add).then_inc(banks_free, 1)
                each_group(dve, body)

        @block.tensor
        def _(pe):
            def transpose_tile(t, slot):
                pe.wait_ge(scaled, t + 1)
                for d in range(DT):
                    last = nc.tensor.transpose(tpv[:, slot, d, :], xt[:, slot, d * P:(d + 1) * P], c["ident"][:])
                last.then_inc(tp_ready, 1)

            transpose_tile(0, 0)

            def token_major(ch, first):
                for t in range(TT):
                    tok = slice(t * P, (t + 1) * P)
                    if first:
                        if t + 1 < TT:
                            pe.wait_ge(ht_lo_done, t)
                            transpose_tile(t + 1, (t + 1) % 2)
                        pe.wait_ge(ht_lo_done, t + 1)
                    pe.wait_ge(banks_free, 16 * ch + t + 1)
                    if isinstance(ch, int) and ch == FV_:
                        pe.wait_ge(ffw_lo_done, 1)
                        for d in range(DT):
                            three_pass(nc, tp[:, t % 4, 0:FH], ht_hi[:, d, tok], ht_lo[:, d, tok], ff_hi[:, d, :],
                                       ff_lo[:, d, :], d == 0, d == DT - 1)
                    for d in range(DT):
                        s = DT * (ch % 2) + d
                        if t == 0:
                            pe.wait_ge(w_lo_done, DT * ch + d + 1)
                        m = three_pass(nc, acc[:, t % 4, :], ht_hi[:, d, tok], ht_lo[:, d, tok], w_hi[:, s, :],
                                       w_lo[:, s, :], d == 0, d == DT - 1)
                        if t == TT - 1 and d < DT - 1:
                            m.then_inc(w_used, 1)
                    m.then_inc(acc_ready, 1)

            def channel_major(ch):
                for k in range(4):
                    col = slice(k * P, (k + 1) * P)
                    with pe.Fori(0, 4) as g:
                        pe.wait_ge(banks_free, 16 * ch + 4 * k + g + 1)
                        for d in range(DT):
                            s = DT * (ch % 2) + d
                            if k == 0:
                                pe.wait_ge(w_lo_done, DT * ch + d + 1)
                            tok = bass.ds(g * BANK, BANK)
                            m = three_pass(nc, acc[:, g, :], w_hi[:, s, col], w_lo[:, s, col], ht_hi[:, d, tok],
                                           ht_lo[:, d, tok], d == 0, d == DT - 1)
                        m.then_inc(acc_ready, 1)

            token_major(0, True)
            with pe.Fori(1, FV_) as ch:
                token_major(ch, False)
            token_major(FV_, False)
            token_major(G_, False)
            channel_major(NT)
            channel_major(NT + 1)


LV = 7
UN = BANK // P


def recurrence(nc, ctx, c, tok_in, ch_in, mix_out):
    def sem(name):
        return ctx.enter_context(nc.semaphore("r_" + name))

    q_in, f_in, v_in, g_in = ([sem(f"{n}_in{k}") for k in range(4)] for n in "qfvg")
    stored = [sem(f"stored{k}") for k in range(2)]
    (zeroed, mask_step, masks_done, k_done, lnf_done, b_done, eb_done, d_done, e_done, ql_done, kl_done, a_ready, pm_done,
     asum_step, kdt_ready, kdt_done, kdv_ready, s_done, o_ready, osq_done, orstd, fin) = (sem(n) for n in (
         "zeroed", "mask_step", "masks_done", "k_done", "lnf_done", "b_done", "eb_done", "d_done", "e_done", "ql_done",
         "kl_done", "a_ready", "pm_done", "asum_step", "kdt_ready", "kdt_done", "kdv_ready", "s_done", "o_ready",
         "osq_done", "orstd", "fin"))
    with ExitStack() as own:
        def sb(name, shape, dt=F32):
            return own.enter_context(nc.sbuf_tensor("r_" + name, shape, dt))

        def ps(name, shape):
            return own.enter_context(nc.psum_tensor("r_" + name, shape, F32))

        q, f = sb("q", [P, 4, BANK]), sb("f", [P, 4, BANK])
        v, g = sb("v", [P, 4, UN, P]), sb("g", [P, 4, UN, P])
        lnf, b = sb("lnf", [P, BANK]), sb("b", [P, BANK])
        eb, k = sb("eb", [P, 2, BANK]), sb("k", [P, 2, BANK])
        e = sb("e", [P, LV + 1, BANK])
        ql, kl = sb("ql", [P, 2, LV, BANK]), sb("kl", [P, 2, LV, BANK])
        qb, kd = sb("qb", [P, 2, BANK]), sb("kd", [P, 2, BANK])
        ones = sb("ones", [P, BANK])
        keep = sb("keep", [P, BANK])
        mask = sb("mask", [P, LV + 1, P])
        pm = sb("pm", [P, 2, LV + 1, P])
        kdt = sb("kdt", [P, 2, P])
        state = sb("state", [P, 2, P])
        junk, oss, ors = sb("junk", [P, 2, P]), sb("oss", [P, 2]), sb("ors", [P, 2])
        mix = sb("mix", [P, 2, UN, P])
        a_ps = [ps(f"a{n}", [P, LV + 1, P]) for n in range(2)]
        kdt_ps, kdv_ps = ps("kdt_ps", [P, BANK]), ps("kdv_ps", [P, BANK])
        o_ps = [ps(f"o{n}", [P, BANK]) for n in range(2)]
        block = own.enter_context(nc.Block())

        def halves(ap, lvl):
            w = 64 >> lvl
            return ap.rearrange("p (n two w) -> p n two w", two=2, w=w)

        def each_head(eng, prologue, unit, epilogue):
            prologue()
            with eng.Fori(0, HH - 1) as h:
                for u in range(4):
                    unit(h, u, True)
                epilogue(h)
            for u in range(4):
                unit(HH - 1, u, u < 3)
            epilogue(HH - 1)

        def nxt(h, u, by=1):
            return h + (u + by) // 4, (u + by) % 4

        @block.sync
        def _(sp):
            def load(h, u):
                sp.dma_start(q[:, u, :], ch_in[0, h, :, u * BANK:(u + 1) * BANK]).then_inc(q_in[u], 16)
                sp.dma_start(f[:, u, :], ch_in[1, h, :, u * BANK:(u + 1) * BANK]).then_inc(f_in[u], 16)
                for dst, group, done in ((v, V_, v_in), (g, G_, g_in)):
                    src = tok_in[group, u * UN:(u + 1) * UN, :, bass.ds(h * P, P)].rearrange("t p e -> p t e")
                    sp.dma_start(dst[:, u], src).then_inc(done[u], 16)

            def prologue():
                for u in range(3):
                    load(0, u)

            def unit(h, u, more):
                sp.wait_ge(fin, 16 * h + 4 * u + 4)
                dst = mix_out[u * UN:(u + 1) * UN, :, bass.ds(h * P, P)].rearrange("t p e -> p t e")
                sp.dma_start(dst, mix[:, u % 2]).then_inc(stored[u % 2], 16)
                if more and not (isinstance(h, int) and u > 0):
                    load(*nxt(h, u, 3))

            each_head(sp, prologue, unit, lambda h: None)
            for n in range(2):
                sp.wait_ge(stored[n], 16 * 2 * HH)

        @block.gpsimd
        def _(pool):
            def prologue():
                nc.gpsimd.memset(kl[:], 0.0).then_inc(zeroed, 1)
                nc.gpsimd.memset(mask[:], 1.0).then_inc(mask_step, 1)
                pool.wait_ge(mask_step, 1)
                step = 1
                for lvl in range(1, LV):
                    w2 = 128 >> lvl
                    m = mask[:, lvl, :].rearrange("p (n w) -> p n w", w=w2)
                    nc.gpsimd.affine_select(out=m, in_=m, compare_op=ALU.is_ge, fill=0.0, base=0,
                                            pattern=[[-w2, P // w2], [0, w2]], channel_multiplier=1).then_inc(mask_step, 1)
                    step += 1
                    pool.wait_ge(mask_step, step)
                    nc.gpsimd.affine_select(out=m, in_=m, compare_op=ALU.is_ge, fill=0.0, base=w2 - 1,
                                            pattern=[[w2, P // w2], [0, w2]], channel_multiplier=-1).then_inc(mask_step, 1)
                    step += 1
                nc.gpsimd.tensor_copy(mask[:, LV, :], c["ident"][:]).then_inc(mask_step, 1)
                step += 1
                pool.wait_ge(mask_step, step)
                pool.sem_inc(masks_done, 1)
                pool.wait_ge(zeroed, 1)
                for part in range(4):
                    prepare(0, 0, part)

            def prepare(h, u, part):
                n = 4 * h + u
                if part == 0:
                    if isinstance(n, int) and n == 0:
                        pool.wait_ge(zeroed, 4)
                    pool.wait_ge(f_in[u], 16 * (h + 1))
                    if not (isinstance(n, int) and n < 2):
                        pool.wait_ge(a_ready, 4 * n - 4)
                    nc.gpsimd.tensor_tensor(k[:, u % 2, :], ones[:], f[:, u, :], ALU.subtract).then_inc(k_done, 1)
                    pool.wait_ge(k_done, n + 1)
                for lvl in ((), (0, 1, 2), (3, 4, 5), (6, 7))[part]:
                    pool.wait_ge(e_done, 8 * n + lvl + 1)
                    if lvl < LV:
                        dst = halves(kl[:, u % 2, lvl, :], lvl)[:, :, 0, :]
                        src = halves(k[:, u % 2, :], lvl)[:, :, 0, :]
                        by = halves(e[:, lvl, :], lvl)[:, :, 0, :]
                    else:
                        dst, src, by = kd[:, u % 2, :], k[:, u % 2, :], e[:, LV, :]
                    nc.gpsimd.tensor_tensor(dst, src, by, ALU.mult).then_inc(kl_done, 1)

            def add_levels(h, i):
                n = 16 * h + i
                pool.wait_ge(pm_done, n + 1)
                for step, half in enumerate((4, 2, 1)):
                    if step:
                        pool.wait_ge(asum_step, 3 * n + step)
                    nc.gpsimd.tensor_tensor(pm[:, i % 2, 0:half, :], pm[:, i % 2, 0:half, :],
                                            pm[:, i % 2, half:2 * half, :], ALU.add).then_inc(asum_step, 1)

            def out_rstd(h, i):
                n = 16 * h + i
                s = slice(i % 2, i % 2 + 1)
                pool.wait_ge(osq_done, n + 1)
                pool.wait_ge(fin, n - 1 if i >= 2 else 16 * h)
                nc.gpsimd.tensor_tensor(ors[:, s], oss[:, s], c["eps_p"][:], ALU.add).then_inc(orstd, 1)
                pool.wait_ge(orstd, 2 * n + 1)
                nc.gpsimd.tensor_tensor(ors[:, s], ors[:, s], c["neg_half"][:, 0:1], ALU.pow).then_inc(orstd, 1)

            def unit(h, u, more):
                for part in range(4):
                    i = 4 * u + part
                    add_levels(h, i)
                    if i >= 1:
                        out_rstd(h, i - 1)
                    if more:
                        prepare(*nxt(h, u), part)

            each_head(pool, prologue, unit, lambda h: out_rstd(h, 15))

        @block.scalar
        def _(act):
            def prepare(h, u, part):
                n = 4 * h + u
                if part == 0:
                    act.wait_ge(f_in[u], 16 * (h + 1))
                    nc.scalar.activation(lnf[:], f[:, u, :], ACT.Ln).then_inc(lnf_done, 1)
                    act.wait_ge(b_done, n + 1)
                    if not (isinstance(n, int) and n < 2):
                        act.wait_ge(s_done, 4 * n - 4)
                    nc.scalar.activation(eb[:, u % 2, :], b[:], ACT.Exp).then_inc(eb_done, 1)
                for lvl in ((0, 1, 2), (3, 4, 5, 6, 7), (), ())[part]:
                    act.wait_ge(d_done, 8 * n + lvl + 1)
                    if lvl < LV:
                        ev = halves(e[:, lvl, :], lvl)
                        nc.scalar.activation(ev[:, :, 1, :], ev[:, :, 1, :], ACT.Exp)
                        nc.scalar.activation(ev[:, :, 0, :], ev[:, :, 0, :], ACT.Exp, scale=-1.0).then_inc(e_done, 1)
                    else:
                        nc.scalar.activation(e[:, LV, :], e[:, LV, :], ACT.Exp, scale=-1.0).then_inc(e_done, 1)

            def square_out(h, i):
                n = 16 * h + i
                act.wait_ge(o_ready, n + 1)
                act.wait_ge(orstd, 2 * (n - 1) if i >= 2 else 32 * h)
                nc.scalar.activation(junk[:, i % 2, :], o_ps[i % 2][:, 0:P], ACT.Square,
                                     accum_out=oss[:, i % 2:i % 2 + 1]).then_inc(osq_done, 1)

            def unit(h, u, more):
                for part in range(4):
                    i = 4 * u + part
                    n = 16 * h + i
                    act.wait_ge(kdt_ready, n + 1)
                    if i >= 2:
                        act.wait_ge(kdv_ready, n - 1)
                    nc.scalar.copy(kdt[:, i % 2, :], kdt_ps[:, 0:P]).then_inc(kdt_done, 1)
                    if i >= 1:
                        square_out(h, i - 1)
                    if more:
                        prepare(*nxt(h, u), part)

            def prologue():
                for part in range(4):
                    prepare(0, 0, part)

            each_head(act, prologue, unit, lambda h: square_out(h, 15))

        @block.vector
        def _(dve):
            def prepare(h, u, part):
                n = 4 * h + u
                if part == 0:
                    dve.wait_ge(lnf_done, n + 1)
                    dve.wait_ge(eb_done, n)
                    nc.vector.tensor_tensor_scan(b[:], keep[:], lnf[:], 0.0, ALU.mult, ALU.add).then_inc(b_done, 1)
                    dve.wait_ge(b_done, n + 1)
                for lvl in ((0, 1, 2), (3, 4, 5, 6, 7), (), ())[part]:
                    if not (isinstance(n, int) and n < 1):
                        dve.wait_ge(kl_done, 8 * n + lvl - 7)
                    w2 = 128 >> lvl if lvl < LV else P
                    bv = b[:].rearrange("p (n w) -> p n w", w=w2)
                    at = w2 // 2 - 1 if lvl < LV else P - 1
                    nc.vector.tensor_tensor(e[:, lvl, :].rearrange("p (n w) -> p n w", w=w2), bv,
                                            bv[:, :, at:at + 1].broadcast_to([P, BANK // w2, w2]),
                                            ALU.subtract).then_inc(d_done, 1)
                for lvl in ((), (0, 1), (2, 3, 4), (5, 6, 7))[part]:
                    if lvl == 0 and not (isinstance(n, int) and n < 2):
                        dve.wait_ge(o_ready, 4 * n - 4)
                    if lvl < LV:
                        dve.wait_ge(e_done, 8 * n + lvl + 1)
                        if lvl == 0:
                            dve.wait_ge(q_in[u], 16 * (h + 1))
                        dst = halves(ql[:, u % 2, lvl, :], lvl)[:, :, 1, :]
                        src = halves(q[:, u, :], lvl)[:, :, 1, :]
                        by = halves(e[:, lvl, :], lvl)[:, :, 1, :]
                    else:
                        dve.wait_ge(eb_done, n + 1)
                        dst, src, by = qb[:, u % 2, :], q[:, u, :], eb[:, u % 2, :]
                    nc.vector.tensor_tensor(dst, src, by, ALU.mult).then_inc(ql_done, 1)

            def mask_levels(h, i):
                n = 16 * h + i
                dve.wait_ge(a_ready, n + 1)
                if i >= 2:
                    dve.wait_ge(o_ready, n - 1)
                nc.vector.tensor_tensor(pm[:, i % 2], a_ps[i % 2][:], mask[:], ALU.mult).then_inc(pm_done, 1)

            def step_state(h, i):
                n = 16 * h + i
                dve.wait_ge(kdv_ready, n + 1)
                new = state[:, (i + 1) % 2, :]
                if i == 0:
                    nc.vector.tensor_copy(new, kdv_ps[:, 0:P]).then_inc(s_done, 1)
                else:
                    dve.wait_ge(s_done, n)
                    at = (i % 4) * P + P - 1
                    nc.vector.scalar_tensor_tensor(new, state[:, i % 2, :], eb[:, i // 4 % 2, at:at + 1], kdv_ps[:, 0:P],
                                                   ALU.mult, ALU.add).then_inc(s_done, 1)

            def finish(h, i):
                n = 16 * h + i
                u, ch = i // 4, i % 4
                dve.wait_ge(orstd, 2 * n + 2)
                if ch == 0:
                    dve.wait_ge(g_in[u], 16 * (h + 1))
                    dve.wait_ge(stored[u % 2], 16 * (2 * h + u // 2))
                nc.vector.scalar_tensor_tensor(mix[:, u % 2, ch, :], o_ps[i % 2][:, 0:P], ors[:, i % 2:i % 2 + 1],
                                               g[:, u, ch, :], ALU.mult, ALU.mult).then_inc(fin, 1)

            def unit(h, u, more):
                for part in range(4):
                    i = 4 * u + part
                    mask_levels(h, i)
                    step_state(h, i)
                    if i >= 2:
                        finish(h, i - 2)
                    if more:
                        prepare(*nxt(h, u), part)

            def prologue():
                nc.vector.memset(ones[:], 1.0).then_inc(zeroed, 1)
                nc.vector.memset(ql[:], 0.0).then_inc(zeroed, 1)
                nc.vector.memset(keep[:], 1.0).then_inc(zeroed, 1)
                dve.wait_ge(zeroed, 4)
                nc.vector.memset(keep[:].rearrange("p (n w) -> p n w", w=P)[:, :, 0:1], 0.0).then_inc(zeroed, 1)
                dve.wait_ge(zeroed, 5)
                for part in range(4):
                    prepare(0, 0, part)
                dve.wait_ge(masks_done, 1)

            def epilogue(h):
                finish(h, 14)
                finish(h, 15)

            each_head(dve, prologue, unit, epilogue)

        @block.tensor
        def _(pe):
            def level_products(h, i):
                n, u = 16 * h + i, i // 4
                t = slice(i % 4 * P, i % 4 * P + P)
                if i % 4 == 0:
                    pe.wait_ge(ql_done, 8 * (4 * h + u) + 8)
                    pe.wait_ge(kl_done, 8 * (4 * h + u) + 8)
                if i >= 2:
                    pe.wait_ge(pm_done, n - 1)
                for lvl in range(LV):
                    nc.tensor.matmul(a_ps[i % 2][:, lvl, :], kl[:, u % 2, lvl, t], ql[:, u % 2, lvl, t], start=True, stop=True)
                nc.tensor.matmul(a_ps[i % 2][:, LV, :], k[:, u % 2, t], q[:, u, t], start=True, stop=True).then_inc(a_ready, 1)

            def output(h, i):
                n, u, ch = 16 * h + i, i // 4, i % 4
                t = slice(ch * P, ch * P + P)
                if ch == 0:
                    pe.wait_ge(v_in[u], 16 * (h + 1))
                pe.wait_ge(asum_step, 3 * n + 3)
                pe.wait_ge(fin, n - 1 if i >= 2 else 16 * h)
                m = nc.tensor.matmul(o_ps[i % 2][:, 0:P], pm[:, i % 2, 0, :], v[:, u, ch, :], start=True, stop=i == 0)
                if i > 0:
                    pe.wait_ge(s_done, n)
                    m = nc.tensor.matmul(o_ps[i % 2][:, 0:P], qb[:, u % 2, t], state[:, i % 2, :], start=False, stop=True)
                m.then_inc(o_ready, 1)

            def unit(h, u, more):
                for part in range(4):
                    i = 4 * u + part
                    n = 16 * h + i
                    level_products(h, i)
                    pe.wait_ge(kdt_done, n)
                    nc.tensor.transpose(kdt_ps[:, 0:P], kd[:, u % 2, part * P:(part + 1) * P], c["ident"][:]).then_inc(kdt_ready, 1)
                    if i >= 1:
                        output(h, i - 1)
                    pe.wait_ge(kdt_done, n + 1)
                    pe.wait_ge(s_done, n)
                    if part == 0:
                        pe.wait_ge(v_in[u], 16 * (h + 1))
                    nc.tensor.matmul(kdv_ps[:, 0:P], kdt[:, i % 2, :], v[:, u, part, :], start=True, stop=True).then_inc(kdv_ready, 1)

            each_head(pe, lambda: None, unit, lambda h: output(h, 15))


KB = S // P
QG = KB // 4
SW = 2 * BANK
FAR = 2.0 ** 100


class Head:

    def __init__(self, n, slot, half):
        self.n, self.slot, self.half = n, slot, half

    def next(self):
        return Head(self.n + 1, 1 - self.slot, self.half + self.slot)

    def last(self):
        return Head(self.n - 1, 1 - self.slot, self.half - 1 + self.slot)


S_ITEMS = sum(1 if i * P + P <= SW else 2 for i in range(KB))
T_ITEMS = sum(4 * g + 4 for g in range(QG))
PREP = 8


def head_order(first, last):
    order = []
    for g in range(QG):
        scores = []
        for i in range(4 * g, 4 * g + 4):
            parts = 1 if (i + 1) * P <= SW else 2
            scores += [("score", i, part, part == parts - 1) for part in range(parts)]
        before = g == 0
        tg = (g - 1) % QG
        blocks = [] if before and first else [("block", tg, kb, before) for kb in range(4 * tg + 4)]
        if blocks:
            blocks += [("flush",), ("copy", tg, before)]
        if not last:
            blocks += [("prep", u) for u in {1: range(6), 2: range(6, PREP)}.get(g, ())]
        order.append(("step", g))
        done = 0
        for k, item in enumerate(scores):
            order.append(item)
            upto = len(blocks) * (k + 1) // len(scores)
            order += blocks[done:upto]
            done = upto
        if not (before and first):
            order.append(("fold", tg, before))
    return order


TAIL = [("block", QG - 1, kb, True) for kb in range(KB)] + [("flush",), ("copy", QG - 1, True), ("fold", QG - 1, True)]


def attention(nc, ctx, c, inp, tok_in, cum_dram, mix_out):
    def sem(name):
        return ctx.enter_context(nc.semaphore("a_" + name))

    names = ("bias_in", "gate_dve", "gate_act", "gate_pe", "gate_pool", "cum_stored", "consts_done", "q_in", "k_in", "v_in",
             "s_ready", "scored", "p_ready", "t_ready", "t_hi", "t_lo", "v_hi_done", "v_cut", "pv_done", "o_copied", "o_ready", "fin",
             "recip")
    sems = {n: sem(n) for n in names}
    (bias_in, gate_dve, gate_act, gate_pe, gate_pool, cum_stored, consts_done, q_in, k_in, v_in, s_ready, scored, p_ready,
     t_ready, t_hi, t_lo, v_hi_done, v_cut, pv_done, o_copied, o_ready, fin, recip_done) = (sems[n] for n in names)
    passed_dve, passed_pool, passed_sp = sem("passed_dve"), sem("passed_pool"), sem("passed_sp")
    cb_in = [sem(f"cb_in{n}") for n in range(2)]
    stored = [sem(f"stored{n}") for n in range(2)]
    with ExitStack() as own:
        def sb(name, shape, dt=F32):
            return own.enter_context(nc.sbuf_tensor("a_" + name, shape, dt))

        def ps(name, shape):
            return own.enter_context(nc.psum_tensor("a_" + name, shape, F32))

        kst, q1, q2 = (sb(n, [P, 2, S], F32R) for n in ("kst", "q1", "q2"))
        vcat = sb("vcat", [P, 2, KB, P], F32R)
        cb = sb("cb", [P, 2, S])
        qraw, kraw = (sb(n, [P, KB, 2, FD]) for n in ("qraw", "kraw"))
        vraw = sb("vraw", [P, KB, FD])
        p = sb("p", [P, 2, 4, S])
        pt_hi, pt_lo = sb("pt_hi", [P, 2, BANK], F32R), sb("pt_lo", [P, 2, BANK], F32R)
        ot = sb("ot", [P, BANK])
        stage = sb("stage", [P, 2, KB, FD])
        low = sb("low", [P, KB, 2])
        total, recip = sb("total", [P, QG, 4]), sb("recip", [P, QG, 4])
        ident_r, beyond_r, beyond = sb("ident_r", [P, P], F32R), sb("beyond_r", [P, P], F32R), sb("beyond", [P, P])
        fold = sb("fold", [P, FD])
        bias = sb("bias", [P, FH])
        gx, gy, gz, prefix, gi = sb("gx", [P, P]), sb("gy", [P, P]), sb("gz", [P, P]), sb("prefix", [P, P]), sb("gi", [P, P], mybir.dt.int32)
        s_ps = [ps(f"s{n}", [P, SW]) for n in range(2)]
        t_ps = [ps(f"t{n}", [P, BANK]) for n in range(2)]
        o_ps, fold_ps = ps("o", [P, BANK]), ps("fold_ps", [P, 4, FD])
        own_block = own.enter_context(ExitStack())

        with nc.Block() as block:
            @block.sync
            def _(sp):
                sp.dma_start(bias[:], bcast(inp["fox_f_bias"], FH)).then_inc(bias_in, 16)
                sp.wait_ge(gate_dve, 8)
                for t in range(TT):
                    sp.dma_start(cum_dram[:, t * P:(t + 1) * P], gz[t * FH:(t + 1) * FH, :]).then_inc(cum_stored, 16)
                sp.wait_ge(cum_stored, 16 * TT)

            @block.gpsimd
            def _(pool):
                nc.gpsimd.iota(gi[:], pattern=[[1, P]], base=0, channel_multiplier=-1).then_inc(gate_pool, 1)
                nc.gpsimd.memset(beyond[:], 0.0).then_inc(gate_pool, 1)
                pool.wait_ge(gate_pool, 2)
                nc.gpsimd.affine_select(out=beyond[:], in_=beyond[:], compare_op=ALU.is_ge, fill=FAR, base=0,
                                        pattern=[[-1, P]], channel_multiplier=1).then_inc(gate_pool, 1)
                pool.wait_ge(consts_done, 2)
                nc.gpsimd.affine_select(out=prefix[:], in_=prefix[:], compare_op=ALU.is_gt, fill=0.0, base=0,
                                        pattern=[[1, P]], channel_multiplier=-1).then_inc(gate_pool, 1)
                pool.wait_ge(gate_pool, 4)

            @block.scalar
            def _(act):
                act.wait_ge(gate_dve, 1)
                nc.scalar.activation(gy[:], gx[:], ACT.Abs).then_inc(gate_act, 1)
                act.wait_ge(gate_act, 1)
                nc.scalar.activation(gy[:], gy[:], ACT.Exp, scale=-1.0).then_inc(gate_act, 1)
                act.wait_ge(gate_act, 2)
                nc.scalar.activation(gy[:], gy[:], ACT.Ln, bias=1.0).then_inc(gate_act, 1)
                act.wait_ge(gate_act, 3)

            @block.vector
            def _(dve):
                xv = gx[:].rearrange("p (t h) -> p t h", h=FH)
                dve.wait_ge(bias_in, 16)
                nc.vector.tensor_tensor(xv, c["ff_logit"][:], bias[:].unsqueeze(1).broadcast_to([P, TT, FH]),
                                        ALU.add).then_inc(gate_dve, 1)
                nc.vector.tensor_copy(ident_r[:], c["ident"][:])
                nc.vector.tensor_tensor(fold[:], c["ident"][:, 0:FD], c["ident"][:, FD:P], ALU.add)
                dve.wait_ge(gate_pool, 1)
                nc.vector.tensor_scalar(gi[:], gi[:], FH - 1, None, ALU.bitwise_and).then_inc(consts_done, 1)
                dve.wait_ge(consts_done, 1)
                nc.vector.tensor_scalar(prefix[:], gi[:], 0.0, None, ALU.is_equal).then_inc(consts_done, 1)
                dve.wait_ge(gate_pool, 3)
                nc.vector.tensor_copy(beyond_r[:], beyond[:])
                dve.wait_ge(gate_act, 3)
                nc.vector.tensor_scalar(gx[:], gx[:], 0.0, None, ALU.min).then_inc(gate_dve, 1)
                dve.wait_ge(gate_dve, 2)
                nc.vector.tensor_tensor(gx[:], gx[:], gy[:], ALU.subtract).then_inc(gate_dve, 1)
                nc.vector.memset(gz[:], 1.0).then_inc(gate_dve, 1)
                dve.wait_ge(gate_pe, 1)
                dve.wait_ge(gate_dve, 4)
                nc.vector.tensor_tensor_scan(gy[:], gz[:], t_ps[0][:, 0:P], 0.0, ALU.mult, ALU.add).then_inc(gate_dve, 1)
                dve.wait_ge(gate_pe, 2)
                dve.wait_ge(gate_dve, 5)
                nc.vector.tensor_copy(gx[:, 0:1], t_ps[1][:, 0:1]).then_inc(gate_dve, 1)
                dve.wait_ge(gate_dve, 6)
                nc.vector.tensor_scalar(gz[:], gy[:], gx[:, 0:1], None, ALU.add).then_inc(gate_dve, 2)
                dve.wait_ge(gate_dve, 8)

            @block.tensor
            def _(pe):
                pe.wait_ge(gate_dve, 3)
                nc.tensor.transpose(t_ps[0][:, 0:P], gx[:], c["ident"][:]).then_inc(gate_pe, 1)
                pe.wait_ge(gate_dve, 5)
                pe.wait_ge(gate_pool, 4)
                nc.tensor.matmul(t_ps[1][:, 0:1], prefix[:], gy[:, P - 1:P], start=True, stop=True).then_inc(gate_pe, 1)

        block = own_block.enter_context(nc.Block())

        def bases(h):
            first = isinstance(h.n, int) and h.n == 0
            return (S_ITEMS * h.n, PREP if first else (T_ITEMS + PREP) * h.n - PREP,
                    0 if first else T_ITEMS * h.n - KB, 0 if first else QG * h.n - 1)

        def each_head(eng, prologue, run):
            prologue()
            run(Head(0, 0, 0), head_order(True, False), bases(Head(0, 0, 0)))
            with eng.Fori(0, (FH - 2) // 2) as m:
                for h in (Head(2 * m + 1, 1, m), Head(2 * m + 2, 0, m + 1)):
                    run(h, head_order(False, False), bases(h))
            h = Head(FH - 1, 1, FH // 2 - 1)
            run(h, head_order(False, True), bases(h))
            end = Head(FH, 0, FH // 2)
            run(end, TAIL, (S_ITEMS * FH, (T_ITEMS + PREP) * FH - KB, T_ITEMS * FH - KB, QG * FH - 1))

        def owner(h, before):
            return h.last() if before else h

        def tile_parts(i):
            n = (i + 1) * P
            return [min(SW, n - at) for at in range(0, n, SW)]

        def last_item(i):
            return sum(len(tile_parts(k)) for k in range(i + 1))

        @block.sync
        def _(sp):
            def load(h):
                for dst, group, done in ((kraw[:, :, 0, :], FK_, k_in), (kraw[:, :, 1, :], FK_, k_in),
                                         (qraw[:, :, 0, :], FQ_, q_in), (qraw[:, :, 1, :], FQ_, q_in), (vraw[:], FV_, v_in)):
                    sp.dma_start(dst, tok_in[group, :, :, bass.ds(h.n * FD, FD)].rearrange("t p e -> p t e")).then_inc(done, 16)
                row = cum_dram[bass.ds(h.n, 1), :].partition_broadcast(P)
                sp.dma_start(cb[:, h.slot:h.slot + 1, :], row).then_inc(cb_in[h.slot], 16)

            def run(h, order, at):
                n_s, n_t, n_pv, n_f = at
                if order is not TAIL and not (isinstance(h.n, int) and h.n == FH - 1):
                    wait_alone(sp, t_ready, n_t, passed_sp)
                    wait_alone(sp, v_cut, h.n + 1, passed_sp)
                    wait_alone(sp, scored, n_s, passed_sp)
                    load(h.next())
                if not (isinstance(h.n, int) and h.n == 0):
                    b = h.last()
                    wait_alone(sp, fin, QG * h.n, passed_sp)
                    sp.dma_start(mix_out[:, :, bass.ds(b.n * FD + FH * FD, FD)].rearrange("t p e -> p t e"),
                                 stage[:, b.slot]).then_inc(stored[b.slot], 16)

            each_head(sp, lambda: load(Head(0, 0, 0)), run)
            for n in range(2):
                sp.wait_ge(stored[n], 16 * FH // 2)

        @block.gpsimd
        def _(pool):
            def cut_v(h):
                wait_alone(pool, v_in, 16 * (h.n + 1), passed_pool)
                v_hi, v_lo = vcat[:, h.slot, :, 0:FD], vcat[:, h.slot, :, FD:P]
                nc.gpsimd.tensor_copy(v_hi, vraw[:]).then_inc(v_hi_done, 1)
                pool.wait_ge(v_hi_done, h.n + 1)
                nc.gpsimd.tensor_tensor(v_lo, vraw[:], v_hi.bitcast(F32), ALU.subtract).then_inc(v_cut, 1)

            def run(h, order, at):
                if order is not TAIL and not (isinstance(h.n, int) and h.n == FH - 1):
                    pool.wait_ge(pv_done, T_ITEMS * h.n)
                    cut_v(h.next())

            each_head(pool, lambda: cut_v(Head(0, 0, 0)), run)

        @block.scalar
        def _(act):
            def prep(h, u, r, t):
                act.wait_ge(t_ready, t + 1)
                dst = (kst, q1)[u % 2][:, h.slot, u // 2 * BANK:(u // 2 + 1) * BANK]
                nc.scalar.copy(dst, t_ps[r % 2][:]).then_inc(t_hi, 1)

            def run(h, order, at):
                n_s, n_t, n_pv, n_f = at
                r = pv = folds = 0
                for item in order:
                    kind = item[0]
                    if kind == "step" and not (isinstance(h.n, int) and h.n == 0):
                        act.wait_ge(fin, QG * h.n + item[1] - QG + 1)
                    elif kind == "score" and item[3]:
                        i = item[1]
                        act.wait_ge(scored, n_s + last_item(i))
                        row = p[:, i // 4 % 2, i % 4, 0:(i + 1) * P]
                        nc.scalar.activation(row, row, ACT.Exp, scale=-1.0, bias=low[:, i, len(tile_parts(i)) - 1:len(tile_parts(i))],
                                             accum_out=total[:, i // 4, i % 4:i % 4 + 1]).then_inc(p_ready, 1)
                    elif kind == "prep":
                        prep(h.next(), item[1], r, n_t + r)
                        r += 1
                    elif kind == "block":
                        _, g, kb, before = item
                        j0 = max(0, kb - 4 * g) * P
                        act.wait_ge(t_ready, n_t + r + 1)
                        if not (isinstance(h.n, int) and h.n == 0 and pv < 2):
                            act.wait_ge(pv_done, n_pv + pv - 1)
                        nc.scalar.copy(pt_hi[:, pv % 2, j0:], t_ps[r % 2][:, j0:]).then_inc(t_hi, 1)
                        r, pv = r + 1, pv + 1
                    elif kind == "copy":
                        act.wait_ge(pv_done, n_pv + pv)
                        act.wait_ge(o_ready, n_f + folds)
                        nc.scalar.copy(ot[:], o_ps[:]).then_inc(o_copied, 1)
                        folds += 1

            def prologue():
                for u in range(PREP):
                    prep(Head(0, 0, 0), u, u, u)

            each_head(act, prologue, run)

        @block.vector
        def _(dve):
            def prep(h, u, r, t):
                dve.wait_ge(t_hi, t + 1)
                cols = slice(u // 2 * BANK, (u // 2 + 1) * BANK)
                if u % 2 == 0:
                    dst = src = kst[FD:P, h.slot, cols]
                    bank = t_ps[r % 2][FD:P, :]
                else:
                    dst, src, bank = q2[:, h.slot, cols], q1[:, h.slot, cols], t_ps[r % 2][:]
                nc.vector.tensor_tensor(dst, bank, src.bitcast(F32), ALU.subtract).then_inc(t_lo, 1)

            def run(h, order, at):
                n_s, n_t, n_pv, n_f = at
                r = pv = folds = s = 0
                for item in order:
                    kind = item[0]
                    if kind == "step":
                        dve.wait_ge(t_ready, n_t + r)
                        if item[1] == 0:
                            dve.wait_ge(cb_in[h.slot], 16 * (h.half + 1))
                    elif kind == "score":
                        _, i, part, ends = item
                        at0, w = part * SW, tile_parts(i)[part]
                        start = FAR
                        if part:
                            dve.wait_ge(scored, n_s + s)
                            start = low[:, i, 0:1]
                        wait_alone(dve, s_ready, n_s + s + 1, passed_dve)
                        nc.vector.tensor_tensor_reduce(out=p[:, i // 4 % 2, i % 4, at0:at0 + w], in0=s_ps[s % 2][:, 0:w],
                                                       in1=cb[:, h.slot, at0:at0 + w], scale=1.0, scalar=start,
                                                       op0=ALU.add, op1=ALU.min,
                                                       accum_out=low[:, i, part:part + 1]).then_inc(scored, 1)
                        s += 1
                    elif kind == "prep":
                        prep(h.next(), item[1], r, n_t + r)
                        r += 1
                    elif kind == "block":
                        _, g, kb, before = item
                        j0 = max(0, kb - 4 * g) * P
                        dve.wait_ge(t_hi, n_t + r + 1)
                        nc.vector.tensor_tensor(pt_lo[:, pv % 2, j0:], t_ps[r % 2][:, j0:], pt_hi[:, pv % 2, j0:].bitcast(F32),
                                                ALU.subtract).then_inc(t_lo, 1)
                        r, pv = r + 1, pv + 1
                    elif kind == "fold":
                        _, g, before = item
                        o = owner(h, before)
                        dve.wait_ge(p_ready, KB * o.n + 4 * g + 4)
                        nc.vector.reciprocal(recip[:, g, :], total[:, g, :]).then_inc(recip_done, 1)
                        dve.wait_ge(recip_done, n_f + folds + 1)
                        dve.wait_ge(o_ready, n_f + folds + 1)
                        if g == 0:
                            dve.wait_ge(stored[o.slot], 16 * o.half)
                        nc.vector.tensor_tensor(stage[:, o.slot, 4 * g:4 * g + 4, :], fold_ps[:],
                                                recip[:, g, :].unsqueeze(2).broadcast_to([P, 4, FD]), ALU.mult).then_inc(fin, 1)
                        folds += 1

            def prologue():
                for u in range(PREP):
                    prep(Head(0, 0, 0), u, u, u)

            each_head(dve, prologue, run)

        @block.tensor
        def _(pe):
            def prep(h, u, r, t):
                if u < 2:
                    pe.wait_ge((k_in, q_in)[u], 32 * (h.n + 1))
                if not (isinstance(t, int) and t < 2):
                    pe.wait_ge(t_lo, t - 1)
                raw = (kraw, qraw)[u % 2]
                for k in range(4):
                    m = nc.tensor.transpose(t_ps[r % 2][:, k * P:(k + 1) * P],
                                            raw[:, u // 2 * 4 + k].rearrange("p two e -> p (two e)"), c["ident"][:])
                m.then_inc(t_ready, 1)

            def run(h, order, at):
                n_s, n_t, n_pv, n_f = at
                r = pv = folds = s = 0
                due = []

                def product():
                    g, kb, before, unit, n = due.pop()
                    o = owner(h, before)
                    j0 = max(0, kb - 4 * g) * P
                    if kb == 0:
                        pe.wait_ge(v_cut, o.n + 1)
                        pe.wait_ge(o_copied, n_f + folds)
                    pe.wait_ge(t_lo, n_t + unit + 1)
                    for part in (pt_hi, pt_lo):
                        m = nc.tensor.matmul(o_ps[:, j0:], vcat[:, o.slot, kb, :], part[:, n % 2, j0:],
                                             start=kb == 0 and part is pt_hi, stop=kb == 4 * g + 3 and part is pt_lo)
                    m.then_inc(pv_done, 1)

                for item in order:
                    kind = item[0]
                    if kind == "score":
                        _, i, part, ends = item
                        at0, w = part * SW, tile_parts(i)[part]
                        if not (isinstance(h.n, int) and h.n == 0 and s < 2):
                            pe.wait_ge(scored, n_s + s - 1)
                        if i == 0:
                            pe.wait_ge(t_lo, n_t)
                        tile = slice(i * P, (i + 1) * P)
                        for b in range(0, w, BANK):
                            bw = min(BANK, w - b)
                            out, keys = s_ps[s % 2][:, b:b + bw], kst[:, h.slot, at0 + b:at0 + b + bw]
                            nc.tensor.matmul(out, q1[:, h.slot, tile], keys, start=True, stop=False)
                            if ends and b + bw == w:
                                nc.tensor.matmul(s_ps[s % 2][:, w - P:w], ident_r[:], beyond_r[:], start=False, stop=False)
                            m = nc.tensor.matmul(out, q2[:, h.slot, tile], keys, start=False, stop=True)
                        m.then_inc(s_ready, 1)
                        s += 1
                    elif kind == "prep":
                        prep(h.next(), item[1], r, n_t + r)
                        r += 1
                    elif kind == "block":
                        _, g, kb, before = item
                        o = owner(h, before)
                        if kb == 0:
                            pe.wait_ge(p_ready, KB * o.n + 4 * g + 4)
                        pe.wait_ge(t_lo, n_t + r - 1)
                        for j in range(max(0, kb - 4 * g), 4):
                            m = nc.tensor.transpose(t_ps[r % 2][:, j * P:(j + 1) * P],
                                                    p[:, g % 2, j, kb * P:(kb + 1) * P], c["ident"][:])
                        m.then_inc(t_ready, 1)
                        if due:
                            product()
                        due.append((g, kb, before, r, pv))
                        r, pv = r + 1, pv + 1
                    elif kind == "flush":
                        product()
                    elif kind == "fold":
                        pe.wait_ge(o_copied, n_f + folds + 1)
                        pe.wait_ge(fin, n_f + folds)
                        for j in range(4):
                            m = nc.tensor.matmul(fold_ps[:, j, :], ot[:, j * P:(j + 1) * P], fold[:], start=True, stop=True)
                        m.then_inc(o_ready, 1)
                        folds += 1

            def prologue():
                for u in range(PREP):
                    prep(Head(0, 0, 0), u, u, u)

            each_head(pe, prologue, run)


HT = TT // 2
FC = DFF // BANK
FT = BANK // P
CW = DM // BANK


def mix_and_mlp(nc, ctx, c, inp, mix_in, out):
    NRAW = 4
    PIECES = 16 + FC * 16
    ADDS = CW * HT * (1 + FC)
    UPS, DOWNS = 8 * FC, CW * HT * FC

    def sem(name):
        return ctx.enter_context(nc.semaphore("m_" + name))

    names = ("w2_in", "out_stored", "w_hi_done", "w_lo_done", "mix_t", "mt_hi_done", "mt_lo_done", "o_ready", "added",
             "squared", "rstd_step", "scaled", "h_t", "ht_hi_done", "ht_lo_done", "up_ready", "relu_done", "sq_done",
             "u_hi_done", "u_lo_done", "down_ready", "w2_scaled")
    (w2_in, out_stored, w_hi_done, w_lo_done, mix_t, mt_hi_done, mt_lo_done, o_ready, added, squared, rstd_step, scaled,
     h_t, ht_hi_done, ht_lo_done, up_ready, relu_done, sq_done, u_hi_done, u_lo_done, down_ready, w2_scaled) = (sem(n) for n in names)
    mix_in_done = [sem(f"mix_in{k}") for k in range(2)]
    raw_in = [sem(f"raw_in{k}") for k in range(NRAW)]
    x_in = [sem(f"x_in{k}") for k in range(HT)]
    with ExitStack() as own:
        def sb(name, shape, dt=F32):
            return own.enter_context(nc.sbuf_tensor("m_" + name, shape, dt))

        ht_hi, ht_lo = sb("ht_hi", [P, DT, HT * P], F32R), sb("ht_lo", [P, DT, HT * P], F32R)
        w_hi, w_lo = sb("w_hi", [P, 16, BANK], F32R), sb("w_lo", [P, 16, BANK], F32R)
        acc = sb("acc", [P, HT, DM])
        raw = sb("raw", [P, NRAW, BANK])
        u_hi, u_lo = sb("u_hi", [P, FT, HT * P], F32R), sb("u_lo", [P, FT, HT * P], F32R)
        relu = sb("relu", [P, 2, BANK])
        w2 = sb("w2", [P, DM])
        mixr = sb("mixr", [P, 2, DM])
        ss, rstd = sb("ss", [P, 2, 2]), sb("rstd", [P, 2])
        mt_hi = u_hi[:, 0:2, :].rearrange("p s (d t) -> p s d t", t=P)
        mt_lo = u_lo[:, 0:2, :].rearrange("p s (d t) -> p s d t", t=P)
        h2 = sb("h2", [P, DM])
        up_ps = own.enter_context(nc.psum_tensor("m_up", [P, 4, BANK], F32))
        down_ps = own.enter_context(nc.psum_tensor("m_down", [P, 4, BANK], F32))
        mtp = down_ps[:, 0:2, :].rearrange("p b (d t) -> p (b d) t", t=P)
        htp = down_ps[:, 2:4, :].rearrange("p b (d t) -> p (b d) t", t=P)
        w_out = inp["w_out"].rearrange("l (d p) n -> p (l d) n", p=P)
        w_up = inp["w_up"].rearrange("l (d p) n -> p (l d) n", p=P)
        w_down = inp["w_down"].rearrange("l (f p) n -> p (l f) n", p=P)
        x_tiles = inp["x"].rearrange("b (t p) d -> (b t) p d", p=P)
        out_tiles = out.rearrange("b (t p) d -> (b t) p d", p=P)
        block = own.enter_context(nc.Block())

        def each_chunk(eng, body):
            with eng.Fori(0, FC - 1) as f:
                body(f, False)
            body(FC - 1, True)

        def out_piece(m):
            return divmod(m, DT)

        @block.sync
        def _(sp):
            def load_piece(m, src, r):
                if not (isinstance(m, int) and m < NRAW):
                    sp.wait_ge(w_lo_done, m - NRAW + 1)
                sp.dma_start(raw[:, r, :], src).then_inc(raw_in[r], 16)

            def load_w_out(half, m):
                k, d = out_piece(m)
                load_piece(PIECES * half + m, w_out[:, d, k * BANK:(k + 1) * BANK], m % NRAW)

            def load_mix(half, t):
                n = HT * half + t
                if n >= 2:
                    sp.wait_ge(mix_t, n - 1)
                sp.dma_start(mixr[:, t % 2, :], mix_in[n]).then_inc(mix_in_done[t % 2], 16)

            load_mix(0, 0)
            sp.dma_start(w2[:], bcast(inp["norm2_w"], DM)).then_inc(w2_in, 16)
            for m in range(8):
                load_w_out(0, m)
            load_mix(0, 1)
            for half in range(2):
                base = PIECES * half
                for m in range(8, 16):
                    load_w_out(half, m)
                for t in range(HT):
                    if half:
                        sp.wait_ge(out_stored, 16 * HT)
                    sp.dma_start(acc[:, t, :], x_tiles[HT * half + t]).then_inc(x_in[t], 16)
                for t in range(2, HT):
                    load_mix(half, t)
                for d in range(DT):
                    load_piece(base + 16 + d, w_up[:, d, 0:BANK], d % NRAW)

                def chunk(f, last):
                    for k in range(8):
                        src = w_down[:, bass.ds(f * FT + k // 2, 1), k % 2 * BANK:(k % 2 + 1) * BANK]
                        load_piece(base + 24 + 16 * f + k, src.rearrange("p one n -> p (one n)"), k % NRAW)
                    if not last:
                        for d in range(DT):
                            load_piece(base + 32 + 16 * f + d, w_up[:, d, bass.ds(f * BANK + BANK, BANK)], d % NRAW)
                        return
                    if half == 0:
                        for m in range(8):
                            load_w_out(1, m)
                        load_mix(1, 0)
                        load_mix(1, 1)
                    for t in range(HT):
                        sp.wait_ge(added, ADDS * half + 16 + 16 * f + 2 * t + 2)
                        sp.dma_start(out_tiles[half * HT + t], acc[:, t, :]).then_inc(out_stored, 16)

                each_chunk(sp, chunk)
            sp.wait_ge(out_stored, 16 * TT)

        @block.gpsimd
        def _(pool):
            def cut_lo(m, s, r):
                pool.wait_ge(w_hi_done, m + 1)
                nc.gpsimd.tensor_tensor(w_lo[:, s, :], raw[:, r, :], w_hi[:, s, :].bitcast(F32), ALU.subtract).then_inc(w_lo_done, 1)

            def tile_rstd(n):
                s = slice(n % 2, n % 2 + 1)
                pool.wait_ge(squared, 2 * n + 2)
                nc.gpsimd.tensor_tensor(rstd[:, s], ss[:, n % 2, 0:1], ss[:, n % 2, 1:2], ALU.add).then_inc(rstd_step, 1)
                pool.wait_ge(rstd_step, 3 * n + 1)
                nc.gpsimd.tensor_tensor(rstd[:, s], rstd[:, s], c["eps_dm"][:], ALU.add).then_inc(rstd_step, 1)
                pool.wait_ge(rstd_step, 3 * n + 2)
                nc.gpsimd.tensor_tensor(rstd[:, s], rstd[:, s], c["neg_half"][:, 0:1], ALU.pow).then_inc(rstd_step, 1)

            for m in range(8):
                cut_lo(m, m, m % NRAW)
            for half in range(2):
                base = PIECES * half
                for m in range(8, 16):
                    cut_lo(base + m, m, m % NRAW)
                for t in range(HT):
                    tile_rstd(HT * half + t)
                for d in range(DT):
                    cut_lo(base + 16 + d, d, d % NRAW)

                def chunk(f, last):
                    for k in range(8):
                        pool.wait_ge(relu_done, UPS * half + 8 * f + k + 1)
                        nc.gpsimd.tensor_tensor(relu[:, k % 2, :], relu[:, k % 2, :], relu[:, k % 2, :], ALU.mult).then_inc(sq_done, 1)
                        cut_lo(base + 24 + 16 * f + k, 8 + k, k % NRAW)
                    for d in range(DT if not (last and half) else 0):
                        cut_lo(base + 32 + 16 * f + d, d, d % NRAW)

                each_chunk(pool, chunk)

        @block.scalar
        def _(act):
            def cut_hi(s, r, uses):
                act.wait_ge(raw_in[r], 16 * uses)
                nc.scalar.copy(w_hi[:, s, :], raw[:, r, :]).then_inc(w_hi_done, 1)

            def square_tile(half, t):
                n = HT * half + t
                act.wait_ge(added, ADDS * half + 2 * t + 2)
                if n >= 2:
                    act.wait_ge(rstd_step, 3 * (n - 2) + 1)
                for k in range(2):
                    act.wait_ge(squared, 2 * n + k)
                    nc.scalar.activation(relu[:, 0, :], acc[:, t, k * BANK:(k + 1) * BANK], ACT.Square,
                                         accum_out=ss[:, t % 2, k:k + 1]).then_inc(squared, 1)

            def mix_hi(half, t):
                n = HT * half + t
                act.wait_ge(mix_t, n + 1)
                if t >= 2:
                    act.wait_ge(o_ready, 2 * (n - 2) + 2)
                nc.scalar.copy(mt_hi[:, t % 2], mtp).then_inc(mt_hi_done, 1)

            def norm_hi(half, t):
                act.wait_ge(h_t, HT * half + t + 1)
                nc.scalar.copy(ht_hi[:, :, t * P:(t + 1) * P], htp).then_inc(ht_hi_done, 1)

            for m in range(8):
                cut_hi(m, m % NRAW, m // NRAW + 1)
            for half in range(2):
                uses = PIECES // NRAW * half
                mix_hi(half, 0)
                for m in range(8, 16):
                    cut_hi(m, m % NRAW, uses + m // NRAW + 1)
                for t in range(HT):
                    if t + 1 < HT:
                        mix_hi(half, t + 1)
                    if t >= 1:
                        norm_hi(half, t - 1)
                    square_tile(half, t)
                norm_hi(half, HT - 1)
                act.wait_ge(o_ready, 2 * HT * (half + 1))
                for d in range(DT):
                    cut_hi(d, d % NRAW, uses + 4 + d // NRAW + 1)

                def chunk(f, last):
                    for k in range(8):
                        n = UPS * half + 8 * f + k
                        act.wait_ge(up_ready, n + 1)
                        if not (isinstance(n, int) and n < 2):
                            act.wait_ge(u_lo_done, n - 1 if k >= 1 else n)
                        nc.scalar.activation(relu[:, k % 2, :], up_ps[:, k % 4, :], ACT.Relu).then_inc(relu_done, 1)
                        if k == 0:
                            act.wait_ge(down_ready, DOWNS * half + 16 * f)
                        cut_hi(8 + k, k % NRAW, uses + 6 + 4 * f + k // NRAW + 1)
                        act.wait_ge(sq_done, n + 1)
                        nc.scalar.copy(u_hi[:, k % 4, k // 4 * BANK:(k // 4 + 1) * BANK], relu[:, k % 2, :]).then_inc(u_hi_done, 1)
                    if not (last and half):
                        act.wait_ge(up_ready, UPS * half + 8 * f + 8)
                        for d in range(DT):
                            cut_hi(d, d % NRAW, uses + 8 + 4 * f + d // NRAW + 1)

                each_chunk(act, chunk)

        @block.vector
        def _(dve):
            def mix_lo(half, t):
                dve.wait_ge(mt_hi_done, HT * half + t + 1)
                nc.vector.tensor_tensor(mt_lo[:, t % 2], mtp, mt_hi[:, t % 2].bitcast(F32), ALU.subtract).then_inc(mt_lo_done, 1)

            def norm_lo(half, t):
                dve.wait_ge(ht_hi_done, HT * half + t + 1)
                tok = slice(t * P, (t + 1) * P)
                nc.vector.tensor_tensor(ht_lo[:, :, tok], htp, ht_hi[:, :, tok].bitcast(F32), ALU.subtract).then_inc(ht_lo_done, 1)

            def add(t, k, bank):
                cols = acc[:, t, k * BANK:(k + 1) * BANK]
                nc.vector.tensor_tensor(cols, cols, bank, ALU.add).then_inc(added, 1)

            def scale_tile(half, t):
                n = HT * half + t
                dve.wait_ge(rstd_step, 3 * n + 3)
                dve.wait_ge(h_t, n)
                nc.vector.scalar_tensor_tensor(h2[:], acc[:, t, :], rstd[:, t % 2:t % 2 + 1], w2[:],
                                               ALU.mult, ALU.mult).then_inc(scaled, 1)

            dve.wait_ge(w2_in, 16)
            nc.vector.tensor_scalar(w2[:], w2[:], float(DM) ** 0.5, None, ALU.mult).then_inc(w2_scaled, 1)
            dve.wait_ge(w2_scaled, 1)
            for half in range(2):
                mix_lo(half, 0)
                for t in range(HT):
                    if t + 1 < HT:
                        mix_lo(half, t + 1)
                    if t >= 1:
                        norm_lo(half, t - 1)
                    dve.wait_ge(x_in[t], 16 * (half + 1))
                    for k in range(2):
                        dve.wait_ge(o_ready, 2 * (HT * half + t) + k + 1)
                        add(t, k, up_ps[:, (2 * t + k) % 4, :])
                    scale_tile(half, t)
                norm_lo(half, HT - 1)

                def chunk(f, last):
                    for k in range(8):
                        dve.wait_ge(u_hi_done, UPS * half + 8 * f + k + 1)
                        tok = slice(k // 4 * BANK, (k // 4 + 1) * BANK)
                        nc.vector.tensor_tensor(u_lo[:, k % 4, tok], relu[:, k % 2, :], u_hi[:, k % 4, tok].bitcast(F32),
                                                ALU.subtract).then_inc(u_lo_done, 1)
                    for t in range(HT):
                        for k in range(CW):
                            n = 16 * f + 2 * t + k
                            dve.wait_ge(added, ADDS * half + n + 1)
                            dve.wait_ge(down_ready, DOWNS * half + n + 1)
                            add(t, k, down_ps[:, (2 * t + k) % 4, :])

                each_chunk(dve, chunk)

        @block.tensor
        def _(pe):
            def turn(src, dst):
                for d in range(DT):
                    m = nc.tensor.transpose(dst[:, d, :], src[:, d * P:(d + 1) * P], c["ident"][:])
                return m

            def turn_mix(half, t):
                n = HT * half + t
                pe.wait_ge(mix_in_done[t % 2], 16 * (n // 2 + 1))
                pe.wait_ge(mt_lo_done, n)
                turn(mixr[:, t % 2, :], mtp).then_inc(mix_t, 1)

            def turn_norm(half, t):
                n = HT * half + t
                pe.wait_ge(scaled, n + 1)
                pe.wait_ge(ht_lo_done, n)
                turn(h2[:], htp).then_inc(h_t, 1)

            for half in range(2):
                pe.wait_ge(added, ADDS * half)
                turn_mix(half, 0)
                for t in range(HT):
                    if t + 1 < HT:
                        turn_mix(half, t + 1)
                    pe.wait_ge(mt_lo_done, HT * half + t + 1)
                    for k in range(2):
                        if t >= 2:
                            pe.wait_ge(added, ADDS * half + 2 * t + k - 3)
                        for d in range(DT):
                            s = DT * k + d
                            if t == 0:
                                pe.wait_ge(w_lo_done, PIECES * half + s + 1)
                            m = three_pass(nc, up_ps[:, (2 * t + k) % 4, :], mt_hi[:, t % 2, d, :], mt_lo[:, t % 2, d, :],
                                           w_hi[:, s, :], w_lo[:, s, :], d == 0, d == DT - 1)
                        m.then_inc(o_ready, 1)
                    if t >= 1:
                        turn_norm(half, t - 1)
                turn_norm(half, HT - 1)
                pe.wait_ge(ht_lo_done, HT * (half + 1))
                pe.wait_ge(added, ADDS * half + 2 * HT)

                def chunk(f, last):
                    for k in range(8):
                        n = UPS * half + 8 * f + k
                        if not (isinstance(n, int) and n < 4):
                            pe.wait_ge(relu_done, n - 3 if k >= 3 else n - k)
                        tok, hid = slice(k // 4 * BANK, (k // 4 + 1) * BANK), slice(k % 4 * P, k % 4 * P + P)
                        for d in range(DT):
                            if k == 0:
                                pe.wait_ge(w_lo_done, PIECES * half + 16 + 16 * f + d + 1)
                            m = three_pass(nc, up_ps[:, k % 4, :], w_hi[:, d, hid], w_lo[:, d, hid], ht_hi[:, d, tok],
                                           ht_lo[:, d, tok], d == 0, d == DT - 1)
                        m.then_inc(up_ready, 1)
                    for t in range(HT):
                        tok = slice(t * P, (t + 1) * P)
                        for k in range(CW):
                            n = 16 * f + 2 * t + k
                            if t == 0 and k == 0:
                                pe.wait_ge(w_lo_done, PIECES * half + 24 + 16 * f + 8)
                            if t % 4 == 0 and k == 0:
                                pe.wait_ge(u_lo_done, UPS * half + 8 * f + t + 4)
                            pe.wait_ge(added, ADDS * half + 16 + n - 3)
                            for i in range(FT):
                                s = 8 + 2 * i + k
                                m = three_pass(nc, down_ps[:, (2 * t + k) % 4, :], u_hi[:, i, tok], u_lo[:, i, tok],
                                               w_hi[:, s, :], w_lo[:, s, :], i == 0, i == FT - 1)
                            m.then_inc(down_ready, 1)

                each_chunk(pe, chunk)


def build(nc, inp, out):
    with ExitStack() as ctx:
        c = constants(nc, ctx, inp)
        tok = nc.dram_tensor("tok_major", (NT, TT, P, BANK), F32, kind="Internal").ap()
        chan = nc.dram_tensor("chan_major", (2, HH, P, S), F32, kind="Internal").ap()
        cum = nc.dram_tensor("cum_gates", (FH, S), F32, kind="Internal").ap()
        mix = nc.dram_tensor("mixed", (TT, P, DM), F32, kind="Internal").ap()
        project(nc, ctx, c, inp, tok, chan)
        recurrence(nc, ctx, c, tok, chan, mix)
        attention(nc, ctx, c, inp, tok, cum, mix)
        mix_and_mlp(nc, ctx, c, inp, mix, out)


_INS = ["x", "lower_bounds", "norm1_w", "w_in", "fox_f_bias", "q_norm_w", "k_norm_w", "hgrn_norm_w", "w_out",
        "norm2_w", "w_up", "w_down"]


def kernel(**inputs):
    import numpy as _np
    import concourse.bacc as _bacc
    from concourse.bass_utils import run_bass_kernel_spmd as _run

    nc = _bacc.Bacc("TRN2", target_bir_lowering=False, num_devices=1, dynamic_dma_scratch_size=1024)
    arrays, args = {}, {}
    for name in _INS:
        a = _np.ascontiguousarray(inputs[name])
        arrays[f"in_{name}"] = a
        args[name] = nc.dram_tensor(f"in_{name}", a.shape, mybir.dt.from_np(a.dtype), kind="ExternalInput").ap()
    out = nc.dram_tensor("out_0", (1, S, DM), F32, kind="ExternalOutput").ap()
    build(nc, args, out)
    r = _run(nc, [arrays], core_ids=[0])
    return r.results[0]["out_0"]
```

```python
from contextlib import ExitStack

import concourse.bass as bass
from concourse import mybir

F32 = mybir.dt.float32
F32R = mybir.dt.float32r
ALU = mybir.AluOpType
ACT = mybir.ActivationFunctionType
AX = mybir.AxisListType

P = 128
BANK = 512
S = 2048
DM = 1024
DT = DM // P
TT = S // P
HH = 4
FH = 8
FD = 64
DFF = 4 * DM
EPS = 1e-6
NT = 5
V_, FQ_, FK_, FV_, G_ = range(NT)


class Ring:

    def __init__(self, slots):
        self.slots = slots

    def slot(self, n):
        return n % self.slots

    def landed(self, n):
        return 16 * (n // self.slots + 1)


def wait_alone(eng, sem, value, passed):
    eng.wait_ge(sem, value)
    eng.sem_inc(passed, 1)


def place_under(nc, names, shapes):
    with ExitStack() as early:
        return [early.enter_context(nc.sbuf_tensor(name, shape, F32)) for name, shape in zip(names, shapes)]


def three_pass(nc, out, l_hi, l_lo, r_hi, r_lo, first, last):
    nc.tensor.matmul(out, l_hi, r_hi, start=first, stop=False)
    nc.tensor.matmul(out, l_hi, r_lo, start=False, stop=False)
    return nc.tensor.matmul(out, l_lo, r_hi, start=False, stop=last)


def constants(nc, ctx, inp):
    def sb(name, shape, dt=F32):
        return ctx.enter_context(nc.sbuf_tensor(name, shape, dt))

    c = {
        "ident": sb("ident", [P, P]),
        "neg_half": sb("neg_half", [P, FH]),
        "eps_dm": sb("eps_dm", [P, 1]),
        "eps_fd": sb("eps_fd", [P, FH]),
        "eps_p": sb("eps_p", [P, 1]),
        "lb": sb("lb", [P, HH]),
        "one_minus_lb": sb("one_minus_lb", [P, HH]),
        "ff_logit": sb("ff_logit", [P, TT, FH]),
        "hgrn_w": sb("hgrn_w", [P, P]),
        "qk_w": sb("qk_w", [P, 2, FD]),
    }
    small_in = ctx.enter_context(nc.semaphore("small_in"))
    pool_step = ctx.enter_context(nc.semaphore("const_pool_step"))
    act_step = ctx.enter_context(nc.semaphore("const_act_step"))
    lb_step = ctx.enter_context(nc.semaphore("const_lb_step"))
    lb_work = sb("lb_work", [P, 3, HH])
    with nc.Block() as block:
        @block.sync
        def _(sp):
            with nc.allow_non_contiguous_dma(reason="512 values"):
                sp.dma_start(c["lb"][:], inp["lower_bounds"].rearrange("l (h p) -> p (l h)", p=P)).then_inc(small_in, 16)
            sp.dma_start(c["hgrn_w"][:], bcast(inp["hgrn_norm_w"], P)).then_inc(small_in, 16)
            sp.dma_start(c["qk_w"][:, 0, :], bcast(inp["q_norm_w"], FD)).then_inc(small_in, 16)
            sp.dma_start(c["qk_w"][:, 1, :], bcast(inp["k_norm_w"], FD)).then_inc(small_in, 16)
            sp.wait_ge(small_in, 64)

        @block.gpsimd
        def _(pool):
            nc.gpsimd.memset(c["neg_half"][:], -0.5)
            nc.gpsimd.memset(c["eps_dm"][:], DM * EPS)
            nc.gpsimd.memset(c["eps_fd"][:], FD * EPS)
            nc.gpsimd.memset(c["eps_p"][:], P * EPS)
            nc.gpsimd.memset(c["ident"][:], 0.0).then_inc(pool_step, 1)
            pool.wait_ge(pool_step, 1)
            nc.gpsimd.affine_select(out=c["ident"][:], in_=c["ident"][:], compare_op=ALU.not_equal, fill=1.0,
                                    base=0, pattern=[[-1, P]], channel_multiplier=1).then_inc(pool_step, 1)
            pool.wait_ge(pool_step, 2)

        @block.vector
        def _(dve):
            dve.wait_ge(small_in, 64)
            nc.vector.tensor_tensor(lb_work[:, 0, :], c["lb"][:], c["lb"][:], ALU.subtract).then_inc(lb_step, 1)
            nc.vector.tensor_scalar(c["qk_w"][:, 0, :], c["qk_w"][:, 0, :], -1.0, None, ALU.mult)
            nc.vector.tensor_scalar(c["qk_w"][:, 1, :], c["qk_w"][:, 1, :], float(FD) ** 0.5, None, ALU.mult)
            nc.vector.tensor_scalar(c["hgrn_w"][:], c["hgrn_w"][:], float(P) ** 0.5, None, ALU.mult)
            dve.wait_ge(act_step, 1)
            nc.vector.reciprocal(lb_work[:, 2, :], lb_work[:, 1, :]).then_inc(lb_step, 1)
            dve.wait_ge(lb_step, 2)
            nc.vector.tensor_tensor(lb_work[:, 0, :], lb_work[:, 1, :], lb_work[:, 2, :], ALU.mult).then_inc(lb_step, 1)
            dve.wait_ge(lb_step, 3)
            nc.vector.tensor_tensor(c["lb"][:], lb_work[:, 0, :], lb_work[:, 0, :], ALU.subtract).then_inc(lb_step, 1)
            dve.wait_ge(lb_step, 4)
            nc.vector.tensor_scalar(c["one_minus_lb"][:], c["lb"][:], -1.0, 1.0, ALU.mult, ALU.add).then_inc(lb_step, 1)
            dve.wait_ge(lb_step, 5)

        @block.scalar
        def _(act):
            act.wait_ge(lb_step, 1)
            nc.scalar.activation(lb_work[:, 1, :], lb_work[:, 0, :], ACT.Exp).then_inc(act_step, 1)
            act.wait_ge(act_step, 1)
    return c


def bcast(row, n):
    return bass.AP(tensor=row.tensor, offset=row.offset, ap=[[0, P], [1, n]])


def project(nc, ctx, c, inp, tok_out, ch_out):
    NW = 16
    NRAW = 2
    CH = 7
    COLS = [1024, 2048, 2560, 3072, 1536, 0, 512]
    FF = 3584
    raw_ring, x_ring = Ring(NRAW), Ring(2)

    def sem(name):
        return ctx.enter_context(nc.semaphore("p_" + name))

    x_in = [sem(f"x_in{k}") for k in range(2)]
    raw_in = [sem(f"raw_in{k}") for k in range(NRAW)]
    stored = [sem(f"stored{k}") for k in range(4)]
    first_in = [sem(f"first_in{k}") for k in range(DT // 2)]
    w1_in, ff_in, squared, rstd_step, scaled, tp_ready = (sem(n) for n in ("w1_in", "ff_in", "squared", "rstd_step", "scaled", "tp_ready"))
    ht_hi_done, ht_lo_done, w_hi_done, w_lo_done, w_used = (sem(n) for n in ("ht_hi", "ht_lo", "w_hi", "w_lo", "w_used"))
    ffw_hi_done, ffw_lo_done, w1_scaled = sem("ffw_hi"), sem("ffw_lo"), sem("w1_scaled")
    acc_ready, banks_free, act_out, summed, qk_rstd, dve_step = (
        sem(n) for n in ("acc_ready", "banks_free", "act_out", "summed", "qk_rstd", "dve_step"))
    with ExitStack() as own:
        def sb(name, shape, dt=F32):
            return own.enter_context(nc.sbuf_tensor("p_" + name, shape, dt))

        ht_hi, ht_lo = sb("ht_hi", [P, DT, S], F32R), sb("ht_lo", [P, DT, S], F32R)
        w_hi = sb("w_hi", [P, NW, BANK], F32R)
        _, first_raw = place_under(nc, ["p_w_lo_low", "p_first_raw"], [[P, DT, BANK]] * 2)
        w_lo = sb("w_lo", [P, NW, BANK], F32R)
        raw = sb("raw", [P, NRAW, BANK])
        stage = sb("stage", [P, 4, BANK])
        xt = sb("xt", [P, 2, DM])
        w1 = sb("w1", [P, DM])
        work = sb("work", [P, BANK])
        ff_raw, ff_hi, ff_lo = sb("ff_raw", [P, DT, FH]), sb("ff_hi", [P, DT, FH], F32R), sb("ff_lo", [P, DT, FH], F32R)
        ss, rstd = sb("ss", [P, 2, 2]), sb("rstd", [P, 2])
        qss, qrs = sb("qss", [P, 2, FH]), sb("qrs", [P, 2, FH])
        acc = own.enter_context(nc.psum_tensor("p_acc", [P, 4, BANK], F32))
        tp = own.enter_context(nc.psum_tensor("p_tp", [P, 4, BANK], F32))
        tpv = tp[:].rearrange("p (u b) (d t) -> p u (b d) t", u=2, t=P)
        x_tiles = inp["x"].rearrange("b (t p) d -> (b t) p d", p=P)
        w_in = inp["w_in"].rearrange("l (d p) n -> p (l d) n", p=P)
        block = own.enter_context(nc.Block())

        def raw_piece(m):
            return first_raw[:, m, :] if m < DT else raw[:, m % NRAW, :]

        def each_group(eng, body):
            with eng.Fori(0, 2) as i:
                for j in range(4):
                    body(i, j, False)
            for i in (2, 3):
                for j in range(4):
                    body(i, j, i == 3)

        def piece_beside(ch, i, j):
            return [8 * (ch + 1) + 4 * (i - 2) + j] if isinstance(i, int) and ch + 1 < CH else []

        @block.sync
        def _(sp):
            def load_x(t, slot):
                sp.dma_start(xt[:, slot, :], x_tiles[t]).then_inc(x_in[slot], 16)

            def load_piece(m):
                ch, d = divmod(m, DT)
                if m >= DT + NRAW:
                    sp.wait_ge(w_lo_done, m - NRAW + 1)
                sp.dma_start(raw[:, m % NRAW, :], w_in[:, d, COLS[ch]:COLS[ch] + BANK]).then_inc(raw_in[m % NRAW], 16)

            load_x(0, 0)
            sp.dma_start(w1[:], bcast(inp["norm1_w"], DM)).then_inc(w1_in, 16)
            for k in range(DT // 2):
                sp.dma_start(first_raw[:, 2 * k:2 * k + 2, :],
                             w_in[:, 2 * k:2 * k + 2, COLS[0]:COLS[0] + BANK]).then_inc(first_in[k], 16)
                if k == 0:
                    load_x(1, 1)
            sp.dma_start(ff_raw[:], w_in[:, :, FF:FF + FH]).then_inc(ff_in, 16)
            sp.wait_ge(tp_ready, 1)
            load_x(2, 0)
            for ch in range(CH):
                def body(i, j, last):
                    if ch == 0 and not (last and j >= 1):
                        sp.wait_ge(tp_ready, 4 * i + j + 2)
                        load_x(4 * i + j + 3, (j + 1) % 2)
                    for m in piece_beside(ch, i, j):
                        if m % DT < DT - NRAW:
                            load_piece(m + NRAW)
                    sp.wait_ge(banks_free, 4 + 16 * ch + 4 * i + j + 1)
                    if ch < NT:
                        dst = tok_out[ch, 4 * i + j]
                    else:
                        dst = ch_out[ch - NT, i, :, j * BANK:(j + 1) * BANK]
                    sp.dma_start(dst, stage[:, j, :]).then_inc(stored[j], 16)
                if ch + 1 < CH:
                    for m in range(NRAW):
                        load_piece(8 * (ch + 1) + m)
                each_group(sp, body)
            for j in range(4):
                sp.wait_ge(stored[j], 16 * 4 * CH)

        @block.gpsimd
        def _(pool):
            steps = [0]

            def tile_rstd(t, slot):
                pool.wait_ge(squared, 2 * t + 2)
                nc.gpsimd.tensor_tensor(rstd[:, slot:slot + 1], ss[:, slot, 0:1], ss[:, slot, 1:2],
                                        ALU.add).then_inc(rstd_step, 1)
                pool.wait_ge(rstd_step, 3 * t + 1)
                nc.gpsimd.tensor_tensor(rstd[:, slot:slot + 1], rstd[:, slot:slot + 1], c["eps_dm"][:],
                                        ALU.add).then_inc(rstd_step, 1)
                pool.wait_ge(rstd_step, 3 * t + 2)
                nc.gpsimd.tensor_tensor(rstd[:, slot:slot + 1], rstd[:, slot:slot + 1], c["neg_half"][:, 0:1],
                                        ALU.pow).then_inc(rstd_step, 1)

            def cut_lo(m):
                s = m % NW
                pool.wait_ge(w_hi_done, m + 1)
                nc.gpsimd.tensor_tensor(w_lo[:, s, :], raw[:, m % NRAW, :], w_hi[:, s, :].bitcast(F32),
                                        ALU.subtract).then_inc(w_lo_done, 1)

            tile_rstd(0, 0)
            tile_rstd(1, 1)
            pool.wait_ge(ffw_hi_done, 1)
            nc.gpsimd.tensor_tensor(ff_lo[:], ff_raw[:], ff_hi[:].bitcast(F32), ALU.subtract).then_inc(ffw_lo_done, 1)
            pool.wait_ge(w_lo_done, DT)
            for ch in range(CH):
                def body(i, j, last):
                    if ch == 0 and not (last and j >= 2):
                        tile_rstd(4 * i + j + 2, j % 2)
                    if ch in (FQ_, FK_):
                        n = 16 * (ch - 1) + 4 * i + j
                        pool.wait_ge(summed, n + 1)
                        nc.gpsimd.tensor_tensor(qrs[:, j % 2, :], qss[:, j % 2, :], c["eps_fd"][:],
                                                ALU.add).then_inc(qk_rstd, 1)
                        pool.wait_ge(qk_rstd, 2 * n + 1)
                        nc.gpsimd.tensor_tensor(qrs[:, j % 2, :], qrs[:, j % 2, :], c["neg_half"][:],
                                                ALU.pow).then_inc(qk_rstd, 1)
                    for m in piece_beside(ch, i, j):
                        cut_lo(m)
                each_group(pool, body)

        @block.scalar
        def _(act):
            def square_tile(i, j):
                act.wait_ge(x_in[j % 2], 16 * (2 * i + j // 2 + 1))
                for half in range(2):
                    act.wait_ge(squared, 2 * (4 * i + j) + half)
                    nc.scalar.activation(work[:], xt[:, j % 2, half * BANK:(half + 1) * BANK], ACT.Square,
                                         accum_out=ss[:, j % 2, half:half + 1]).then_inc(squared, 1)

            def tile_hi(t, slot):
                act.wait_ge(tp_ready, t + 1)
                nc.scalar.copy(ht_hi[:, :, bass.ds(t * P, P)], tpv[:, slot]).then_inc(ht_hi_done, 1)

            def cut_hi(m):
                if m < DT:
                    act.wait_ge(first_in[m // 2], 16)
                else:
                    act.wait_ge(raw_in[m % NRAW], raw_ring.landed(m - DT))
                if m >= NW:
                    ch, d = divmod(m - NW, DT)
                    if d == DT - 1:
                        act.wait_ge(acc_ready, 16 * (ch + 1))
                    else:
                        act.wait_ge(w_used, (DT - 1) * ch + d + 1)
                nc.scalar.copy(w_hi[:, m % NW, :], raw_piece(m)).then_inc(w_hi_done, 1)

            square_tile(0, 0)
            for m in (0, 1):
                cut_hi(m)
            square_tile(0, 1)
            for m in (2, 3):
                cut_hi(m)
            tile_hi(0, 0)
            for m in range(4, DT):
                cut_hi(m)
            act.wait_ge(ff_in, 16)
            nc.scalar.copy(ff_hi[:], ff_raw[:]).then_inc(ffw_hi_done, 1)
            for ch in range(CH):
                def body(i, j, last):
                    n = 16 * ch + 4 * i + j
                    if ch == 0:
                        if not (last and j == 3):
                            tile_hi(4 * i + j + 1, (j + 1) % 2)
                        if not (last and j >= 2):
                            square_tile(i + (j + 2) // 4, (j + 2) % 4)
                    for m in piece_beside(ch, i, j):
                        cut_hi(m)
                    k = {FQ_: 0, FK_: 1, G_: 2, CH - 1: 3}.get(ch)
                    if k is not None:
                        act.wait_ge(acc_ready, n + 1)
                        act.wait_ge(banks_free, 4 + n)
                        nc.scalar.activation(work[:], acc[:, j, :],
                                             ACT.Square if ch in (FQ_, FK_) else ACT.Sigmoid).then_inc(act_out, 1)
                each_group(act, body)

        @block.vector
        def _(dve):
            def scale_tile(t, slot):
                dve.wait_ge(rstd_step, 3 * t + 3)
                nc.vector.scalar_tensor_tensor(xt[:, slot, :], xt[:, slot, :], rstd[:, slot:slot + 1], w1[:],
                                               ALU.mult, ALU.mult).then_inc(scaled, 1)

            def tile_lo(t, slot):
                dve.wait_ge(ht_hi_done, t + 1)
                nc.vector.tensor_tensor(ht_lo[:, :, bass.ds(t * P, P)], tpv[:, slot],
                                        ht_hi[:, :, bass.ds(t * P, P)].bitcast(F32), ALU.subtract).then_inc(ht_lo_done, 1)

            def cut_lo(m):
                dve.wait_ge(w_hi_done, m + 1)
                nc.vector.tensor_tensor(w_lo[:, m, :], raw_piece(m), w_hi[:, m, :].bitcast(F32), ALU.subtract).then_inc(w_lo_done, 1)

            dve.sem_inc(banks_free, 4)
            dve.wait_ge(w1_in, 16)
            nc.vector.tensor_scalar(w1[:], w1[:], float(DM) ** 0.5, None, ALU.mult).then_inc(w1_scaled, 1)
            dve.wait_ge(w1_scaled, 1)
            scale_tile(0, 0)
            for m in range(4):
                cut_lo(m)
            scale_tile(1, 1)
            tile_lo(0, 0)
            for m in range(4, DT):
                cut_lo(m)
            for ch in range(CH):
                def body(i, j, last):
                    n = 16 * ch + 4 * i + j
                    if ch == 0:
                        if not (last and j == 3):
                            tile_lo(4 * i + j + 1, (j + 1) % 2)
                        if not (last and j >= 2):
                            scale_tile(4 * i + j + 2, j % 2)
                    dve.wait_ge(acc_ready, n + 1)
                    src, dst = acc[:, j, :], stage[:, j, :]
                    if ch in (FQ_, FK_):
                        k = n - 16 * FQ_
                        dve.wait_ge(act_out, k + 1)
                        nc.vector.tensor_reduce(qss[:, j % 2, :], work[:].rearrange("p (h e) -> p h e", h=FH),
                                                AX.X, ALU.add).then_inc(summed, 1)
                    dve.wait_ge(stored[j], 16 * (4 * ch + i))
                    if ch in (V_, FV_):
                        if ch == FV_:
                            nc.vector.tensor_copy(c["ff_logit"][:, 4 * i + j, :], tp[:, j, 0:FH])
                        nc.vector.tensor_copy(dst, src).then_inc(banks_free, 1)
                    elif ch in (FQ_, FK_):
                        heads = dst.rearrange("p (h e) -> p h e", h=FH)
                        nc.vector.tensor_tensor(heads, src.rearrange("p (h e) -> p h e", h=FH),
                                                c["qk_w"][:, ch - FQ_:ch - FQ_ + 1, :].broadcast_to([P, FH, FD]),
                                                ALU.mult).then_inc(dve_step, 1)
                        dve.wait_ge(dve_step, k + 1)
                        dve.wait_ge(qk_rstd, 2 * k + 2)
                        nc.vector.tensor_tensor(heads, heads, qrs[:, j % 2, :].unsqueeze(2).broadcast_to([P, FH, FD]),
                                                ALU.mult).then_inc(banks_free, 1)
                    elif ch == G_:
                        k = n - 32
                        dve.wait_ge(act_out, 32 + n - 16 * G_ + 1)
                        nc.vector.tensor_tensor(dst, src, work[:], ALU.mult).then_inc(dve_step, 1)
                        dve.wait_ge(dve_step, 32 + n - 16 * G_ + 1)
                        nc.vector.tensor_tensor(dst.rearrange("p (h e) -> p h e", h=HH),
                                                dst.rearrange("p (h e) -> p h e", h=HH),
                                                c["hgrn_w"][:].unsqueeze(1).broadcast_to([P, HH, P]),
                                                ALU.mult).then_inc(banks_free, 1)
                    elif ch == NT:
                        nc.vector.tensor_scalar(dst, src, float(P) ** -0.5, None, ALU.mult).then_inc(banks_free, 1)
                    else:
                        dve.wait_ge(act_out, 48 + n - 16 * (CH - 1) + 1)
                        nc.vector.tensor_scalar(dst, work[:], c["one_minus_lb"][:, bass.ds(i, 1)],
                                                c["lb"][:, bass.ds(i, 1)], ALU.mult, ALU.add).then_inc(banks_free, 1)
                each_group(dve, body)

        @block.tensor
        def _(pe):
            def transpose_tile(t, slot):
                pe.wait_ge(scaled, t + 1)
                for d in range(DT):
                    last = nc.tensor.transpose(tpv[:, slot, d, :], xt[:, slot, d * P:(d + 1) * P], c["ident"][:])
                last.then_inc(tp_ready, 1)

            transpose_tile(0, 0)

            def token_major(ch, first):
                for t in range(TT):
                    tok = slice(t * P, (t + 1) * P)
                    if first:
                        if t + 1 < TT:
                            pe.wait_ge(ht_lo_done, t)
                            transpose_tile(t + 1, (t + 1) % 2)
                        pe.wait_ge(ht_lo_done, t + 1)
                    pe.wait_ge(banks_free, 16 * ch + t + 1)
                    if isinstance(ch, int) and ch == FV_:
                        pe.wait_ge(ffw_lo_done, 1)
                        for d in range(DT):
                            three_pass(nc, tp[:, t % 4, 0:FH], ht_hi[:, d, tok], ht_lo[:, d, tok], ff_hi[:, d, :],
                                       ff_lo[:, d, :], d == 0, d == DT - 1)
                    for d in range(DT):
                        s = DT * (ch % 2) + d
                        if t == 0:
                            pe.wait_ge(w_lo_done, DT * ch + d + 1)
                        m = three_pass(nc, acc[:, t % 4, :], ht_hi[:, d, tok], ht_lo[:, d, tok], w_hi[:, s, :],
                                       w_lo[:, s, :], d == 0, d == DT - 1)
                        if t == TT - 1 and d < DT - 1:
                            m.then_inc(w_used, 1)
                    m.then_inc(acc_ready, 1)

            def channel_major(ch):
                for k in range(4):
                    col = slice(k * P, (k + 1) * P)
                    with pe.Fori(0, 4) as g:
                        pe.wait_ge(banks_free, 16 * ch + 4 * k + g + 1)
                        for d in range(DT):
                            s = DT * (ch % 2) + d
                            if k == 0:
                                pe.wait_ge(w_lo_done, DT * ch + d + 1)
                            tok = bass.ds(g * BANK, BANK)
                            m = three_pass(nc, acc[:, g, :], w_hi[:, s, col], w_lo[:, s, col], ht_hi[:, d, tok],
                                           ht_lo[:, d, tok], d == 0, d == DT - 1)
                        m.then_inc(acc_ready, 1)

            token_major(0, True)
            with pe.Fori(1, FV_) as ch:
                token_major(ch, False)
            token_major(FV_, False)
            token_major(G_, False)
            channel_major(NT)
            channel_major(NT + 1)


LV = 7
UN = BANK // P


def recurrence(nc, ctx, c, tok_in, ch_in, mix_out):
    def sem(name):
        return ctx.enter_context(nc.semaphore("r_" + name))

    q_in, f_in, v_in, g_in = ([sem(f"{n}_in{k}") for k in range(4)] for n in "qfvg")
    stored = [sem(f"stored{k}") for k in range(2)]
    (zeroed, blank_done, mask_step, masks_done, k_done, lnf_done, b_done, eb_done, d_done, e_done, ql_done, kl_done, a_ready, pm_done,
     kdt_ready, kdt_done, kdv_ready, s_done, o_ready, osq_done, orstd, fin) = (sem(n) for n in (
         "zeroed", "blank_done", "mask_step", "masks_done", "k_done", "lnf_done", "b_done", "eb_done", "d_done", "e_done", "ql_done",
         "kl_done", "a_ready", "pm_done", "kdt_ready", "kdt_done", "kdv_ready", "s_done", "o_ready",
         "osq_done", "orstd", "fin"))
    with ExitStack() as own:
        def sb(name, shape, dt=F32):
            return own.enter_context(nc.sbuf_tensor("r_" + name, shape, dt))

        def ps(name, shape):
            return own.enter_context(nc.psum_tensor("r_" + name, shape, F32))

        q, f = sb("q", [P, 4, BANK]), sb("f", [P, 4, BANK])
        v, g = sb("v", [P, 4, UN, P]), sb("g", [P, 4, UN, P])
        lnf, b = sb("lnf", [P, BANK]), sb("b", [P, BANK])
        eb, k = sb("eb", [P, 2, BANK]), sb("k", [P, 2, BANK])
        e = sb("e", [P, 2, LV + 1, BANK])
        ql, kl = sb("ql", [P, 2, LV, BANK]), sb("kl", [P, 2, LV, BANK])
        qb, kd = sb("qb", [P, 2, BANK]), sb("kd", [P, 2, BANK])
        ones = sb("ones", [P, BANK])
        keep = sb("keep", [P, BANK])
        mask = sb("mask", [P, LV + 1, P])
        pm = sb("pm", [P, 2, LV + 1, P])
        kdt = sb("kdt", [P, 2, P])
        state = sb("state", [P, 2, P])
        junk, oss, ors = sb("junk", [P, 2, P]), sb("oss", [P, 2]), sb("ors", [P, 2])
        mix = sb("mix", [P, 2, UN, P])
        a_ps = [ps(f"a{n}", [P, LV + 1, P]) for n in range(2)]
        kdt_ps, kdv_ps = ps("kdt_ps", [P, BANK]), ps("kdv_ps", [P, BANK])
        o_ps = [ps(f"o{n}", [P, BANK]) for n in range(2)]
        block = own.enter_context(nc.Block())

        def halves(ap, lvl):
            w = 64 >> lvl
            return ap.rearrange("p (n two w) -> p n two w", two=2, w=w)

        def each_head(eng, prologue, unit, epilogue):
            prologue()
            with eng.Fori(0, HH - 1) as h:
                for u in range(4):
                    unit(h, u)
                epilogue(h)
            for u in range(4):
                unit(HH - 1, u)
            epilogue(HH - 1)

        def nxt(h, u, by=1):
            return h + (u + by) // 4, (u + by) % 4

        def next_chunk(h, i):
            if isinstance(h, int) and i == 15:
                return None
            return h + (i + 1) // 16, (i + 1) % 16

        EXPONENTS = ((), (0, 1, 2, 3), (4, 5, 6), (7,), ())

        def first_parts(prepare):
            for part in range(5):
                prepare(0, 0, part)
            prepare(0, 1, 0)
            prepare(0, 1, 1)

        def prepare_beside(prepare, h, u, chunk):
            for by, part in (((1, 2),), ((1, 3),), ((1, 4), (2, 0)), ((2, 1),))[chunk]:
                if not (isinstance(h, int) and u + by > 3):
                    prepare(*nxt(h, u, by), part)

        @block.sync
        def _(sp):
            def load(h, u):
                sp.dma_start(q[:, u, :], ch_in[0, h, :, u * BANK:(u + 1) * BANK]).then_inc(q_in[u], 16)
                sp.dma_start(f[:, u, :], ch_in[1, h, :, u * BANK:(u + 1) * BANK]).then_inc(f_in[u], 16)
                for dst, group, done in ((v, V_, v_in), (g, G_, g_in)):
                    src = tok_in[group, u * UN:(u + 1) * UN, :, bass.ds(h * P, P)].rearrange("t p e -> p t e")
                    sp.dma_start(dst[:, u], src).then_inc(done[u], 16)

            def prologue():
                for u in range(3):
                    load(0, u)

            def unit(h, u):
                sp.wait_ge(fin, 16 * h + 4 * u + 4)
                dst = mix_out[u * UN:(u + 1) * UN, :, bass.ds(h * P, P)].rearrange("t p e -> p t e")
                sp.dma_start(dst, mix[:, u % 2]).then_inc(stored[u % 2], 16)
                if not (isinstance(h, int) and u > 0):
                    load(*nxt(h, u, 3))

            each_head(sp, prologue, unit, lambda h: None)
            for n in range(2):
                sp.wait_ge(stored[n], 16 * 2 * HH)

        @block.gpsimd
        def _(pool):
            def prologue():
                pool.sem_inc(kl_done, 8)
                nc.gpsimd.memset(kl[:, 0], 0.0).then_inc(zeroed, 1)
                pool.wait_ge(zeroed, 1)
                for part in range(5):
                    prepare(0, 0, part)
                nc.gpsimd.memset(mask[:], 1.0).then_inc(mask_step, 1)
                pool.wait_ge(mask_step, 1)
                step = 1
                for lvl in range(1, LV):
                    w2 = 128 >> lvl
                    m = mask[:, lvl, :].rearrange("p (n w) -> p n w", w=w2)
                    nc.gpsimd.affine_select(out=m, in_=m, compare_op=ALU.is_ge, fill=0.0, base=0,
                                            pattern=[[-w2, P // w2], [0, w2]], channel_multiplier=1).then_inc(mask_step, 1)
                    step += 1
                    pool.wait_ge(mask_step, step)
                    nc.gpsimd.affine_select(out=m, in_=m, compare_op=ALU.is_ge, fill=0.0, base=w2 - 1,
                                            pattern=[[w2, P // w2], [0, w2]], channel_multiplier=-1).then_inc(mask_step, 1)
                    step += 1
                nc.gpsimd.tensor_copy(mask[:, LV, :], c["ident"][:]).then_inc(mask_step, 1)
                step += 1
                pool.wait_ge(mask_step, step)
                pool.sem_inc(masks_done, 1)
                nc.gpsimd.memset(kl[:, 1], 0.0).then_inc(zeroed, 1)
                pool.wait_ge(zeroed, 2)

            def prepare(h, u, part):
                n = 4 * h + u
                if part == 2:
                    if isinstance(n, int) and n == 0:
                        pool.wait_ge(blank_done, 1)
                    pool.wait_ge(f_in[u], 16 * (h + 1))
                    if not (isinstance(n, int) and n < 2):
                        pool.wait_ge(a_ready, 4 * n - 4)
                    nc.gpsimd.tensor_tensor(k[:, u % 2, :], ones[:], f[:, u, :], ALU.subtract).then_inc(k_done, 1)
                    pool.wait_ge(k_done, n + 1)
                for lvl in ((), (), (0, 1, 2), (3, 4, 5), (6, 7))[part]:
                    pool.wait_ge(e_done, 8 * n + lvl + 1)
                    if lvl < LV:
                        dst = halves(kl[:, u % 2, lvl, :], lvl)[:, :, 0, :]
                        src = halves(k[:, u % 2, :], lvl)[:, :, 0, :]
                        by = halves(e[:, u % 2, lvl, :], lvl)[:, :, 0, :]
                    else:
                        dst, src, by = kd[:, u % 2, :], k[:, u % 2, :], e[:, u % 2, LV, :]
                    nc.gpsimd.tensor_tensor(dst, src, by, ALU.mult).then_inc(kl_done, 1)

            def out_rstd(h, i):
                n = 16 * h + i
                s = slice(i % 2, i % 2 + 1)
                pool.wait_ge(osq_done, n + 1)
                pool.wait_ge(fin, n - 1 if i >= 2 else 16 * h)
                nc.gpsimd.tensor_tensor(ors[:, s], oss[:, s], c["eps_p"][:], ALU.add).then_inc(orstd, 1)
                pool.wait_ge(orstd, 2 * n + 1)
                nc.gpsimd.tensor_tensor(ors[:, s], ors[:, s], c["neg_half"][:, 0:1], ALU.pow).then_inc(orstd, 1)

            def unit(h, u):
                for part in range(4):
                    i = 4 * u + part
                    if i >= 1:
                        out_rstd(h, i - 1)
                    prepare_beside(prepare, h, u, part)

            each_head(pool, prologue, unit, lambda h: out_rstd(h, 15))

        @block.scalar
        def _(act):
            def prepare(h, u, part):
                n = 4 * h + u
                if part == 0:
                    act.wait_ge(f_in[u], 16 * (h + 1))
                    nc.scalar.activation(lnf[:], f[:, u, :], ACT.Ln).then_inc(lnf_done, 1)
                if part == 2:
                    act.wait_ge(b_done, n + 1)
                    if not (isinstance(n, int) and n < 2):
                        act.wait_ge(s_done, 4 * n - 4)
                    nc.scalar.activation(eb[:, u % 2, :], b[:], ACT.Exp).then_inc(eb_done, 1)
                for lvl in EXPONENTS[part]:
                    act.wait_ge(d_done, 8 * n + lvl + 1)
                    if lvl < LV:
                        ev = halves(e[:, u % 2, lvl, :], lvl)
                        nc.scalar.activation(ev[:, :, 1, :], ev[:, :, 1, :], ACT.Exp)
                        nc.scalar.activation(ev[:, :, 0, :], ev[:, :, 0, :], ACT.Exp, scale=-1.0).then_inc(e_done, 1)
                    else:
                        nc.scalar.activation(e[:, u % 2, LV, :], e[:, u % 2, LV, :], ACT.Exp, scale=-1.0).then_inc(e_done, 1)

            def turned(h, i):
                n = 16 * h + i
                act.wait_ge(kdt_ready, n + 1)
                if not (isinstance(n, int) and n < 2):
                    act.wait_ge(kdv_ready, n - 1)
                nc.scalar.copy(kdt[:, i % 2, :], kdt_ps[:, 0:P]).then_inc(kdt_done, 1)

            def square_out(h, i):
                n = 16 * h + i
                act.wait_ge(o_ready, n + 1)
                act.wait_ge(orstd, 2 * (n - 1) if i >= 2 else 32 * h)
                nc.scalar.activation(junk[:, i % 2, :], o_ps[i % 2][:, 0:P], ACT.Square,
                                     accum_out=oss[:, i % 2:i % 2 + 1]).then_inc(osq_done, 1)

            def unit(h, u):
                for part in range(4):
                    i = 4 * u + part
                    if next_chunk(h, i):
                        turned(*next_chunk(h, i))
                    if i >= 1:
                        square_out(h, i - 1)
                    prepare_beside(prepare, h, u, part)

            def prologue():
                first_parts(prepare)
                turned(0, 0)

            each_head(act, prologue, unit, lambda h: square_out(h, 15))

        @block.vector
        def _(dve):
            def prepare(h, u, part):
                n = 4 * h + u
                if part == 0:
                    dve.wait_ge(lnf_done, n + 1)
                    dve.wait_ge(eb_done, n)
                    nc.vector.tensor_tensor_scan(b[:], keep[:], lnf[:], 0.0, ALU.mult, ALU.add).then_inc(b_done, 1)
                    dve.wait_ge(b_done, n + 1)
                for lvl in EXPONENTS[part]:
                    if not (isinstance(n, int) and n < 2):
                        dve.wait_ge(kl_done, 8 * n + lvl - 7)
                    w2 = 128 >> lvl if lvl < LV else P
                    bv = b[:].rearrange("p (n w) -> p n w", w=w2)
                    at = w2 // 2 - 1 if lvl < LV else P - 1
                    nc.vector.tensor_tensor(e[:, u % 2, lvl, :].rearrange("p (n w) -> p n w", w=w2), bv,
                                            bv[:, :, at:at + 1].broadcast_to([P, BANK // w2, w2]),
                                            ALU.subtract).then_inc(d_done, 1)
                for lvl in ((), (), (0, 1), (2, 3, 4, 5), (6, 7))[part]:
                    if lvl in (0, LV) and not (isinstance(n, int) and n < 2):
                        dve.wait_ge(o_ready if lvl else a_ready, 4 * n - 4)
                    if lvl < LV:
                        dve.wait_ge(e_done, 8 * n + lvl + 1)
                        if lvl == 0:
                            dve.wait_ge(q_in[u], 16 * (h + 1))
                        dst = halves(ql[:, u % 2, lvl, :], lvl)[:, :, 1, :]
                        src = halves(q[:, u, :], lvl)[:, :, 1, :]
                        by = halves(e[:, u % 2, lvl, :], lvl)[:, :, 1, :]
                    else:
                        dve.wait_ge(eb_done, n + 1)
                        dst, src, by = qb[:, u % 2, :], q[:, u, :], eb[:, u % 2, :]
                    nc.vector.tensor_tensor(dst, src, by, ALU.mult).then_inc(ql_done, 1)

            def mask_levels(h, i):
                n = 16 * h + i
                dve.wait_ge(a_ready, n + 1)
                if i >= 2:
                    dve.wait_ge(o_ready, n - 1)
                nc.vector.tensor_tensor(pm[:, i % 2], a_ps[i % 2][:], mask[:], ALU.mult).then_inc(pm_done, 1)

            def step_state(h, i):
                n = 16 * h + i
                dve.wait_ge(kdv_ready, n + 1)
                new = state[:, (i + 1) % 2, :]
                if i == 0:
                    nc.vector.tensor_copy(new, kdv_ps[:, 0:P]).then_inc(s_done, 1)
                else:
                    dve.wait_ge(s_done, n)
                    at = (i % 4) * P + P - 1
                    nc.vector.scalar_tensor_tensor(new, state[:, i % 2, :], eb[:, i // 4 % 2, at:at + 1], kdv_ps[:, 0:P],
                                                   ALU.mult, ALU.add).then_inc(s_done, 1)

            def finish(h, i):
                n = 16 * h + i
                u, ch = i // 4, i % 4
                dve.wait_ge(orstd, 2 * n + 2)
                if ch == 0:
                    dve.wait_ge(g_in[u], 16 * (h + 1))
                    dve.wait_ge(stored[u % 2], 16 * (2 * h + u // 2))
                nc.vector.scalar_tensor_tensor(mix[:, u % 2, ch, :], o_ps[i % 2][:, 0:P], ors[:, i % 2:i % 2 + 1],
                                               g[:, u, ch, :], ALU.mult, ALU.mult).then_inc(fin, 1)

            def unit(h, u):
                for part in range(4):
                    i = 4 * u + part
                    mask_levels(h, i)
                    step_state(h, i)
                    if i >= 2:
                        finish(h, i - 2)
                    prepare_beside(prepare, h, u, part)

            def prologue():
                nc.vector.memset(ones[:], 1.0).then_inc(blank_done, 1)
                nc.vector.memset(keep[:], 1.0).then_inc(blank_done, 1)
                dve.wait_ge(blank_done, 2)
                nc.vector.memset(keep[:].rearrange("p (n w) -> p n w", w=P)[:, :, 0:1], 0.0).then_inc(blank_done, 1)
                dve.wait_ge(blank_done, 3)
                prepare(0, 0, 0)
                prepare(0, 0, 1)
                nc.vector.memset(ql[:, 0], 0.0).then_inc(blank_done, 1)
                dve.wait_ge(blank_done, 4)
                for part in range(2, 5):
                    prepare(0, 0, part)
                nc.vector.memset(ql[:, 1], 0.0).then_inc(blank_done, 1)
                prepare(0, 1, 0)
                prepare(0, 1, 1)
                dve.wait_ge(blank_done, 5)
                dve.wait_ge(masks_done, 1)

            def epilogue(h):
                finish(h, 14)
                finish(h, 15)

            each_head(dve, prologue, unit, epilogue)

        @block.tensor
        def _(pe):
            def level_products(h, i):
                n, u = 16 * h + i, i // 4
                t = slice(i % 4 * P, i % 4 * P + P)
                if i % 4 == 0:
                    pe.wait_ge(ql_done, 8 * (4 * h + u) + 8)
                    pe.wait_ge(kl_done, 8 * (4 * h + u) + 16)
                if i >= 2:
                    pe.wait_ge(pm_done, n - 1)
                for lvl in range(LV):
                    nc.tensor.matmul(a_ps[i % 2][:, lvl, :], kl[:, u % 2, lvl, t], ql[:, u % 2, lvl, t], start=True, stop=True)
                nc.tensor.matmul(a_ps[i % 2][:, LV, :], k[:, u % 2, t], q[:, u, t], start=True, stop=True).then_inc(a_ready, 1)

            def turn(h, i):
                n, u = 16 * h + i, i // 4
                if i % 4 == 0:
                    pe.wait_ge(kl_done, 8 * (4 * h + u) + 16)
                if not (isinstance(n, int) and n < 1):
                    pe.wait_ge(kdt_done, n)
                nc.tensor.transpose(kdt_ps[:, 0:P], kd[:, u % 2, i % 4 * P:(i % 4 + 1) * P],
                                    c["ident"][:]).then_inc(kdt_ready, 1)

            def output(h, i):
                n, u, ch = 16 * h + i, i // 4, i % 4
                t = slice(ch * P, ch * P + P)
                if ch == 0:
                    pe.wait_ge(v_in[u], 16 * (h + 1))
                pe.wait_ge(pm_done, n + 1)
                pe.wait_ge(fin, n - 1 if i >= 2 else 16 * h)
                for lvl in range(LV + 1):
                    m = nc.tensor.matmul(o_ps[i % 2][:, 0:P], pm[:, i % 2, lvl, :], v[:, u, ch, :], start=lvl == 0,
                                         stop=i == 0 and lvl == LV)
                if i > 0:
                    pe.wait_ge(s_done, n)
                    m = nc.tensor.matmul(o_ps[i % 2][:, 0:P], qb[:, u % 2, t], state[:, i % 2, :], start=False, stop=True)
                m.then_inc(o_ready, 1)

            def unit(h, u):
                for part in range(4):
                    i = 4 * u + part
                    n = 16 * h + i
                    level_products(h, i)
                    if next_chunk(h, i):
                        turn(*next_chunk(h, i))
                    if i >= 1:
                        output(h, i - 1)
                    pe.wait_ge(kdt_done, n + 1)
                    pe.wait_ge(s_done, n)
                    if part == 0:
                        pe.wait_ge(v_in[u], 16 * (h + 1))
                    nc.tensor.matmul(kdv_ps[:, 0:P], kdt[:, i % 2, :], v[:, u, part, :], start=True, stop=True).then_inc(kdv_ready, 1)

            each_head(pe, lambda: turn(0, 0), unit, lambda h: output(h, 15))


KB = S // P
QG = KB // 4
SW = 2 * BANK
FAR = 2.0 ** 100


class Head:

    def __init__(self, n, slot, half):
        self.n, self.slot, self.half = n, slot, half

    def next(self):
        return Head(self.n + 1, 1 - self.slot, self.half + self.slot)

    def last(self):
        return Head(self.n - 1, 1 - self.slot, self.half - 1 + self.slot)


def tile_parts(i):
    n = (i + 1) * P
    if i == KB - 1:
        return [BANK] * 2 + [BANK // 2] * 4
    return [min(BANK, n - at) for at in range(0, n, BANK)]




S_RING, T_RING, LAG = 3, 4, 3
S_ITEMS = sum(len(tile_parts(i)) for i in range(KB))
T_ITEMS = sum(4 * g + 4 for g in range(QG))
PREP = 3 * QG
RING = T_ITEMS + PREP + QG
assert RING % T_RING == 0 and S_ITEMS % S_RING == 0


def head_order(first=False, last=False, tail=False):
    def blocks_of(g):
        return [(0 if g < QG - 1 else 1, g, kb) for kb in range(4 * g + 4)]

    order = []
    for g in range(1 if tail else QG):
        tg = (g - 1) % QG
        blocks = [] if first and g == 0 else blocks_of(tg)
        before = [(1, tg - 1, kb) for kb in range(4 * tg)] if g == 0 else blocks_of((g - 2) % QG)
        if first and g <= 1:
            before = []
        due = before[-LAG:] + blocks
        work = []
        for k, block in enumerate(blocks):
            work.append([("block",) + block])
            if before or k >= LAG:
                work[-1].append(("product",) + due[k if before else k - LAG])
            if k == LAG - 1 and before:
                work[-1].append(("copy",) + before[-1][:2])
            if k == LAG and before:
                work[-1].append(("fold",) + before[-1][:2])
        if tail:
            work += [[("product",) + block] for block in due[-LAG:]] + [[("copy",) + due[-1][:2], ("fold",) + due[-1][:2]]]
            return [item for items in work for item in items]
        if not last and g > 0:
            for k in range(4):
                work.insert((k + 1) * (len(blocks) + 4) // 5, [("prep", 4 * (g - 1) + k)])
        order.append(("step", g))
        done, delayed = 0, []
        scores = [(i, part) for i in range(4 * g, 4 * g + 4) for part in range(len(tile_parts(i)))]
        for k, (i, part) in enumerate(scores):
            order.append(("score", i, part))
            upto = len(work) * max(0, k + 2 - S_RING) // (len(scores) + 1 - S_RING)
            for items in work[done:upto]:
                order += items + delayed
                delayed = []
            done = upto
            if part == len(tile_parts(i)) - 1:
                delayed.append(("exp", i))
            if len(delayed) > 1:
                order.append(delayed.pop(0))
        order += delayed
    return order


def ring_kinds(order):
    return [item[0] for item in order if item[0] in ("block", "prep", "fold")]


def attention(nc, ctx, c, inp, tok_in, cum_dram, mix_out):
    def sem(name):
        return ctx.enter_context(nc.semaphore("a_" + name))

    names = ("bias_in", "gate_dve", "gate_act", "gate_pe", "gate_pool", "cum_stored", "consts_done", "q_in", "k_in", "v_in",
             "s_ready", "scored", "p_ready", "t_ready", "t_hi", "t_lo", "u_out", "hi_done", "k_cut", "q_cut", "v_cut",
             "pv_done", "o_copied", "fin", "recip_done")
    (bias_in, gate_dve, gate_act, gate_pe, gate_pool, cum_stored, consts_done, q_in, k_in, v_in, s_ready, scored, p_ready,
     t_ready, t_hi, t_lo, u_out, hi_done, k_cut, q_cut, v_cut, pv_done, o_copied, fin, recip_done) = (sem(n) for n in names)
    passed_dve, passed_pool, passed_sp = sem("passed_dve"), sem("passed_pool"), sem("passed_sp")
    cb_in = [sem(f"cb_in{n}") for n in range(2)]
    stored = [sem(f"stored{n}") for n in range(2)]
    with ExitStack() as own:
        def sb(name, shape, dt=F32):
            return own.enter_context(nc.sbuf_tensor("a_" + name, shape, dt))

        def ps(name, shape):
            return own.enter_context(nc.psum_tensor("a_" + name, shape, F32))

        kst, q1, q2 = (sb(n, [P, 2, S], F32R) for n in ("kst", "q1", "q2"))
        vcat = sb("vcat", [P, 2, KB, P], F32R)
        cb = sb("cb", [P, 2, S])
        qraw, kraw, vraw = (sb(n, [P, KB, FD]) for n in ("qraw", "kraw", "vraw"))
        kcat, qcat1, qcat2 = (sb(n, [P, KB, 2, FD], F32R) for n in ("kcat", "qcat1", "qcat2"))
        p = sb("p", [P, 2, 4, S])
        pt_hi, pt_lo = sb("pt_hi", [P, 4, BANK], F32R), sb("pt_lo", [P, 4, BANK], F32R)
        ot = sb("ot", [P, BANK])
        stage = sb("stage", [P, 2, KB, FD])
        low = sb("low", [P, KB, 6])
        total, recip = sb("total", [P, QG, 4]), sb("recip", [P, QG, 4])
        ident_r, beyond_r, beyond = sb("ident_r", [P, P], F32R), sb("beyond_r", [P, P], F32R), sb("beyond", [P, P])
        fold = sb("fold", [P, FD])
        bias = sb("bias", [P, FH])
        gx, gy, gz, prefix, gi = sb("gx", [P, P]), sb("gy", [P, P]), sb("gz", [P, P]), sb("prefix", [P, P]), sb("gi", [P, P], mybir.dt.int32)
        s_ps = [ps(f"s{n}", [P, BANK]) for n in range(S_RING)]
        t_ps = [ps(f"t{n}", [P, BANK]) for n in range(T_RING)]
        o_ps = ps("o", [P, BANK])
        own_block = own.enter_context(ExitStack())

        def load(sp, h):
            for dst, group, done in ((kraw, FK_, k_in), (qraw, FQ_, q_in), (vraw, FV_, v_in)):
                sp.dma_start(dst[:], tok_in[group, :, :, bass.ds(h.n * FD, FD)].rearrange("t p e -> p t e")).then_inc(done, 16)

        def load_gate(sp, h):
            row = cum_dram[bass.ds(h.n, 1), :].partition_broadcast(P)
            sp.dma_start(cb[:, h.slot:h.slot + 1, :], row).then_inc(cb_in[h.slot], 16)

        def cut_pair(eng, ops, raw, hi, lo, counter, count, done):
            ops.tensor_copy(hi, raw[:]).then_inc(counter, 1)
            eng.wait_ge(counter, count)
            ops.tensor_tensor(lo, raw[:], hi.bitcast(F32), ALU.subtract).then_inc(done, 1)

        def cut_k(eng, ops, counter, count):
            cut_pair(eng, ops, kraw, kcat[:, :, 0, :], kcat[:, :, 1, :], counter, count, k_cut)

        def cut_q(eng, ops, counter, count):
            ops.tensor_copy(qcat1[:, :, 1, :], qraw[:]).then_inc(q_cut, 1)
            cut_pair(eng, ops, qraw, qcat1[:, :, 0, :], qcat2[:, :, 0, :], counter, count, q_cut)
            ops.tensor_tensor(qcat2[:, :, 1, :], qraw[:], qcat1[:, :, 0, :].bitcast(F32), ALU.subtract).then_inc(q_cut, 1)

        def cut_v(eng, ops, h, counter, count):
            cut_pair(eng, ops, vraw, vcat[:, h.slot, :, 0:FD], vcat[:, h.slot, :, FD:P], counter, count, v_cut)

        def unit_places(h, u):
            part, quarter = u // QG, u % QG
            return (kcat, qcat1, qcat2)[part], (kst, q1, q2)[part][:, h.slot, quarter * BANK:(quarter + 1) * BANK], range(4 * quarter, 4 * quarter + 4)

        def unit_out(act, h, u, slot, ring):
            act.wait_ge(t_ready, ring + 1)
            nc.scalar.copy(unit_places(h, u)[1], t_ps[slot][:]).then_inc(u_out, 1)

        def unit_in(pe, h, u, slot):
            cat, _, tiles = unit_places(h, u)
            if u == 0:
                pe.wait_ge(k_cut, h.n + 1)
            elif u == QG:
                pe.wait_ge(q_cut, 3 * (h.n + 1))
            for k, t in enumerate(tiles):
                m = nc.tensor.matmul(t_ps[slot][:, k * P:(k + 1) * P], cat[:, t].rearrange("p two e -> p (two e)"), ident_r[:],
                                     start=True, stop=True)
            m.then_inc(t_ready, 1)

        first_head = Head(0, 0, 0)
        with nc.Block() as block:
            @block.sync
            def _(sp):
                sp.dma_start(bias[:], bcast(inp["fox_f_bias"], FH)).then_inc(bias_in, 16)
                load(sp, first_head)
                sp.wait_ge(gate_dve, 8)
                for t in range(TT):
                    sp.dma_start(cum_dram[:, t * P:(t + 1) * P], gz[t * FH:(t + 1) * FH, :]).then_inc(cum_stored, 16)
                sp.wait_ge(cum_stored, 16 * TT)
                load_gate(sp, first_head)
                sp.wait_ge(k_cut, 1)
                sp.wait_ge(q_cut, 3)
                sp.wait_ge(v_cut, 1)
                load(sp, first_head.next())

            @block.gpsimd
            def _(pool):
                nc.gpsimd.iota(gi[:], pattern=[[1, P]], base=0, channel_multiplier=-1).then_inc(gate_pool, 1)
                nc.gpsimd.memset(beyond[:], 0.0).then_inc(gate_pool, 1)
                pool.wait_ge(gate_pool, 2)
                nc.gpsimd.affine_select(out=beyond[:], in_=beyond[:], compare_op=ALU.is_ge, fill=FAR, base=0,
                                        pattern=[[-1, P]], channel_multiplier=1).then_inc(gate_pool, 1)
                pool.wait_ge(consts_done, 3)
                nc.gpsimd.affine_select(out=prefix[:], in_=prefix[:], compare_op=ALU.is_gt, fill=0.0, base=0,
                                        pattern=[[1, P]], channel_multiplier=-1).then_inc(gate_pool, 1)
                pool.wait_ge(gate_pool, 4)

            @block.scalar
            def _(act):
                act.wait_ge(gate_dve, 1)
                nc.scalar.activation(gy[:], gx[:], ACT.Abs).then_inc(gate_act, 1)
                act.wait_ge(gate_act, 1)
                nc.scalar.activation(gy[:], gy[:], ACT.Exp, scale=-1.0).then_inc(gate_act, 1)
                act.wait_ge(gate_act, 2)
                nc.scalar.activation(gy[:], gy[:], ACT.Ln, bias=1.0).then_inc(gate_act, 1)
                act.wait_ge(gate_act, 3)
                for u in range(PREP):
                    unit_out(act, first_head, u, u % T_RING, u)
                act.wait_ge(u_out, PREP)

            @block.vector
            def _(dve):
                xv = gx[:].rearrange("p (t h) -> p t h", h=FH)
                dve.wait_ge(bias_in, 16)
                nc.vector.tensor_tensor(xv, c["ff_logit"][:], bias[:].unsqueeze(1).broadcast_to([P, TT, FH]),
                                        ALU.add).then_inc(gate_dve, 1)
                nc.vector.tensor_copy(ident_r[:], c["ident"][:]).then_inc(consts_done, 1)
                nc.vector.tensor_tensor(fold[:], c["ident"][:, 0:FD], c["ident"][:, FD:P], ALU.add)
                dve.wait_ge(gate_pool, 1)
                nc.vector.tensor_scalar(gi[:], gi[:], FH - 1, None, ALU.bitwise_and).then_inc(consts_done, 1)
                dve.wait_ge(consts_done, 2)
                nc.vector.tensor_scalar(prefix[:], gi[:], 0.0, None, ALU.is_equal).then_inc(consts_done, 1)
                dve.wait_ge(gate_pool, 3)
                nc.vector.tensor_copy(beyond_r[:], beyond[:])
                dve.wait_ge(k_in, 16)
                cut_k(dve, nc.vector, consts_done, 4)
                dve.wait_ge(gate_act, 3)
                nc.vector.tensor_scalar(gx[:], gx[:], 0.0, None, ALU.min).then_inc(gate_dve, 1)
                dve.wait_ge(gate_dve, 2)
                nc.vector.tensor_tensor(gx[:], gx[:], gy[:], ALU.subtract).then_inc(gate_dve, 1)
                nc.vector.memset(gz[:], 1.0).then_inc(gate_dve, 1)
                dve.wait_ge(gate_pe, 1)
                dve.wait_ge(gate_dve, 4)
                nc.vector.tensor_tensor_scan(gy[:], gz[:], s_ps[0][:, 0:P], 0.0, ALU.mult, ALU.add).then_inc(gate_dve, 1)
                dve.wait_ge(gate_pe, 2)
                dve.wait_ge(gate_dve, 5)
                nc.vector.tensor_copy(gx[:, 0:1], s_ps[1][:, 0:1]).then_inc(gate_dve, 1)
                dve.wait_ge(gate_dve, 6)
                nc.vector.tensor_scalar(gz[:], gy[:], gx[:, 0:1], None, ALU.add).then_inc(gate_dve, 2)
                dve.wait_ge(q_in, 16)
                cut_q(dve, nc.vector, consts_done, 5)
                dve.wait_ge(v_in, 16)
                cut_v(dve, nc.vector, first_head, consts_done, 6)
                dve.wait_ge(gate_dve, 8)

            @block.tensor
            def _(pe):
                pe.wait_ge(gate_dve, 3)
                nc.tensor.transpose(s_ps[0][:, 0:P], gx[:], c["ident"][:]).then_inc(gate_pe, 1)
                pe.wait_ge(consts_done, 3)
                for u in range(T_RING):
                    unit_in(pe, first_head, u, u)
                pe.wait_ge(gate_dve, 5)
                pe.wait_ge(gate_pool, 4)
                nc.tensor.matmul(s_ps[1][:, 0:1], prefix[:], gy[:, P - 1:P], start=True, stop=True).then_inc(gate_pe, 1)
                for u in range(T_RING, PREP):
                    pe.wait_ge(u_out, u + 1 - T_RING)
                    unit_in(pe, first_head, u, u % T_RING)

        block = own_block.enter_context(nc.Block())

        class At:

            def __init__(self, h, order, before):
                first = before is None
                after = order is TAIL
                self.score = S_ITEMS * h.n
                self.block = 0 if first else T_ITEMS * h.n - KB
                self.product = 0 if first else T_ITEMS * h.n - KB - LAG
                self.fold = 0 if first else QG * h.n - 2
                self.prep = PREP * h.n + (0 if after else PREP)
                self.ring = self.block + self.prep + self.fold
                self.slot = (0 if first else -KB - 2) + (0 if after else PREP)
                self.recent = (["prep"] * T_RING if first else ring_kinds(before))[-T_RING:]

        TAIL = head_order(tail=True)
        FIRST, MIDDLE, LAST = head_order(first=True), head_order(), head_order(last=True)
        assert ring_kinds(FIRST)[-T_RING:] == ring_kinds(MIDDLE)[-T_RING:]

        def each_head(eng, run):
            h = first_head
            run(h, FIRST, At(h, FIRST, None))
            with eng.Fori(0, (FH - 2) // 2) as m:
                for h in (Head(2 * m + 1, 1, m), Head(2 * m + 2, 0, m + 1)):
                    run(h, MIDDLE, At(h, MIDDLE, MIDDLE))
            h = Head(FH - 1, 1, FH // 2 - 1)
            run(h, LAST, At(h, LAST, MIDDLE))
            h = Head(FH, 0, FH // 2)
            run(h, TAIL, At(h, TAIL, LAST))

        def last_item(i):
            return sum(len(tile_parts(k)) for k in range(i + 1))

        def queries(g, kb):
            return max(0, kb - 4 * g) * P

        def owner(h, before):
            return h.last() if before else h

        @block.sync
        def _(sp):
            def run(h, order, at):
                if order is FIRST or order is MIDDLE:
                    if order is MIDDLE:
                        wait_alone(sp, v_cut, h.n + 1, passed_sp)
                        load(sp, h.next())
                        wait_alone(sp, scored, at.score, passed_sp)
                    load_gate(sp, h.next())
                if order is not FIRST:
                    b = h.last()
                    wait_alone(sp, fin, QG * h.n, passed_sp)
                    sp.dma_start(mix_out[:, :, bass.ds(b.n * FD + FH * FD, FD)].rearrange("t p e -> p t e"),
                                 stage[:, b.slot]).then_inc(stored[b.slot], 16)

            each_head(sp, run)
            for n in range(2):
                sp.wait_ge(stored[n], 16 * FH // 2)

        @block.gpsimd
        def _(pool):
            def run(h, order, at):
                if order is FIRST or order is MIDDLE:
                    m = h.next()
                    counts = [3 * h.n + 1, 3 * h.n + 2, 3 * h.n + 3]
                    wait_alone(pool, t_ready, at.ring, passed_pool)
                    wait_alone(pool, k_in, 16 * (m.n + 1), passed_pool)
                    cut_k(pool, nc.gpsimd, hi_done, counts[0])
                    wait_alone(pool, q_in, 16 * (m.n + 1), passed_pool)
                    cut_q(pool, nc.gpsimd, hi_done, counts[1])
                    wait_alone(pool, v_in, 16 * (m.n + 1), passed_pool)
                    if order is MIDDLE:
                        wait_alone(pool, pv_done, T_ITEMS * h.n, passed_pool)
                    cut_v(pool, nc.gpsimd, m, hi_done, counts[2])

            each_head(pool, run)

        @block.scalar
        def _(act):
            def run(h, order, at):
                ring = blocks = products = 0
                for item in order:
                    kind, slot = item[0], (at.slot + ring) % T_RING
                    if kind == "step" and order is not FIRST:
                        act.wait_ge(fin, QG * h.n + item[1] - QG + 1)
                    elif kind == "exp":
                        i = item[1]
                        n = len(tile_parts(i)) - 1
                        act.wait_ge(scored, at.score + last_item(i))
                        row = p[:, i // 4 % 2, i % 4, 0:(i + 1) * P]
                        nc.scalar.activation(row, row, ACT.Exp, scale=-1.0, bias=low[:, i, n:n + 1],
                                             accum_out=total[:, i // 4, i % 4:i % 4 + 1]).then_inc(p_ready, 1)
                    elif kind == "prep":
                        unit_out(act, h.next(), item[1], slot, at.ring + ring)
                        ring += 1
                    elif kind == "block":
                        _, _, g, kb = item
                        j0 = queries(g, kb)
                        act.wait_ge(t_ready, at.ring + ring + 1)
                        if not (order is FIRST and blocks < 4):
                            act.wait_ge(pv_done, at.block + blocks - 3)
                        nc.scalar.copy(pt_hi[:, blocks % 4, j0:], t_ps[slot][:, j0:]).then_inc(t_hi, 1)
                        ring, blocks = ring + 1, blocks + 1
                    elif kind == "product":
                        products += 1
                    elif kind == "copy":
                        act.wait_ge(pv_done, at.product + products)
                        act.wait_ge(t_ready, at.ring + ring)
                        nc.scalar.copy(ot[:], o_ps[:]).then_inc(o_copied, 1)
                    elif kind == "fold":
                        ring += 1

            each_head(act, run)

        @block.vector
        def _(dve):
            def run(h, order, at):
                ring = blocks = folds = s = 0
                for item in order:
                    kind, slot = item[0], (at.slot + ring) % T_RING
                    if kind == "step":
                        dve.wait_ge(t_ready, at.ring + ring)
                        if item[1] == 0:
                            dve.wait_ge(cb_in[h.slot], 16 * (h.half + 1))
                    elif kind == "score":
                        _, i, part = item
                        at0, w = sum(tile_parts(i)[:part]), tile_parts(i)[part]
                        start = FAR
                        if part:
                            dve.wait_ge(scored, at.score + s)
                            start = low[:, i, part - 1:part]
                        wait_alone(dve, s_ready, at.score + s + 1, passed_dve)
                        nc.vector.tensor_tensor_reduce(out=p[:, i // 4 % 2, i % 4, at0:at0 + w], in0=s_ps[s % S_RING][:, 0:w],
                                                       in1=cb[:, h.slot, at0:at0 + w], scale=1.0, scalar=start,
                                                       op0=ALU.add, op1=ALU.min,
                                                       accum_out=low[:, i, part:part + 1]).then_inc(scored, 1)
                        s += 1
                    elif kind == "prep":
                        ring += 1
                    elif kind == "block":
                        _, _, g, kb = item
                        j0 = queries(g, kb)
                        dve.wait_ge(t_hi, at.block + blocks + 1)
                        nc.vector.tensor_tensor(pt_lo[:, blocks % 4, j0:], t_ps[slot][:, j0:],
                                                pt_hi[:, blocks % 4, j0:].bitcast(F32), ALU.subtract).then_inc(t_lo, 1)
                        ring, blocks = ring + 1, blocks + 1
                    elif kind == "fold":
                        _, before, g = item
                        o = owner(h, before)
                        dve.wait_ge(p_ready, KB * o.n + 4 * g + 4)
                        nc.vector.reciprocal(recip[:, g, :], total[:, g, :]).then_inc(recip_done, 1)
                        dve.wait_ge(recip_done, at.fold + folds + 1)
                        dve.wait_ge(t_ready, at.ring + ring + 1)
                        if g == 0:
                            dve.wait_ge(stored[o.slot], 16 * o.half)
                        nc.vector.tensor_tensor(stage[:, o.slot, 4 * g:4 * g + 4, :],
                                                t_ps[slot][:, 0:4 * FD].rearrange("p (j e) -> p j e", e=FD),
                                                recip[:, g, :].unsqueeze(2).broadcast_to([P, 4, FD]), ALU.mult).then_inc(fin, 1)
                        ring, folds = ring + 1, folds + 1

            each_head(dve, run)

        @block.tensor
        def _(pe):
            bank_read = {"block": t_lo, "prep": u_out, "fold": fin}

            def run(h, order, at):
                s = products = folds = blocks = 0
                units = list(at.recent)
                for item in order:
                    kind, slot = item[0], (at.slot + len(units)) % T_RING
                    if kind in bank_read:
                        old = units[-T_RING]
                        count = units[T_RING:].count(old) - units[-T_RING:].count(old) + 1
                        pe.wait_ge(bank_read[old], {"block": at.block, "prep": at.prep, "fold": at.fold}[old] + count)
                        units.append(kind)
                    if kind == "score":
                        _, i, part = item
                        at0, w = sum(tile_parts(i)[:part]), tile_parts(i)[part]
                        if not (order is FIRST and s < S_RING):
                            pe.wait_ge(scored, at.score + s + 1 - S_RING)
                        if s == 0:
                            pe.wait_ge(u_out, at.prep)
                        tile = slice(i * P, (i + 1) * P)
                        out, keys = s_ps[s % S_RING], kst[:, h.slot, at0:at0 + w]
                        nc.tensor.matmul(out[:, 0:w], q1[:, h.slot, tile], keys, start=True, stop=False)
                        if part == len(tile_parts(i)) - 1:
                            nc.tensor.matmul(out[:, w - P:w], ident_r[:], beyond_r[:], start=False, stop=False)
                        nc.tensor.matmul(out[:, 0:w], q2[:, h.slot, tile], keys, start=False, stop=True).then_inc(s_ready, 1)
                        s += 1
                    elif kind == "prep":
                        unit_in(pe, h.next(), item[1], slot)
                    elif kind == "block":
                        _, before, g, kb = item
                        if kb == 0:
                            pe.wait_ge(p_ready, KB * owner(h, before).n + 4 * g + 4)
                        for j in range(max(0, kb - 4 * g), 4):
                            m = nc.tensor.transpose(t_ps[slot][:, j * P:(j + 1) * P], p[:, g % 2, j, kb * P:(kb + 1) * P], c["ident"][:])
                        m.then_inc(t_ready, 1)
                        blocks += 1
                    elif kind == "product":
                        _, before, g, kb = item
                        o, j0 = owner(h, before), queries(g, kb)
                        place = (products - (0 if order is FIRST else LAG)) % 4
                        if kb == 0:
                            pe.wait_ge(v_cut, o.n + 1)
                            if not (order is FIRST and g == 0):
                                pe.wait_ge(o_copied, QG * o.n + g)
                        pe.wait_ge(t_lo, at.product + products + 1)
                        for part in (pt_hi, pt_lo):
                            m = nc.tensor.matmul(o_ps[:, j0:], vcat[:, o.slot, kb, :], part[:, place, j0:],
                                                 start=kb == 0 and part is pt_hi, stop=kb == 4 * g + 3 and part is pt_lo)
                        m.then_inc(pv_done, 1)
                        products += 1
                    elif kind == "fold":
                        _, before, g = item
                        pe.wait_ge(o_copied, QG * owner(h, before).n + g + 1)
                        for j in range(4):
                            m = nc.tensor.matmul(t_ps[slot][:, j * FD:(j + 1) * FD], ot[:, j * P:(j + 1) * P], fold[:],
                                                 start=True, stop=True)
                        m.then_inc(t_ready, 1)

            each_head(pe, run)


HT = TT // 2
FC = DFF // BANK
FT = BANK // P
CW = DM // BANK


def mix_and_mlp(nc, ctx, c, inp, mix_in, out):
    NRAW = 4
    PIECES = FC * 16
    OUTS = CW * DT
    ADDS = CW * HT * (1 + FC)
    UPS, DOWNS = 8 * FC, CW * HT * FC

    def sem(name):
        return ctx.enter_context(nc.semaphore("m_" + name))

    names = ("w2_in", "out_stored", "w_hi_done", "w_lo_done", "mix_t", "mt_hi_done", "mt_lo_done", "o_ready", "added",
             "squared", "rstd_step", "scaled", "h_t", "ht_hi_done", "ht_lo_done", "up_ready", "relu_done", "sq_done",
             "u_hi_done", "u_lo_done", "down_ready", "w2_scaled", "out_hi_done", "out_lo_done")
    (w2_in, out_stored, w_hi_done, w_lo_done, mix_t, mt_hi_done, mt_lo_done, o_ready, added, squared, rstd_step, scaled,
     h_t, ht_hi_done, ht_lo_done, up_ready, relu_done, sq_done, u_hi_done, u_lo_done, down_ready, w2_scaled, out_hi_done,
     out_lo_done) = (sem(n) for n in names)
    out_in = [sem(f"out_in{k}") for k in range(4)]
    mix_in_done = [sem(f"mix_in{k}") for k in range(2)]
    raw_in = [sem(f"raw_in{k}") for k in range(NRAW)]
    x_in = [sem(f"x_in{k}") for k in range(HT)]
    with ExitStack() as own:
        def sb(name, shape, dt=F32):
            return own.enter_context(nc.sbuf_tensor("m_" + name, shape, dt))

        ht_hi = sb("ht_hi", [P, DT, HT * P], F32R)
        out_raw, = place_under(nc, ["m_out_raw"], [[P, DT, DM]])
        ht_lo = sb("ht_lo", [P, DT, HT * P], F32R)
        w_hi, w_lo = sb("w_hi", [P, 16, BANK], F32R), sb("w_lo", [P, 16, BANK], F32R)
        acc = sb("acc", [P, HT, DM])
        raw = sb("raw", [P, NRAW, BANK])
        u_hi, u_lo = sb("u_hi", [P, FT, HT * P], F32R), sb("u_lo", [P, FT, HT * P], F32R)
        relu = sb("relu", [P, 2, BANK])
        w2 = sb("w2", [P, DM])
        mixr = sb("mixr", [P, 2, DM])
        ss, rstd = sb("ss", [P, 2, 2]), sb("rstd", [P, 2])
        mt_hi = u_hi[:, 0:2, :].rearrange("p s (d t) -> p s d t", t=P)
        mt_lo = u_lo[:, 0:2, :].rearrange("p s (d t) -> p s d t", t=P)
        h2 = sb("h2", [P, DM])
        up_ps = own.enter_context(nc.psum_tensor("m_up", [P, 4, BANK], F32))
        down_ps = own.enter_context(nc.psum_tensor("m_down", [P, 4, BANK], F32))
        mtp = down_ps[:, 0:2, :].rearrange("p b (d t) -> p (b d) t", t=P)
        htp = down_ps[:, 2:4, :].rearrange("p b (d t) -> p (b d) t", t=P)
        w_out = inp["w_out"].rearrange("l (d p) n -> p (l d) n", p=P)
        w_up = inp["w_up"].rearrange("l (d p) n -> p (l d) n", p=P)
        w_down = inp["w_down"].rearrange("l (f p) n -> p (l f) n", p=P)
        x_tiles = inp["x"].rearrange("b (t p) d -> (b t) p d", p=P)
        out_tiles = out.rearrange("b (t p) d -> (b t) p d", p=P)
        block = own.enter_context(nc.Block())

        def each_chunk(eng, body):
            body(0, False)
            with eng.Fori(1, FC - 1) as f:
                body(f, False)
            body(FC - 1, True)

        def out_piece(m):
            return divmod(m, DT)

        def raw_out(m):
            k, d = out_piece(m)
            return out_raw[:, d, k * BANK:(k + 1) * BANK]

        @block.sync
        def _(sp):
            def load_piece(m, src, r):
                if not (isinstance(m, int) and m < NRAW):
                    sp.wait_ge(w_lo_done, m - NRAW + 1)
                sp.dma_start(raw[:, r, :], src).then_inc(raw_in[r], 16)

            def load_w_out(n):
                k, d = n // 2, n % 2 * 4
                sp.dma_start(out_raw[:, d:d + 4, k * BANK:(k + 1) * BANK],
                             w_out[:, d:d + 4, k * BANK:(k + 1) * BANK]).then_inc(out_in[n], 16)

            def load_mix(half, t):
                n = HT * half + t
                if n >= 2:
                    sp.wait_ge(mix_t, n - 1)
                sp.dma_start(mixr[:, t % 2, :], mix_in[n]).then_inc(mix_in_done[t % 2], 16)

            load_mix(0, 0)
            load_w_out(0)
            load_w_out(1)
            load_mix(0, 1)
            sp.dma_start(w2[:], bcast(inp["norm2_w"], DM)).then_inc(w2_in, 16)
            load_w_out(2)
            load_w_out(3)
            for half in range(2):
                base = PIECES * half
                load_mix(half, 2)
                for t in range(HT):
                    if half:
                        sp.wait_ge(out_stored, 16 * HT)
                    sp.dma_start(acc[:, t, :], x_tiles[HT * half + t]).then_inc(x_in[t], 16)
                    if t + 3 < HT:
                        load_mix(half, t + 3)
                for d in range(DT):
                    load_piece(base + d, w_up[:, d, 0:BANK], d % NRAW)

                def chunk(f, last):
                    for k in range(8):
                        src = w_down[:, bass.ds(f * FT + k // 2, 1), k % 2 * BANK:(k % 2 + 1) * BANK]
                        load_piece(base + 8 + 16 * f + k, src.rearrange("p one n -> p (one n)"), k % NRAW)
                    if not last:
                        for d in range(DT):
                            load_piece(base + 16 + 16 * f + d, w_up[:, d, bass.ds(f * BANK + BANK, BANK)], d % NRAW)
                        return
                    if half == 0:
                        sp.wait_ge(up_ready, UPS)
                        for n in range(4):
                            load_w_out(n)
                        load_mix(1, 0)
                        load_mix(1, 1)
                    for t in range(HT):
                        sp.wait_ge(added, ADDS * half + 16 + 16 * f + 2 * t + 2)
                        sp.dma_start(out_tiles[half * HT + t], acc[:, t, :]).then_inc(out_stored, 16)

                each_chunk(sp, chunk)
            sp.wait_ge(out_stored, 16 * TT)

        @block.gpsimd
        def _(pool):
            def cut_lo(m, s, r):
                pool.wait_ge(w_hi_done, m + 1)
                nc.gpsimd.tensor_tensor(w_lo[:, s, :], raw[:, r, :], w_hi[:, s, :].bitcast(F32), ALU.subtract).then_inc(w_lo_done, 1)

            def tile_rstd(n):
                s = slice(n % 2, n % 2 + 1)
                pool.wait_ge(squared, 2 * n + 2)
                nc.gpsimd.tensor_tensor(rstd[:, s], ss[:, n % 2, 0:1], ss[:, n % 2, 1:2], ALU.add).then_inc(rstd_step, 1)
                pool.wait_ge(rstd_step, 3 * n + 1)
                nc.gpsimd.tensor_tensor(rstd[:, s], rstd[:, s], c["eps_dm"][:], ALU.add).then_inc(rstd_step, 1)
                pool.wait_ge(rstd_step, 3 * n + 2)
                nc.gpsimd.tensor_tensor(rstd[:, s], rstd[:, s], c["neg_half"][:, 0:1], ALU.pow).then_inc(rstd_step, 1)

            for half in range(2):
                base = PIECES * half
                for t in range(HT):
                    tile_rstd(HT * half + t)
                pool.wait_ge(w_lo_done, base + DT)

                def chunk(f, last):
                    for k in range(8):
                        pool.wait_ge(relu_done, UPS * half + 8 * f + k + 1)
                        nc.gpsimd.tensor_tensor(relu[:, k % 2, :], relu[:, k % 2, :], relu[:, k % 2, :], ALU.mult).then_inc(sq_done, 1)
                        cut_lo(base + 8 + 16 * f + k, 8 + k, k % NRAW)
                    for d in range(0 if last else DT):
                        cut_lo(base + 16 + 16 * f + d, d, d % NRAW)

                each_chunk(pool, chunk)

        @block.scalar
        def _(act):
            def cut_hi(s, r, uses):
                act.wait_ge(raw_in[r], 16 * uses)
                nc.scalar.copy(w_hi[:, s, :], raw[:, r, :]).then_inc(w_hi_done, 1)

            def cut_out_hi(half, m):
                act.wait_ge(out_in[m // 4], 16 * (half + 1))
                nc.scalar.copy(w_hi[:, m, :], raw_out(m)).then_inc(out_hi_done, 1)

            def square_tile(half, t):
                n = HT * half + t
                act.wait_ge(added, ADDS * half + 2 * t + 2)
                if n >= 2:
                    act.wait_ge(rstd_step, 3 * (n - 2) + 1)
                for k in range(2):
                    act.wait_ge(squared, 2 * n + k)
                    nc.scalar.activation(relu[:, 0, :], acc[:, t, k * BANK:(k + 1) * BANK], ACT.Square,
                                         accum_out=ss[:, t % 2, k:k + 1]).then_inc(squared, 1)

            def mix_hi(half, t):
                n = HT * half + t
                act.wait_ge(mix_t, n + 1)
                if t >= 2:
                    act.wait_ge(o_ready, 2 * (n - 2) + 2)
                nc.scalar.copy(mt_hi[:, t % 2], mtp).then_inc(mt_hi_done, 1)

            def norm_hi(half, t):
                act.wait_ge(h_t, HT * half + t + 1)
                nc.scalar.copy(ht_hi[:, :, t * P:(t + 1) * P], htp).then_inc(ht_hi_done, 1)

            for half in range(2):
                uses = PIECES // NRAW * half
                mix_hi(half, 0)
                if half:
                    act.wait_ge(down_ready, DOWNS)
                for m in range(8 * half, OUTS):
                    if m == OUTS - 4:
                        mix_hi(half, 1)
                    cut_out_hi(half, m)
                for t in range(HT):
                    if 1 <= t < HT - 1:
                        mix_hi(half, t + 1)
                    if t == HT - 1:
                        act.wait_ge(o_ready, 2 * HT * (half + 1) - 1)
                        for d in range(DT // 2):
                            cut_hi(d, d % NRAW, uses + 1)
                    if t >= 1:
                        norm_hi(half, t - 1)
                    if t == HT - 1:
                        for d in range(DT // 2, DT):
                            cut_hi(d, d % NRAW, uses + 2)
                    square_tile(half, t)
                norm_hi(half, HT - 1)
                act.wait_ge(o_ready, 2 * HT * (half + 1))

                def chunk(f, last):
                    for k in range(8):
                        n = UPS * half + 8 * f + k
                        act.wait_ge(up_ready, n + 1)
                        if not (isinstance(n, int) and n < 2):
                            act.wait_ge(u_lo_done, n - 1 if k >= 1 else n)
                        if isinstance(f, int) and f == 0 and k == 0:
                            act.wait_ge(squared, 2 * HT * (half + 1))
                        nc.scalar.activation(relu[:, k % 2, :], up_ps[:, k % 4, :], ACT.Relu).then_inc(relu_done, 1)
                        if k == 0:
                            act.wait_ge(down_ready, DOWNS * half + 16 * f)
                        cut_hi(8 + k, k % NRAW, uses + 2 + 4 * f + k // NRAW + 1)
                        act.wait_ge(sq_done, n + 1)
                        nc.scalar.copy(u_hi[:, k % 4, k // 4 * BANK:(k // 4 + 1) * BANK], relu[:, k % 2, :]).then_inc(u_hi_done, 1)
                    if not (last and half):
                        act.wait_ge(up_ready, UPS * half + 8 * f + 8)
                        for d in range(DT):
                            if last:
                                cut_out_hi(1, d)
                            else:
                                cut_hi(d, d % NRAW, uses + 4 + 4 * f + d // NRAW + 1)

                each_chunk(act, chunk)

        @block.vector
        def _(dve):
            def mix_lo(half, t):
                dve.wait_ge(mt_hi_done, HT * half + t + 1)
                nc.vector.tensor_tensor(mt_lo[:, t % 2], mtp, mt_hi[:, t % 2].bitcast(F32), ALU.subtract).then_inc(mt_lo_done, 1)

            def cut_out_lo(half, m):
                dve.wait_ge(out_hi_done, OUTS * half + m + 1)
                nc.vector.tensor_tensor(w_lo[:, m, :], raw_out(m), w_hi[:, m, :].bitcast(F32), ALU.subtract).then_inc(out_lo_done, 1)

            def cut_up_lo(half, d):
                dve.wait_ge(w_hi_done, PIECES * half + d + 1)
                nc.vector.tensor_tensor(w_lo[:, d, :], raw[:, d % NRAW, :], w_hi[:, d, :].bitcast(F32), ALU.subtract).then_inc(w_lo_done, 1)

            def norm_lo(half, t):
                dve.wait_ge(ht_hi_done, HT * half + t + 1)
                tok = slice(t * P, (t + 1) * P)
                nc.vector.tensor_tensor(ht_lo[:, :, tok], htp, ht_hi[:, :, tok].bitcast(F32), ALU.subtract).then_inc(ht_lo_done, 1)

            def add(t, k, bank):
                cols = acc[:, t, k * BANK:(k + 1) * BANK]
                nc.vector.tensor_tensor(cols, cols, bank, ALU.add).then_inc(added, 1)

            def scale_tile(half, t):
                n = HT * half + t
                dve.wait_ge(rstd_step, 3 * n + 3)
                dve.wait_ge(h_t, n)
                nc.vector.scalar_tensor_tensor(h2[:], acc[:, t, :], rstd[:, t % 2:t % 2 + 1], w2[:],
                                               ALU.mult, ALU.mult).then_inc(scaled, 1)

            for half in range(2):
                mix_lo(half, 0)
                for m in range(8 * half, OUTS):
                    if m == OUTS - 4:
                        mix_lo(half, 1)
                    cut_out_lo(half, m)
                if half == 0:
                    dve.wait_ge(w2_in, 16)
                    nc.vector.tensor_scalar(w2[:], w2[:], float(DM) ** 0.5, None, ALU.mult).then_inc(w2_scaled, 1)
                    dve.wait_ge(w2_scaled, 1)
                dve.wait_ge(out_lo_done, OUTS * (half + 1))
                for t in range(HT):
                    if 1 <= t < HT - 1:
                        mix_lo(half, t + 1)
                    if t == HT - 1:
                        if half:
                            dve.wait_ge(w_lo_done, PIECES)
                        for d in range(DT // 2):
                            cut_up_lo(half, d)
                    if t >= 1:
                        norm_lo(half, t - 1)
                    dve.wait_ge(x_in[t], 16 * (half + 1))
                    for k in range(2):
                        dve.wait_ge(o_ready, 2 * (HT * half + t) + k + 1)
                        add(t, k, up_ps[:, (2 * t + k) % 4, :])
                    if t == HT - 1:
                        for d in range(DT // 2, DT):
                            cut_up_lo(half, d)
                    scale_tile(half, t)
                norm_lo(half, HT - 1)

                def chunk(f, last):
                    for k in range(8):
                        dve.wait_ge(u_hi_done, UPS * half + 8 * f + k + 1)
                        tok = slice(k // 4 * BANK, (k // 4 + 1) * BANK)
                        nc.vector.tensor_tensor(u_lo[:, k % 4, tok], relu[:, k % 2, :], u_hi[:, k % 4, tok].bitcast(F32),
                                                ALU.subtract).then_inc(u_lo_done, 1)
                    for t in range(HT):
                        for k in range(CW):
                            n = 16 * f + 2 * t + k
                            dve.wait_ge(added, ADDS * half + n + 1)
                            dve.wait_ge(down_ready, DOWNS * half + n + 1)
                            add(t, k, down_ps[:, (2 * t + k) % 4, :])
                        if last and half == 0:
                            cut_out_lo(1, t)

                each_chunk(dve, chunk)

        @block.tensor
        def _(pe):
            def turn(src, dst):
                for d in range(DT):
                    m = nc.tensor.transpose(dst[:, d, :], src[:, d * P:(d + 1) * P], c["ident"][:])
                return m

            def turn_mix(half, t):
                n = HT * half + t
                pe.wait_ge(mix_in_done[t % 2], 16 * (n // 2 + 1))
                pe.wait_ge(mt_lo_done, n)
                turn(mixr[:, t % 2, :], mtp).then_inc(mix_t, 1)

            def turn_norm(half, t):
                n = HT * half + t
                pe.wait_ge(scaled, n + 1)
                pe.wait_ge(ht_lo_done, n)
                turn(h2[:], htp).then_inc(h_t, 1)

            for half in range(2):
                if half:
                    pe.wait_ge(added, ADDS - 2)
                turn_mix(half, 0)
                for t in range(HT):
                    if t + 1 < HT:
                        turn_mix(half, t + 1)
                    pe.wait_ge(mt_lo_done, HT * half + t + 1)
                    for k in range(2):
                        if t >= 2:
                            pe.wait_ge(added, ADDS * half + 2 * t + k - 3)
                        for d in range(DT):
                            s = DT * k + d
                            if t == 0:
                                pe.wait_ge(out_lo_done, OUTS * half + s + 1)
                            m = three_pass(nc, up_ps[:, (2 * t + k) % 4, :], mt_hi[:, t % 2, d, :], mt_lo[:, t % 2, d, :],
                                           w_hi[:, s, :], w_lo[:, s, :], d == 0, d == DT - 1)
                        m.then_inc(o_ready, 1)
                    if t >= 1:
                        turn_norm(half, t - 1)

                def chunk(f, last):
                    first = isinstance(f, int) and f == 0
                    for k in range(8):
                        n = UPS * half + 8 * f + k
                        if first and k < 4:
                            pe.wait_ge(added, ADDS * half + 2 * HT - 3 + k)
                            pe.wait_ge(ht_lo_done, HT * half + 4)
                        else:
                            pe.wait_ge(relu_done, n - 3 if k >= 3 else n - k)
                        if first and k == 2:
                            turn_norm(half, HT - 1)
                        elif first and k == 4:
                            pe.wait_ge(ht_lo_done, HT * (half + 1))
                        tok, hid = slice(k // 4 * BANK, (k // 4 + 1) * BANK), slice(k % 4 * P, k % 4 * P + P)
                        for d in range(DT):
                            if k == 0:
                                pe.wait_ge(w_lo_done, PIECES * half + 16 * f + d + 1)
                            m = three_pass(nc, up_ps[:, k % 4, :], w_hi[:, d, hid], w_lo[:, d, hid], ht_hi[:, d, tok],
                                           ht_lo[:, d, tok], d == 0, d == DT - 1)
                        m.then_inc(up_ready, 1)
                    for t in range(HT):
                        tok = slice(t * P, (t + 1) * P)
                        for k in range(CW):
                            n = 16 * f + 2 * t + k
                            if t % 4 == 0 and k == 0:
                                pe.wait_ge(u_lo_done, UPS * half + 8 * f + t + 4)
                            pe.wait_ge(added, ADDS * half + 16 + n - 3)
                            for i in range(FT):
                                s = 8 + 2 * i + k
                                if t == 0:
                                    pe.wait_ge(w_lo_done, PIECES * half + 16 * f + s + 1)
                                m = three_pass(nc, down_ps[:, (2 * t + k) % 4, :], u_hi[:, i, tok], u_lo[:, i, tok],
                                               w_hi[:, s, :], w_lo[:, s, :], i == 0, i == FT - 1)
                            m.then_inc(down_ready, 1)

                each_chunk(pe, chunk)


def build(nc, inp, out):
    with ExitStack() as ctx:
        c = constants(nc, ctx, inp)
        tok = nc.dram_tensor("tok_major", (NT, TT, P, BANK), F32, kind="Internal").ap()
        chan = nc.dram_tensor("chan_major", (2, HH, P, S), F32, kind="Internal").ap()
        cum = nc.dram_tensor("cum_gates", (FH, S), F32, kind="Internal").ap()
        mix = nc.dram_tensor("mixed", (TT, P, DM), F32, kind="Internal").ap()
        project(nc, ctx, c, inp, tok, chan)
        recurrence(nc, ctx, c, tok, chan, mix)
        attention(nc, ctx, c, inp, tok, cum, mix)
        mix_and_mlp(nc, ctx, c, inp, mix, out)


_INS = ["x", "lower_bounds", "norm1_w", "w_in", "fox_f_bias", "q_norm_w", "k_norm_w", "hgrn_norm_w", "w_out",
        "norm2_w", "w_up", "w_down"]


def kernel(**inputs):
    import numpy as _np
    import concourse.bacc as _bacc
    from concourse.bass_utils import run_bass_kernel_spmd as _run

    nc = _bacc.Bacc("TRN2", target_bir_lowering=False, num_devices=1, dynamic_dma_scratch_size=1024)
    arrays, args = {}, {}
    for name in _INS:
        a = _np.ascontiguousarray(inputs[name])
        arrays[f"in_{name}"] = a
        args[name] = nc.dram_tensor(f"in_{name}", a.shape, mybir.dt.from_np(a.dtype), kind="ExternalInput").ap()
    out = nc.dram_tensor("out_0", (1, S, DM), F32, kind="ExternalOutput").ap()
    build(nc, args, out)
    r = _run(nc, [arrays], core_ids=[0])
    return r.results[0]["out_0"]
```

```python
from contextlib import ExitStack

import concourse.bass as bass
from concourse import mybir

F32 = mybir.dt.float32
F32R = mybir.dt.float32r
ALU = mybir.AluOpType
ACT = mybir.ActivationFunctionType
AX = mybir.AxisListType

P = 128
BANK = 512
S = 2048
DM = 1024
DT = DM // P
TT = S // P
HH = 4
FH = 8
FD = 64
DFF = 4 * DM
EPS = 1e-6
NT = 5
V_, FQ_, FK_, FV_, G_ = range(NT)
START = 1


class Ring:

    def __init__(self, slots):
        self.slots = slots

    def slot(self, n):
        return n % self.slots

    def landed(self, n):
        return 16 * (n // self.slots + 1)


def wait_alone(eng, sem, value, passed):
    eng.wait_ge(sem, value)
    eng.sem_inc(passed, 1)


def place_under(nc, names, shapes):
    with ExitStack() as early:
        return [early.enter_context(nc.sbuf_tensor(name, shape, F32)) for name, shape in zip(names, shapes)]


def three_pass(nc, out, l_hi, l_lo, r_hi, r_lo, first, last):
    nc.tensor.matmul(out, l_hi, r_hi, start=first, stop=False)
    nc.tensor.matmul(out, l_hi, r_lo, start=False, stop=False)
    return nc.tensor.matmul(out, l_lo, r_hi, start=False, stop=last)


def constants(nc, ctx):
    def sb(name, shape, dt=F32):
        return ctx.enter_context(nc.sbuf_tensor(name, shape, dt))

    c = {
        "ident": sb("ident", [P, P]),
        "neg_half": sb("neg_half", [P, FH]),
        "eps_dm": sb("eps_dm", [P, 1]),
        "eps_fd": sb("eps_fd", [P, FH]),
        "eps_p": sb("eps_p", [P, 1]),
        "lb": sb("lb", [P, HH]),
        "one_minus_lb": sb("one_minus_lb", [P, HH]),
        "hgrn_w": sb("hgrn_w", [P, P]),
        "qk_w": sb("qk_w", [P, 2, FD]),
        "lb_work": sb("lb_work", [P, 3, HH]),
    }
    for name in ("small_in", "pool_made", "act_made", "dve_made"):
        c[name] = ctx.enter_context(nc.semaphore("const_" + name))
    return c


def load_small(nc, sp, c, inp):
    with nc.allow_non_contiguous_dma(reason="512 values"):
        sp.dma_start(c["lb"][:], inp["lower_bounds"].rearrange("l (h p) -> p (l h)", p=P)).then_inc(c["small_in"], 16)
    sp.dma_start(c["hgrn_w"][:], bcast(inp["hgrn_norm_w"], P)).then_inc(c["small_in"], 16)
    sp.dma_start(c["qk_w"][:, 0, :], bcast(inp["q_norm_w"], FD)).then_inc(c["small_in"], 16)
    sp.dma_start(c["qk_w"][:, 1, :], bcast(inp["k_norm_w"], FD)).then_inc(c["small_in"], 16)


def pool_constants(nc, pool, c):
    nc.gpsimd.memset(c["ident"][:], 0.0).then_inc(c["pool_made"], 1)
    pool.wait_ge(c["pool_made"], 1)
    nc.gpsimd.affine_select(out=c["ident"][:], in_=c["ident"][:], compare_op=ALU.not_equal, fill=1.0,
                            base=0, pattern=[[-1, P]], channel_multiplier=1).then_inc(c["pool_made"], 1)
    nc.gpsimd.memset(c["neg_half"][:], -0.5).then_inc(c["pool_made"], 1)
    nc.gpsimd.memset(c["eps_dm"][:], DM * EPS).then_inc(c["pool_made"], 1)
    nc.gpsimd.memset(c["eps_fd"][:], FD * EPS).then_inc(c["pool_made"], 1)
    nc.gpsimd.memset(c["eps_p"][:], P * EPS).then_inc(c["pool_made"], 1)
    pool.wait_ge(c["pool_made"], 6)


def act_constants(nc, act, c):
    act.wait_ge(c["dve_made"], 1)
    nc.scalar.activation(c["lb_work"][:, 1, :], c["lb_work"][:, 0, :], ACT.Exp).then_inc(c["act_made"], 1)


def dve_weights(nc, dve, c):
    made, work = c["dve_made"], c["lb_work"]
    dve.wait_ge(c["small_in"], 64)
    nc.vector.tensor_tensor(work[:, 0, :], c["lb"][:], c["lb"][:], ALU.subtract).then_inc(made, 1)
    nc.vector.tensor_scalar(c["qk_w"][:, 0, :], c["qk_w"][:, 0, :], -1.0, None, ALU.mult).then_inc(made, 1)
    nc.vector.tensor_scalar(c["qk_w"][:, 1, :], c["qk_w"][:, 1, :], float(FD) ** 0.5, None, ALU.mult).then_inc(made, 1)
    nc.vector.tensor_scalar(c["hgrn_w"][:], c["hgrn_w"][:], float(P) ** 0.5, None, ALU.mult).then_inc(made, 1)


def dve_lower_bounds(nc, dve, c):
    made, work = c["dve_made"], c["lb_work"]
    dve.wait_ge(c["act_made"], 1)
    nc.vector.reciprocal(work[:, 2, :], work[:, 1, :]).then_inc(made, 1)
    dve.wait_ge(made, 5)
    nc.vector.tensor_tensor(work[:, 0, :], work[:, 1, :], work[:, 2, :], ALU.mult).then_inc(made, 1)
    dve.wait_ge(made, 6)
    nc.vector.tensor_tensor(c["lb"][:], work[:, 0, :], work[:, 0, :], ALU.subtract).then_inc(made, 1)
    dve.wait_ge(made, 7)
    nc.vector.tensor_scalar(c["one_minus_lb"][:], c["lb"][:], -1.0, 1.0, ALU.mult, ALU.add).then_inc(made, 1)
    dve.wait_ge(made, 8)


def bcast(row, n):
    return bass.AP(tensor=row.tensor, offset=row.offset, ap=[[0, P], [1, n]])


def project(nc, ctx, c, inp, tok_out, ch_out, cum_out):
    NW = 16
    NRAW = 2
    CH = 7
    COLS = [1024, 2048, 2560, 3072, 1536, 0, 512]
    FF = 3584
    raw_ring, x_ring = Ring(NRAW), Ring(2)

    def sem(name):
        return ctx.enter_context(nc.semaphore("p_" + name))

    x_in = [sem(f"x_in{k}") for k in range(2)]
    raw_in = [sem(f"raw_in{k}") for k in range(NRAW)]
    stored = [sem(f"stored{k}") for k in range(4)]
    first_in = [sem(f"first_in{k}") for k in range(DT // 2)]
    w1_in, ff_in, squared, rstd_step, scaled, tp_ready = (
        sem(n) for n in ("w1_in", "ff_in", "squared", "rstd_step", "scaled", "tp_ready"))
    ht_hi_done, ht_lo_done, w_hi_done, w_lo_done, w_used = (sem(n) for n in ("ht_hi", "ht_lo", "w_hi", "w_lo", "w_used"))
    bias_in, ff_ready, gate_act, gate_dve, cum_stored = (sem(n) for n in ("bias_in", "ff_ready", "gate_act", "gate_dve", "cum_stored"))
    ffw_hi_done, ffw_lo_done, w1_scaled = sem("ffw_hi"), sem("ffw_lo"), sem("w1_scaled")
    acc_ready, banks_free, act_out, summed, qk_rstd, dve_step = (
        sem(n) for n in ("acc_ready", "banks_free", "act_out", "summed", "qk_rstd", "dve_step"))
    with ExitStack() as own:
        def sb(name, shape, dt=F32):
            return own.enter_context(nc.sbuf_tensor("p_" + name, shape, dt))

        ht_hi, ht_lo = sb("ht_hi", [P, DT, S], F32R), sb("ht_lo", [P, DT, S], F32R)
        w_hi = sb("w_hi", [P, NW, BANK], F32R)
        _, first_raw = place_under(nc, ["p_w_lo_low", "p_first_raw"], [[P, DT, BANK]] * 2)
        w_lo = sb("w_lo", [P, NW, BANK], F32R)
        raw = sb("raw", [P, NRAW, BANK])
        stage = sb("stage", [P, 4, BANK])
        xt = sb("xt", [P, 2, DM])
        w1 = sb("w1", [P, DM])
        work = sb("work", [P, BANK])
        ff_raw, ff_hi, ff_lo = sb("ff_raw", [P, DT, FH]), sb("ff_hi", [P, DT, FH], F32R), sb("ff_lo", [P, DT, FH], F32R)
        f_bias, one = sb("f_bias", [FH, 1]), sb("one", [FH, 1])
        gate = xt[0:FH].rearrange("h a b -> h (a b)")
        ss, rstd = sb("ss", [P, 2, 2]), sb("rstd", [P, 2])
        qss, qrs = sb("qss", [P, 2, FH]), sb("qrs", [P, 2, FH])
        acc = own.enter_context(nc.psum_tensor("p_acc", [P, 4, BANK], F32))
        tp = own.enter_context(nc.psum_tensor("p_tp", [P, 4, BANK], F32))
        tpv = tp[:].rearrange("p (u b) (d t) -> p u (b d) t", u=2, t=P)
        gate_ps = tp[0:FH].rearrange("h a b -> h (a b)")
        x_tiles = inp["x"].rearrange("b (t p) d -> (b t) p d", p=P)
        w_in = inp["w_in"].rearrange("l (d p) n -> p (l d) n", p=P)
        block = own.enter_context(nc.Block())

        def raw_piece(m):
            return first_raw[:, m, :] if m < DT else raw[:, m % NRAW, :]

        def each_group(eng, body):
            with eng.Fori(0, 2) as i:
                for j in range(4):
                    body(i, j, False)
            for i in (2, 3):
                for j in range(4):
                    body(i, j, i == 3)

        def piece_beside(ch, i, j):
            return [8 * (ch + 1) + 4 * (i - 2) + j] if isinstance(i, int) and ch + 1 < CH else []

        @block.sync
        def _(sp):
            def load_x(t, slot):
                sp.dma_start(xt[:, slot, :], x_tiles[t]).then_inc(x_in[slot], 16)

            def load_piece(m):
                ch, d = divmod(m, DT)
                if m >= DT + NRAW:
                    sp.wait_ge(w_lo_done, m - NRAW + 1)
                sp.dma_start(raw[:, m % NRAW, :], w_in[:, d, COLS[ch]:COLS[ch] + BANK]).then_inc(raw_in[m % NRAW], 16)

            load_x(0, 0)
            for j in range(4):
                sp.sem_inc(stored[j], 16 * START)
            sp.dma_start(w1[:], bcast(inp["norm1_w"], DM)).then_inc(w1_in, 16)
            for k in range(DT // 2):
                sp.dma_start(first_raw[:, 2 * k:2 * k + 2, :],
                             w_in[:, 2 * k:2 * k + 2, COLS[0]:COLS[0] + BANK]).then_inc(first_in[k], 16)
                if k == 0:
                    load_x(1, 1)
            sp.dma_start(ff_raw[:], w_in[:, :, FF:FF + FH]).then_inc(ff_in, 16)
            load_small(nc, sp, c, inp)
            with nc.allow_non_contiguous_dma(reason="8 values"):
                sp.dma_start(f_bias[:], inp["fox_f_bias"].rearrange("l h -> h l")).then_inc(bias_in, 16)
            sp.wait_ge(tp_ready, 1)
            load_x(2, 0)
            for ch in range(CH):
                def body(i, j, last):
                    if ch == 0 and not (last and j >= 1):
                        sp.wait_ge(tp_ready, 4 * i + j + 2)
                        load_x(4 * i + j + 3, (j + 1) % 2)
                    for m in piece_beside(ch, i, j):
                        if m % DT < DT - NRAW:
                            load_piece(m + NRAW)
                    sp.wait_ge(banks_free, 4 + 16 * ch + 4 * i + j + 1)
                    if ch < NT:
                        dst = tok_out[ch, 4 * i + j]
                    else:
                        dst = ch_out[ch - NT, i, :, j * BANK:(j + 1) * BANK]
                    sp.dma_start(dst, stage[:, j, :]).then_inc(stored[j], 16)
                if ch + 1 < CH:
                    for m in range(NRAW):
                        load_piece(8 * (ch + 1) + m)
                each_group(sp, body)
                if ch == NT:
                    sp.wait_ge(gate_dve, 5)
                    sp.dma_start(cum_out, gate).then_inc(cum_stored, 16)
            for j in range(4):
                sp.wait_ge(stored[j], 16 * (START + 4 * CH))
            sp.wait_ge(cum_stored, 16)

        @block.gpsimd
        def _(pool):
            def tile_rstd(t, slot):
                pool.wait_ge(squared, 2 * t + 2)
                nc.gpsimd.tensor_tensor(rstd[:, slot:slot + 1], ss[:, slot, 0:1], ss[:, slot, 1:2],
                                        ALU.add).then_inc(rstd_step, 1)
                pool.wait_ge(rstd_step, 3 * t + 1)
                nc.gpsimd.tensor_tensor(rstd[:, slot:slot + 1], rstd[:, slot:slot + 1], c["eps_dm"][:],
                                        ALU.add).then_inc(rstd_step, 1)
                pool.wait_ge(rstd_step, 3 * t + 2)
                nc.gpsimd.tensor_tensor(rstd[:, slot:slot + 1], rstd[:, slot:slot + 1], c["neg_half"][:, 0:1],
                                        ALU.pow).then_inc(rstd_step, 1)

            def cut_lo(m):
                s = m % NW
                pool.wait_ge(w_hi_done, m + 1)
                nc.gpsimd.tensor_tensor(w_lo[:, s, :], raw[:, m % NRAW, :], w_hi[:, s, :].bitcast(F32),
                                        ALU.subtract).then_inc(w_lo_done, 1)

            pool_constants(nc, pool, c)
            tile_rstd(0, 0)
            tile_rstd(1, 1)
            pool.wait_ge(ffw_hi_done, 1)
            nc.gpsimd.tensor_tensor(ff_lo[:], ff_raw[:], ff_hi[:].bitcast(F32), ALU.subtract).then_inc(ffw_lo_done, 1)
            pool.wait_ge(w_lo_done, DT)
            for ch in range(CH):
                def body(i, j, last):
                    if ch == 0 and not (last and j >= 2):
                        tile_rstd(4 * i + j + 2, j % 2)
                    if ch in (FQ_, FK_):
                        n = 16 * (ch - 1) + 4 * i + j
                        pool.wait_ge(summed, n + 1)
                        nc.gpsimd.tensor_tensor(qrs[:, j % 2, :], qss[:, j % 2, :], c["eps_fd"][:],
                                                ALU.add).then_inc(qk_rstd, 1)
                        pool.wait_ge(qk_rstd, 2 * n + 1)
                        nc.gpsimd.tensor_tensor(qrs[:, j % 2, :], qrs[:, j % 2, :], c["neg_half"][:],
                                                ALU.pow).then_inc(qk_rstd, 1)
                    for m in piece_beside(ch, i, j):
                        cut_lo(m)
                each_group(pool, body)

        @block.scalar
        def _(act):
            def square_tile(i, j):
                act.wait_ge(x_in[j % 2], 16 * (2 * i + j // 2 + 1))
                for half in range(2):
                    act.wait_ge(squared, 2 * (4 * i + j) + half)
                    nc.scalar.activation(work[:], xt[:, j % 2, half * BANK:(half + 1) * BANK], ACT.Square,
                                         accum_out=ss[:, j % 2, half:half + 1]).then_inc(squared, 1)

            def tile_hi(t, slot):
                act.wait_ge(tp_ready, t + 1)
                nc.scalar.copy(ht_hi[:, :, bass.ds(t * P, P)], tpv[:, slot]).then_inc(ht_hi_done, 1)

            def cut_hi(m):
                if m < DT:
                    act.wait_ge(first_in[m // 2], 16)
                else:
                    act.wait_ge(raw_in[m % NRAW], raw_ring.landed(m - DT))
                if m >= NW:
                    ch, d = divmod(m - NW, DT)
                    if d == DT - 1:
                        act.wait_ge(acc_ready, 16 * (ch + 1))
                    else:
                        act.wait_ge(w_used, (DT - 1) * ch + d + 1)
                nc.scalar.copy(w_hi[:, m % NW, :], raw_piece(m)).then_inc(w_hi_done, 1)

            def log_sigmoid():
                act.wait_ge(gate_dve, 1)
                nc.scalar.activation(gate_ps, gate, ACT.Abs).then_inc(gate_act, 1)
                act.wait_ge(gate_act, 1)
                nc.scalar.activation(gate_ps, gate_ps, ACT.Exp, scale=-1.0).then_inc(gate_act, 1)
                act.wait_ge(gate_act, 2)
                nc.scalar.activation(gate_ps, gate_ps, ACT.Ln, bias=1.0).then_inc(gate_act, 1)

            square_tile(0, 0)
            for m in (0, 1):
                cut_hi(m)
            square_tile(0, 1)
            for m in (2, 3):
                cut_hi(m)
            tile_hi(0, 0)
            for m in range(4, DT):
                cut_hi(m)
            act_constants(nc, act, c)
            act.wait_ge(ff_in, 16)
            nc.scalar.copy(ff_hi[:], ff_raw[:]).then_inc(ffw_hi_done, 1)
            for ch in range(CH):
                def body(i, j, last):
                    n = 16 * ch + 4 * i + j
                    if ch == 0:
                        if not (last and j == 3):
                            tile_hi(4 * i + j + 1, (j + 1) % 2)
                        if not (last and j >= 2):
                            square_tile(i + (j + 2) // 4, (j + 2) % 4)
                    for m in piece_beside(ch, i, j):
                        cut_hi(m)
                    if ch == NT and isinstance(i, int) and i == 2 and j == 0:
                        log_sigmoid()
                    k = {FQ_: 0, FK_: 1, G_: 2, CH - 1: 3}.get(ch)
                    if k is not None:
                        act.wait_ge(acc_ready, n + 1)
                        act.wait_ge(banks_free, 4 + n)
                        nc.scalar.activation(work[:], acc[:, j, :],
                                             ACT.Square if ch in (FQ_, FK_) else ACT.Sigmoid).then_inc(act_out, 1)
                each_group(act, body)

        @block.vector
        def _(dve):
            def scale_tile(t, slot):
                dve.wait_ge(rstd_step, 3 * t + 3)
                nc.vector.scalar_tensor_tensor(xt[:, slot, :], xt[:, slot, :], rstd[:, slot:slot + 1], w1[:],
                                               ALU.mult, ALU.mult).then_inc(scaled, 1)

            def tile_lo(t, slot):
                dve.wait_ge(ht_hi_done, t + 1)
                nc.vector.tensor_tensor(ht_lo[:, :, bass.ds(t * P, P)], tpv[:, slot],
                                        ht_hi[:, :, bass.ds(t * P, P)].bitcast(F32), ALU.subtract).then_inc(ht_lo_done, 1)

            def cut_lo(m):
                dve.wait_ge(w_hi_done, m + 1)
                nc.vector.tensor_tensor(w_lo[:, m, :], raw_piece(m), w_hi[:, m, :].bitcast(F32), ALU.subtract).then_inc(w_lo_done, 1)

            def gate_logits():
                dve.wait_ge(bias_in, 16)
                dve.wait_ge(ff_ready, 1)
                nc.vector.tensor_scalar(gate, gate_ps, f_bias[:, 0:1], None, ALU.add).then_inc(gate_dve, 1)

            def gate_sums():
                dve.wait_ge(gate_act, 3)
                nc.vector.tensor_scalar(gate, gate, 0.0, None, ALU.min).then_inc(gate_dve, 1)
                dve.wait_ge(gate_dve, 2)
                nc.vector.tensor_tensor(gate, gate, gate_ps, ALU.subtract).then_inc(gate_dve, 1)
                nc.vector.memset(one[:], 1.0).then_inc(gate_dve, 1)
                dve.wait_ge(gate_dve, 4)
                nc.vector.tensor_tensor_scan(gate, one[:, 0:1].broadcast_to([FH, S]), gate, 0.0, ALU.mult,
                                            ALU.add).then_inc(gate_dve, 1)

            dve.sem_inc(banks_free, 4)
            dve.wait_ge(w1_in, 16)
            nc.vector.tensor_scalar(w1[:], w1[:], float(DM) ** 0.5, None, ALU.mult).then_inc(w1_scaled, 1)
            dve.wait_ge(w1_scaled, 1)
            scale_tile(0, 0)
            for m in range(4):
                cut_lo(m)
            scale_tile(1, 1)
            tile_lo(0, 0)
            for m in range(4, DT):
                cut_lo(m)
            dve_weights(nc, dve, c)
            for ch in range(CH):
                def body(i, j, last):
                    n = 16 * ch + 4 * i + j
                    if ch == 0:
                        if not (last and j == 3):
                            tile_lo(4 * i + j + 1, (j + 1) % 2)
                        if not (last and j >= 2):
                            scale_tile(4 * i + j + 2, j % 2)
                    if ch == NT and isinstance(i, int) and i == 2 and j == 0:
                        gate_logits()
                    if ch == NT and isinstance(i, int) and i == 3 and j == 0:
                        gate_sums()
                        dve_lower_bounds(nc, dve, c)
                    dve.wait_ge(acc_ready, n + 1)
                    src, dst = acc[:, j, :], stage[:, j, :]
                    if ch in (FQ_, FK_):
                        k = n - 16 * FQ_
                        dve.wait_ge(act_out, k + 1)
                        nc.vector.tensor_reduce(qss[:, j % 2, :], work[:].rearrange("p (h e) -> p h e", h=FH),
                                                AX.X, ALU.add).then_inc(summed, 1)
                    dve.wait_ge(stored[j], 16 * (START + 4 * ch + i))
                    if ch in (V_, FV_):
                        nc.vector.tensor_copy(dst, src).then_inc(banks_free, 1)
                    elif ch in (FQ_, FK_):
                        heads = dst.rearrange("p (h e) -> p h e", h=FH)
                        nc.vector.tensor_tensor(heads, src.rearrange("p (h e) -> p h e", h=FH),
                                                c["qk_w"][:, ch - FQ_:ch - FQ_ + 1, :].broadcast_to([P, FH, FD]),
                                                ALU.mult).then_inc(dve_step, 1)
                        dve.wait_ge(dve_step, k + 1)
                        dve.wait_ge(qk_rstd, 2 * k + 2)
                        nc.vector.tensor_tensor(heads, heads, qrs[:, j % 2, :].unsqueeze(2).broadcast_to([P, FH, FD]),
                                                ALU.mult).then_inc(banks_free, 1)
                    elif ch == G_:
                        k = n - 32
                        dve.wait_ge(act_out, 32 + n - 16 * G_ + 1)
                        nc.vector.tensor_tensor(dst, src, work[:], ALU.mult).then_inc(dve_step, 1)
                        dve.wait_ge(dve_step, 32 + n - 16 * G_ + 1)
                        nc.vector.tensor_tensor(dst.rearrange("p (h e) -> p h e", h=HH),
                                                dst.rearrange("p (h e) -> p h e", h=HH),
                                                c["hgrn_w"][:].unsqueeze(1).broadcast_to([P, HH, P]),
                                                ALU.mult).then_inc(banks_free, 1)
                    elif ch == NT:
                        nc.vector.tensor_scalar(dst, src, float(P) ** -0.5, None, ALU.mult).then_inc(banks_free, 1)
                    else:
                        dve.wait_ge(act_out, 48 + n - 16 * (CH - 1) + 1)
                        nc.vector.tensor_scalar(dst, work[:], c["one_minus_lb"][:, bass.ds(i, 1)],
                                                c["lb"][:, bass.ds(i, 1)], ALU.mult, ALU.add).then_inc(banks_free, 1)
                each_group(dve, body)

        @block.tensor
        def _(pe):
            def transpose_tile(t, slot):
                pe.wait_ge(scaled, t + 1)
                for d in range(DT):
                    last = nc.tensor.transpose(tpv[:, slot, d, :], xt[:, slot, d * P:(d + 1) * P], c["ident"][:])
                last.then_inc(tp_ready, 1)

            pe.wait_ge(c["pool_made"], 2)
            transpose_tile(0, 0)

            def token_major(ch, first):
                for t in range(TT):
                    tok = slice(t * P, (t + 1) * P)
                    if first:
                        if t + 1 < TT:
                            pe.wait_ge(ht_lo_done, t)
                            transpose_tile(t + 1, (t + 1) % 2)
                        pe.wait_ge(ht_lo_done, t + 1)
                    pe.wait_ge(banks_free, 16 * ch + t + 1)
                    for d in range(DT):
                        s = DT * (ch % 2) + d
                        if t == 0:
                            pe.wait_ge(w_lo_done, DT * ch + d + 1)
                        m = three_pass(nc, acc[:, t % 4, :], ht_hi[:, d, tok], ht_lo[:, d, tok], w_hi[:, s, :],
                                       w_lo[:, s, :], d == 0, d == DT - 1)
                        if t == TT - 1 and d < DT - 1:
                            m.then_inc(w_used, 1)
                    m.then_inc(acc_ready, 1)

            def forget_logits():
                pe.wait_ge(ffw_lo_done, 1)
                for g in range(4):
                    tok = slice(g * BANK, (g + 1) * BANK)
                    for d in range(DT):
                        m = three_pass(nc, tp[0:FH, g, :], ff_hi[:, d, :], ff_lo[:, d, :], ht_hi[:, d, tok], ht_lo[:, d, tok],
                                       d == 0, d == DT - 1)
                m.then_inc(ff_ready, 1)

            def channel_major(ch):
                for k in range(4):
                    col = slice(k * P, (k + 1) * P)
                    with pe.Fori(0, 4) as g:
                        pe.wait_ge(banks_free, 16 * ch + 4 * k + g + 1)
                        for d in range(DT):
                            s = DT * (ch % 2) + d
                            if k == 0:
                                pe.wait_ge(w_lo_done, DT * ch + d + 1)
                            tok = bass.ds(g * BANK, BANK)
                            m = three_pass(nc, acc[:, g, :], w_hi[:, s, col], w_lo[:, s, col], ht_hi[:, d, tok],
                                           ht_lo[:, d, tok], d == 0, d == DT - 1)
                        m.then_inc(acc_ready, 1)

            token_major(0, True)
            with pe.Fori(1, NT) as ch:
                token_major(ch, False)
            forget_logits()
            channel_major(NT)
            channel_major(NT + 1)


LV = 7
UN = BANK // P


def recurrence(nc, ctx, c, tok_in, ch_in, mix_out):
    def sem(name):
        return ctx.enter_context(nc.semaphore("r_" + name))

    q_in, f_in, v_in, g_in = ([sem(f"{n}_in{k}") for k in range(4)] for n in "qfvg")
    stored = [sem(f"stored{k}") for k in range(2)]
    (zeroed, blank_done, mask_step, masks_done, k_done, lnf_done, b_done, eb_done, d_done, e_done, ql_done, kl_done, a_ready, pm_done,
     kdt_ready, kdt_done, kdv_ready, s_done, o_ready, osq_done, orstd, fin) = (sem(n) for n in (
         "zeroed", "blank_done", "mask_step", "masks_done", "k_done", "lnf_done", "b_done", "eb_done", "d_done", "e_done", "ql_done",
         "kl_done", "a_ready", "pm_done", "kdt_ready", "kdt_done", "kdv_ready", "s_done", "o_ready",
         "osq_done", "orstd", "fin"))
    with ExitStack() as own:
        def sb(name, shape, dt=F32):
            return own.enter_context(nc.sbuf_tensor("r_" + name, shape, dt))

        def ps(name, shape):
            return own.enter_context(nc.psum_tensor("r_" + name, shape, F32))

        q, f = sb("q", [P, 4, BANK]), sb("f", [P, 4, BANK])
        v, g = sb("v", [P, 4, UN, P]), sb("g", [P, 4, UN, P])
        lnf, b = sb("lnf", [P, BANK]), sb("b", [P, BANK])
        eb, k = sb("eb", [P, 2, BANK]), sb("k", [P, 2, BANK])
        e = sb("e", [P, 2, LV + 1, BANK])
        ql, kl = sb("ql", [P, 2, LV, BANK]), sb("kl", [P, 2, LV, BANK])
        qb, kd = sb("qb", [P, 2, BANK]), sb("kd", [P, 2, BANK])
        ones = sb("ones", [P, BANK])
        keep = sb("keep", [P, BANK])
        mask = sb("mask", [P, LV + 1, P])
        pm = sb("pm", [P, 2, LV + 1, P])
        kdt = sb("kdt", [P, 2, P])
        state = sb("state", [P, 2, P])
        junk, oss, ors = sb("junk", [P, 2, P]), sb("oss", [P, 2]), sb("ors", [P, 2])
        mix = sb("mix", [P, 2, UN, P])
        a_ps = [ps(f"a{n}", [P, LV + 1, P]) for n in range(2)]
        kdt_ps, kdv_ps = ps("kdt_ps", [P, BANK]), ps("kdv_ps", [P, BANK])
        o_ps = [ps(f"o{n}", [P, BANK]) for n in range(2)]
        block = own.enter_context(nc.Block())

        def halves(ap, lvl):
            w = 64 >> lvl
            return ap.rearrange("p (n two w) -> p n two w", two=2, w=w)

        def each_head(eng, prologue, unit, epilogue):
            prologue()
            with eng.Fori(0, HH - 1) as h:
                for u in range(4):
                    unit(h, u)
                epilogue(h)
            for u in range(4):
                unit(HH - 1, u)
            epilogue(HH - 1)

        def nxt(h, u, by=1):
            return h + (u + by) // 4, (u + by) % 4

        def next_chunk(h, i):
            if isinstance(h, int) and i == 15:
                return None
            return h + (i + 1) // 16, (i + 1) % 16

        EXPONENTS = ((), (0, 1, 2, 3), (4, 5, 6), (7,), ())

        def first_parts(prepare):
            for part in range(5):
                prepare(0, 0, part)
            prepare(0, 1, 0)
            prepare(0, 1, 1)

        def prepare_beside(prepare, h, u, chunk):
            for by, part in (((1, 2),), ((1, 3),), ((1, 4), (2, 0)), ((2, 1),))[chunk]:
                if not (isinstance(h, int) and u + by > 3):
                    prepare(*nxt(h, u, by), part)

        @block.sync
        def _(sp):
            def load(h, u):
                sp.dma_start(q[:, u, :], ch_in[0, h, :, u * BANK:(u + 1) * BANK]).then_inc(q_in[u], 16)
                sp.dma_start(f[:, u, :], ch_in[1, h, :, u * BANK:(u + 1) * BANK]).then_inc(f_in[u], 16)
                for dst, group, done in ((v, V_, v_in), (g, G_, g_in)):
                    src = tok_in[group, u * UN:(u + 1) * UN, :, bass.ds(h * P, P)].rearrange("t p e -> p t e")
                    sp.dma_start(dst[:, u], src).then_inc(done[u], 16)

            def prologue():
                for n in range(2):
                    sp.sem_inc(stored[n], 16 * START)
                for u in range(3):
                    load(0, u)

            def unit(h, u):
                sp.wait_ge(fin, START + 16 * h + 4 * u + 4)
                dst = mix_out[u * UN:(u + 1) * UN, :, bass.ds(h * P, P)].rearrange("t p e -> p t e")
                sp.dma_start(dst, mix[:, u % 2]).then_inc(stored[u % 2], 16)
                if not (isinstance(h, int) and u > 0):
                    load(*nxt(h, u, 3))

            each_head(sp, prologue, unit, lambda h: None)
            for n in range(2):
                sp.wait_ge(stored[n], 16 * (START + 2 * HH))

        @block.gpsimd
        def _(pool):
            def prologue():
                pool.sem_inc(orstd, START)
                pool.sem_inc(kl_done, 8)
                nc.gpsimd.memset(kl[:, 0], 0.0).then_inc(zeroed, 1)
                pool.wait_ge(zeroed, 1)
                for part in range(5):
                    prepare(0, 0, part)
                nc.gpsimd.memset(mask[:], 1.0).then_inc(mask_step, 1)
                pool.wait_ge(mask_step, 1)
                step = 1
                for lvl in range(1, LV):
                    w2 = 128 >> lvl
                    m = mask[:, lvl, :].rearrange("p (n w) -> p n w", w=w2)
                    nc.gpsimd.affine_select(out=m, in_=m, compare_op=ALU.is_ge, fill=0.0, base=0,
                                            pattern=[[-w2, P // w2], [0, w2]], channel_multiplier=1).then_inc(mask_step, 1)
                    step += 1
                    pool.wait_ge(mask_step, step)
                    nc.gpsimd.affine_select(out=m, in_=m, compare_op=ALU.is_ge, fill=0.0, base=w2 - 1,
                                            pattern=[[w2, P // w2], [0, w2]], channel_multiplier=-1).then_inc(mask_step, 1)
                    step += 1
                nc.gpsimd.tensor_copy(mask[:, LV, :], c["ident"][:]).then_inc(mask_step, 1)
                step += 1
                pool.wait_ge(mask_step, step)
                pool.sem_inc(masks_done, 1)
                nc.gpsimd.memset(kl[:, 1], 0.0).then_inc(zeroed, 1)
                pool.wait_ge(zeroed, 2)

            def prepare(h, u, part):
                n = 4 * h + u
                if part == 2:
                    if isinstance(n, int) and n == 0:
                        pool.wait_ge(blank_done, 1)
                    pool.wait_ge(f_in[u], 16 * (h + 1))
                    if not (isinstance(n, int) and n < 2):
                        pool.wait_ge(a_ready, START + 4 * n - 4)
                    nc.gpsimd.tensor_tensor(k[:, u % 2, :], ones[:], f[:, u, :], ALU.subtract).then_inc(k_done, 1)
                    pool.wait_ge(k_done, n + 1)
                for lvl in ((), (), (0, 1, 2), (3, 4, 5), (6, 7))[part]:
                    pool.wait_ge(e_done, 8 * n + lvl + 1)
                    if lvl < LV:
                        dst = halves(kl[:, u % 2, lvl, :], lvl)[:, :, 0, :]
                        src = halves(k[:, u % 2, :], lvl)[:, :, 0, :]
                        by = halves(e[:, u % 2, lvl, :], lvl)[:, :, 0, :]
                    else:
                        dst, src, by = kd[:, u % 2, :], k[:, u % 2, :], e[:, u % 2, LV, :]
                    nc.gpsimd.tensor_tensor(dst, src, by, ALU.mult).then_inc(kl_done, 1)

            def out_rstd(h, i):
                n = 16 * h + i
                s = slice(i % 2, i % 2 + 1)
                pool.wait_ge(osq_done, n + 1)
                pool.wait_ge(fin, START + (n - 1 if i >= 2 else 16 * h))
                nc.gpsimd.tensor_tensor(ors[:, s], oss[:, s], c["eps_p"][:], ALU.add).then_inc(orstd, 1)
                pool.wait_ge(orstd, START + 2 * n + 1)
                nc.gpsimd.tensor_tensor(ors[:, s], ors[:, s], c["neg_half"][:, 0:1], ALU.pow).then_inc(orstd, 1)

            def unit(h, u):
                for part in range(4):
                    i = 4 * u + part
                    prepare_beside(prepare, h, u, part)
                    if i >= 1:
                        out_rstd(h, i - 1)

            each_head(pool, prologue, unit, lambda h: out_rstd(h, 15))

        @block.scalar
        def _(act):
            def prepare(h, u, part):
                n = 4 * h + u
                if part == 0:
                    act.wait_ge(f_in[u], 16 * (h + 1))
                    nc.scalar.activation(lnf[:], f[:, u, :], ACT.Ln).then_inc(lnf_done, 1)
                if part == 2:
                    act.wait_ge(b_done, n + 1)
                    if not (isinstance(n, int) and n < 2):
                        act.wait_ge(s_done, START + 4 * n - 4)
                    nc.scalar.activation(eb[:, u % 2, :], b[:], ACT.Exp).then_inc(eb_done, 1)
                for lvl in EXPONENTS[part]:
                    act.wait_ge(d_done, 8 * n + lvl + 1)
                    if lvl < LV:
                        ev = halves(e[:, u % 2, lvl, :], lvl)
                        nc.scalar.activation(ev[:, :, 1, :], ev[:, :, 1, :], ACT.Exp)
                        nc.scalar.activation(ev[:, :, 0, :], ev[:, :, 0, :], ACT.Exp, scale=-1.0).then_inc(e_done, 1)
                    else:
                        nc.scalar.activation(e[:, u % 2, LV, :], e[:, u % 2, LV, :], ACT.Exp, scale=-1.0).then_inc(e_done, 1)

            def turned(h, i):
                n = 16 * h + i
                act.wait_ge(kdt_ready, n + 1)
                if not (isinstance(n, int) and n < 2):
                    act.wait_ge(kdv_ready, START + n - 1)
                nc.scalar.copy(kdt[:, i % 2, :], kdt_ps[:, 0:P]).then_inc(kdt_done, 1)

            def square_out(h, i):
                n = 16 * h + i
                act.wait_ge(o_ready, START + n + 1)
                act.wait_ge(orstd, START + (2 * (n - 1) if i >= 2 else 32 * h))
                nc.scalar.activation(junk[:, i % 2, :], o_ps[i % 2][:, 0:P], ACT.Square,
                                     accum_out=oss[:, i % 2:i % 2 + 1]).then_inc(osq_done, 1)

            def unit(h, u):
                for part in range(4):
                    i = 4 * u + part
                    if next_chunk(h, i):
                        turned(*next_chunk(h, i))
                    if i >= 1:
                        square_out(h, i - 1)
                    prepare_beside(prepare, h, u, part)

            def prologue():
                first_parts(prepare)
                turned(0, 0)

            each_head(act, prologue, unit, lambda h: square_out(h, 15))

        @block.vector
        def _(dve):
            def prepare(h, u, part):
                n = 4 * h + u
                if part == 0:
                    dve.wait_ge(lnf_done, n + 1)
                    dve.wait_ge(eb_done, n)
                    nc.vector.tensor_tensor_scan(b[:], keep[:], lnf[:], 0.0, ALU.mult, ALU.add).then_inc(b_done, 1)
                    dve.wait_ge(b_done, n + 1)
                for lvl in EXPONENTS[part]:
                    if not (isinstance(n, int) and n < 2):
                        dve.wait_ge(kl_done, 8 * n + lvl - 7)
                    w2 = 128 >> lvl if lvl < LV else P
                    bv = b[:].rearrange("p (n w) -> p n w", w=w2)
                    at = w2 // 2 - 1 if lvl < LV else P - 1
                    nc.vector.tensor_tensor(e[:, u % 2, lvl, :].rearrange("p (n w) -> p n w", w=w2), bv,
                                            bv[:, :, at:at + 1].broadcast_to([P, BANK // w2, w2]),
                                            ALU.subtract).then_inc(d_done, 1)
                for lvl in ((), (), (0, 1), (2, 3, 4, 5), (6, 7))[part]:
                    if lvl in (0, LV) and not (isinstance(n, int) and n < 2):
                        dve.wait_ge(o_ready if lvl else a_ready, START + 4 * n - 4)
                    if lvl < LV:
                        dve.wait_ge(e_done, 8 * n + lvl + 1)
                        if lvl == 0:
                            dve.wait_ge(q_in[u], 16 * (h + 1))
                        dst = halves(ql[:, u % 2, lvl, :], lvl)[:, :, 1, :]
                        src = halves(q[:, u, :], lvl)[:, :, 1, :]
                        by = halves(e[:, u % 2, lvl, :], lvl)[:, :, 1, :]
                    else:
                        dve.wait_ge(eb_done, n + 1)
                        dst, src, by = qb[:, u % 2, :], q[:, u, :], eb[:, u % 2, :]
                    nc.vector.tensor_tensor(dst, src, by, ALU.mult).then_inc(ql_done, 1)

            def mask_levels(h, i):
                n = 16 * h + i
                dve.wait_ge(a_ready, START + n + 1)
                if i >= 2:
                    dve.wait_ge(o_ready, START + n - 1)
                nc.vector.tensor_tensor(pm[:, i % 2], a_ps[i % 2][:], mask[:], ALU.mult).then_inc(pm_done, 1)

            def step_state(h, i):
                n = 16 * h + i
                dve.wait_ge(kdv_ready, START + n + 1)
                new = state[:, (i + 1) % 2, :]
                if i == 0:
                    nc.vector.tensor_copy(new, kdv_ps[:, 0:P]).then_inc(s_done, 1)
                else:
                    dve.wait_ge(s_done, START + n)
                    at = (i % 4) * P + P - 1
                    nc.vector.scalar_tensor_tensor(new, state[:, i % 2, :], eb[:, i // 4 % 2, at:at + 1], kdv_ps[:, 0:P],
                                                   ALU.mult, ALU.add).then_inc(s_done, 1)

            def finish(h, i):
                n = 16 * h + i
                u, ch = i // 4, i % 4
                dve.wait_ge(orstd, START + 2 * n + 2)
                if ch == 0:
                    dve.wait_ge(g_in[u], 16 * (h + 1))
                    dve.wait_ge(stored[u % 2], 16 * (START + 2 * h + u // 2))
                nc.vector.scalar_tensor_tensor(mix[:, u % 2, ch, :], o_ps[i % 2][:, 0:P], ors[:, i % 2:i % 2 + 1],
                                               g[:, u, ch, :], ALU.mult, ALU.mult).then_inc(fin, 1)

            def unit(h, u):
                for part in range(4):
                    i = 4 * u + part
                    mask_levels(h, i)
                    step_state(h, i)
                    if i >= 2:
                        finish(h, i - 2)
                    prepare_beside(prepare, h, u, part)

            def prologue():
                dve.sem_inc(fin, START)
                dve.sem_inc(s_done, START)
                nc.vector.memset(ones[:], 1.0).then_inc(blank_done, 1)
                nc.vector.memset(keep[:], 1.0).then_inc(blank_done, 1)
                dve.wait_ge(blank_done, 2)
                nc.vector.memset(keep[:].rearrange("p (n w) -> p n w", w=P)[:, :, 0:1], 0.0).then_inc(blank_done, 1)
                dve.wait_ge(blank_done, 3)
                nc.vector.memset(ql[:, 0], 0.0).then_inc(blank_done, 1)
                prepare(0, 0, 0)
                prepare(0, 0, 1)
                dve.wait_ge(blank_done, 4)
                for part in range(2, 5):
                    prepare(0, 0, part)
                nc.vector.memset(ql[:, 1], 0.0).then_inc(blank_done, 1)
                prepare(0, 1, 0)
                prepare(0, 1, 1)
                dve.wait_ge(blank_done, 5)
                dve.wait_ge(masks_done, 1)

            def epilogue(h):
                finish(h, 14)
                finish(h, 15)

            each_head(dve, prologue, unit, epilogue)

        @block.tensor
        def _(pe):
            def level_products(h, i):
                n, u = 16 * h + i, i // 4
                t = slice(i % 4 * P, i % 4 * P + P)
                if i >= 2:
                    pe.wait_ge(pm_done, n - 1)
                for lvl in range(LV):
                    if i % 4 == 0:
                        pe.wait_ge(ql_done, 8 * (4 * h + u) + lvl + 1)
                        pe.wait_ge(kl_done, 8 * (4 * h + u) + lvl + 9)
                    nc.tensor.matmul(a_ps[i % 2][:, lvl, :], kl[:, u % 2, lvl, t], ql[:, u % 2, lvl, t], start=True, stop=True)
                nc.tensor.matmul(a_ps[i % 2][:, LV, :], k[:, u % 2, t], q[:, u, t], start=True, stop=True).then_inc(a_ready, 1)

            def turn(h, i):
                n, u = 16 * h + i, i // 4
                if i % 4 == 0:
                    pe.wait_ge(kl_done, 8 * (4 * h + u) + 16)
                if not (isinstance(n, int) and n < 1):
                    pe.wait_ge(kdt_done, n)
                nc.tensor.transpose(kdt_ps[:, 0:P], kd[:, u % 2, i % 4 * P:(i % 4 + 1) * P],
                                    c["ident"][:]).then_inc(kdt_ready, 1)

            def output(h, i):
                n, u, ch = 16 * h + i, i // 4, i % 4
                t = slice(ch * P, ch * P + P)
                if ch == 0:
                    pe.wait_ge(v_in[u], 16 * (h + 1))
                pe.wait_ge(pm_done, n + 1)
                pe.wait_ge(fin, START + (n - 1 if i >= 2 else 16 * h))
                for lvl in range(LV + 1):
                    m = nc.tensor.matmul(o_ps[i % 2][:, 0:P], pm[:, i % 2, lvl, :], v[:, u, ch, :], start=lvl == 0,
                                         stop=i == 0 and lvl == LV)
                if i > 0:
                    pe.wait_ge(s_done, START + n)
                    m = nc.tensor.matmul(o_ps[i % 2][:, 0:P], qb[:, u % 2, t], state[:, i % 2, :], start=False, stop=True)
                m.then_inc(o_ready, 1)

            def unit(h, u):
                for part in range(4):
                    i = 4 * u + part
                    n = 16 * h + i
                    level_products(h, i)
                    if next_chunk(h, i):
                        turn(*next_chunk(h, i))
                    if i >= 1:
                        output(h, i - 1)
                    pe.wait_ge(kdt_done, n + 1)
                    pe.wait_ge(s_done, START + n)
                    if part == 0:
                        pe.wait_ge(v_in[u], 16 * (h + 1))
                    nc.tensor.matmul(kdv_ps[:, 0:P], kdt[:, i % 2, :], v[:, u, part, :], start=True, stop=True).then_inc(kdv_ready, 1)

            def prologue():
                for count in (a_ready, kdv_ready, o_ready):
                    pe.sem_inc(count, START)
                turn(0, 0)

            each_head(pe, prologue, unit, lambda h: output(h, 15))


KB = S // P
QG = KB // 4
FAR = 2.0 ** 100


class Head:

    def __init__(self, n, slot, half):
        self.n, self.slot, self.half = n, slot, half

    def next(self):
        return Head(self.n + 1, 1 - self.slot, self.half + self.slot)

    def last(self):
        return Head(self.n - 1, 1 - self.slot, self.half - 1 + self.slot)


def tile_parts(i):
    n = (i + 1) * P
    if i in (2, 3):
        return [BANK // 2, n - BANK // 2]
    return [min(BANK, n - at) for at in range(0, n, BANK)]




S_RING, T_RING, LAG = 3, 4, 3
LO_AFTER = 1
S_ITEMS = sum(len(tile_parts(i)) for i in range(KB))
T_ITEMS = sum(4 * g + 4 for g in range(QG))
PREP = 3 * QG
RING = T_ITEMS + PREP + QG
assert RING % T_RING == 0 and S_ITEMS % S_RING == 0


def head_order(first=False, last=False, tail=False):
    def blocks_of(g):
        return [(0 if g < QG - 1 else 1, g, kb) for kb in range(4 * g + 4)]

    order = []
    for g in range(1 if tail else QG):
        tg = (g - 1) % QG
        blocks = [] if first and g == 0 else blocks_of(tg)
        before = [(1, tg - 1, kb) for kb in range(4 * tg)] if g == 0 else blocks_of((g - 2) % QG)
        if first and g <= 1:
            before = []
        due = before[-LAG:] + blocks
        work = []
        for k, block in enumerate(blocks):
            work.append([("block",) + block])
            if before or k >= LAG:
                work[-1].append(("product",) + due[k if before else k - LAG])
            if k == LAG - 1 and before:
                work[-1].append(("copy",) + before[-1][:2])
            if k == LAG and before:
                work[-1].append(("fold",) + before[-1][:2])
        if tail:
            work += [[("product",) + block] for block in due[-LAG:]] + [[("copy",) + due[-1][:2], ("fold",) + due[-1][:2]]]
            return [item for items in work for item in items]
        if not last and g > 0:
            for k in range(4):
                work.insert((k + 1) * (len(blocks) + 4) // 5, [("prep", 4 * (g - 1) + k)])
        order.append(("step", g))
        done, delayed = 0, []
        scores = [(i, part) for i in range(4 * g, 4 * g + 4) for part in range(len(tile_parts(i)))]
        for k, (i, part) in enumerate(scores):
            order.append(("score", i, part))
            upto = len(work) * k // (len(scores) - 1)
            for items in work[done:upto]:
                order += items + delayed
                delayed = []
            done = upto
            if part == len(tile_parts(i)) - 1:
                delayed.append(("exp", i))
            if len(delayed) > 1:
                order.append(delayed.pop(0))
        order += delayed
    return order


def with_lows(order):
    out, waiting, units, blocks = [], [], 0, 0
    for item in order:
        if item[0] == "fold":
            out, waiting = out + waiting, []
        out.append(item)
        if item[0] in ("block", "prep", "fold"):
            if item[0] == "block":
                waiting.append(("lo", item[2], item[3], units, blocks))
                blocks += 1
            units += 1
            while waiting and units - 1 - waiting[0][3] >= LO_AFTER:
                out.append(waiting.pop(0))
    return out + waiting


def ring_kinds(order):
    return [item[0] for item in order if item[0] in ("block", "prep", "fold")]


def attention(nc, ctx, c, tok_in, cum_in, mix_out):
    def sem(name):
        return ctx.enter_context(nc.semaphore("a_" + name))

    names = ("mask_step", "consts_done", "q_in", "k_in", "v_in",
             "s_ready", "scored", "p_ready", "t_ready", "t_hi", "t_lo", "u_out", "hi_done", "k_cut", "q_cut", "v_cut",
             "pv_done", "o_copied", "fin", "recip_done")
    (mask_step, consts_done, q_in, k_in, v_in, s_ready, scored, p_ready,
     t_ready, t_hi, t_lo, u_out, hi_done, k_cut, q_cut, v_cut, pv_done, o_copied, fin, recip_done) = (sem(n) for n in names)
    passed_dve, passed_pool, passed_sp = sem("passed_dve"), sem("passed_pool"), sem("passed_sp")
    cb_in = [sem(f"cb_in{n}") for n in range(2)]
    stored = [sem(f"stored{n}") for n in range(2)]
    with ExitStack() as own:
        def sb(name, shape, dt=F32):
            return own.enter_context(nc.sbuf_tensor("a_" + name, shape, dt))

        def ps(name, shape):
            return own.enter_context(nc.psum_tensor("a_" + name, shape, F32))

        kst, q1, q2 = (sb(n, [P, 2, S], F32R) for n in ("kst", "q1", "q2"))
        vcat = sb("vcat", [P, 2, KB, P], F32R)
        cb = sb("cb", [P, 2, S])
        qraw, kraw, vraw = (sb(n, [P, KB, FD]) for n in ("qraw", "kraw", "vraw"))
        kcat, qcat1, qcat2 = (sb(n, [P, KB, 2, FD], F32R) for n in ("kcat", "qcat1", "qcat2"))
        p = sb("p", [P, 2, 4, S])
        pt_hi, pt_lo = sb("pt_hi", [P, 4, BANK], F32R), sb("pt_lo", [P, 4, BANK], F32R)
        ot = sb("ot", [P, BANK])
        stage = sb("stage", [P, 2, KB, FD])
        low = sb("low", [P, KB, 6])
        total, recip = sb("total", [P, QG, 4]), sb("recip", [P, QG, 4])
        ident_r, beyond_r, beyond = sb("ident_r", [P, P], F32R), sb("beyond_r", [P, P], F32R), sb("beyond", [P, P])
        fold = sb("fold", [P, FD])
        s_ps = [ps(f"s{n}", [P, BANK]) for n in range(S_RING)]
        t_ps = [ps(f"t{n}", [P, BANK]) for n in range(T_RING)]
        o_ps = ps("o", [P, BANK])

        def load(sp, h):
            for dst, group, done in ((kraw, FK_, k_in), (qraw, FQ_, q_in), (vraw, FV_, v_in)):
                sp.dma_start(dst[:], tok_in[group, :, :, bass.ds(h.n * FD, FD)].rearrange("t p e -> p t e")).then_inc(done, 16)

        def load_gate(sp, h):
            row = cum_in[bass.ds(h.n, 1), :].partition_broadcast(P)
            sp.dma_start(cb[:, h.slot:h.slot + 1, :], row).then_inc(cb_in[h.slot], 16)

        def cut_pair(eng, ops, raw, hi, lo, counter, count, done):
            ops.tensor_copy(hi, raw[:]).then_inc(counter, 1)
            eng.wait_ge(counter, count)
            ops.tensor_tensor(lo, raw[:], hi.bitcast(F32), ALU.subtract).then_inc(done, 1)

        def cut_k(eng, ops, counter, count):
            cut_pair(eng, ops, kraw, kcat[:, :, 0, :], kcat[:, :, 1, :], counter, count, k_cut)

        def cut_q(eng, ops, counter, count):
            ops.tensor_copy(qcat1[:, :, 1, :], qraw[:]).then_inc(q_cut, 1)
            cut_pair(eng, ops, qraw, qcat1[:, :, 0, :], qcat2[:, :, 0, :], counter, count, q_cut)
            ops.tensor_tensor(qcat2[:, :, 1, :], qraw[:], qcat1[:, :, 0, :].bitcast(F32), ALU.subtract).then_inc(q_cut, 1)

        def cut_v(eng, ops, h, counter, count):
            cut_pair(eng, ops, vraw, vcat[:, h.slot, :, 0:FD], vcat[:, h.slot, :, FD:P], counter, count, v_cut)

        def unit_places(h, u):
            part, quarter = u // QG, u % QG
            cat, transposed = (kcat, qcat1, qcat2)[part], (kst, q1, q2)[part]
            return cat, transposed[:, h.slot, quarter * BANK:(quarter + 1) * BANK], range(4 * quarter, 4 * quarter + 4)

        def unit_out(act, h, u, slot, ring):
            act.wait_ge(t_ready, ring + 1)
            nc.scalar.copy(unit_places(h, u)[1], t_ps[slot][:]).then_inc(u_out, 1)

        def unit_in(pe, h, u, slot):
            cat, _, tiles = unit_places(h, u)
            if u == 0:
                pe.wait_ge(k_cut, h.n + 1)
            elif u == QG:
                pe.wait_ge(q_cut, 3 * (h.n + 1))
            for k, t in enumerate(tiles):
                m = nc.tensor.matmul(t_ps[slot][:, k * P:(k + 1) * P], cat[:, t].rearrange("p two e -> p (two e)"), ident_r[:],
                                     start=True, stop=True)
            m.then_inc(t_ready, 1)

        first_head = Head(0, 0, 0)
        block = own.enter_context(nc.Block())

        class At:

            def __init__(self, h, order, before):
                first = before is None
                after = order is TAIL
                self.score = S_ITEMS * h.n
                self.block = 0 if first else T_ITEMS * h.n - KB
                self.product = 0 if first else T_ITEMS * h.n - KB - LAG
                self.fold = 0 if first else QG * h.n - 2
                self.prep = PREP * h.n + (0 if after else PREP)
                self.ring = self.block + self.prep + self.fold
                self.slot = (0 if first else -KB - 2) + (0 if after else PREP)
                self.recent = (["prep"] * T_RING if first else ring_kinds(before))[-T_RING:]

        TAIL = with_lows(head_order(tail=True))
        FIRST, MIDDLE, LAST = (with_lows(order) for order in (head_order(first=True), head_order(), head_order(last=True)))
        assert ring_kinds(FIRST)[-T_RING:] == ring_kinds(MIDDLE)[-T_RING:]

        def each_head(eng, run):
            h = first_head
            run(h, FIRST, At(h, FIRST, None))
            with eng.Fori(0, (FH - 2) // 2) as m:
                for h in (Head(2 * m + 1, 1, m), Head(2 * m + 2, 0, m + 1)):
                    run(h, MIDDLE, At(h, MIDDLE, MIDDLE))
            h = Head(FH - 1, 1, FH // 2 - 1)
            run(h, LAST, At(h, LAST, MIDDLE))
            h = Head(FH, 0, FH // 2)
            run(h, TAIL, At(h, TAIL, LAST))

        def last_item(i):
            return sum(len(tile_parts(k)) for k in range(i + 1))

        def queries(g, kb):
            return max(0, kb - 4 * g) * P

        def owner(h, before):
            return h.last() if before else h

        @block.sync
        def _(sp):
            def run(h, order, at):
                if order is FIRST or order is MIDDLE:
                    if order is MIDDLE:
                        wait_alone(sp, v_cut, h.n + 1, passed_sp)
                        load(sp, h.next())
                        wait_alone(sp, scored, at.score, passed_sp)
                    load_gate(sp, h.next())
                if order is not FIRST:
                    b = h.last()
                    wait_alone(sp, fin, QG * h.n, passed_sp)
                    sp.dma_start(mix_out[:, :, bass.ds(b.n * FD + FH * FD, FD)].rearrange("t p e -> p t e"),
                                 stage[:, b.slot]).then_inc(stored[b.slot], 16)

            load(sp, first_head)
            load_gate(sp, first_head)
            for n in range(2):
                sp.sem_inc(stored[n], 16 * START)
            sp.wait_ge(v_cut, 1)
            load(sp, first_head.next())
            each_head(sp, run)
            for n in range(2):
                sp.wait_ge(stored[n], 16 * (START + FH // 2))

        @block.gpsimd
        def _(pool):
            def run(h, order, at):
                if order is FIRST or order is MIDDLE:
                    m = h.next()
                    counts = [3 * m.n + 1, 3 * m.n + 2, 3 * m.n + 3]
                    wait_alone(pool, t_ready, at.ring, passed_pool)
                    wait_alone(pool, k_in, 16 * (m.n + 1), passed_pool)
                    cut_k(pool, nc.gpsimd, hi_done, counts[0])
                    wait_alone(pool, q_in, 16 * (m.n + 1), passed_pool)
                    cut_q(pool, nc.gpsimd, hi_done, counts[1])
                    wait_alone(pool, v_in, 16 * (m.n + 1), passed_pool)
                    if order is MIDDLE:
                        wait_alone(pool, pv_done, T_ITEMS * h.n, passed_pool)
                    cut_v(pool, nc.gpsimd, m, hi_done, counts[2])

            nc.gpsimd.memset(beyond[:], 0.0).then_inc(mask_step, 1)
            pool.wait_ge(mask_step, 1)
            nc.gpsimd.affine_select(out=beyond[:], in_=beyond[:], compare_op=ALU.is_ge, fill=FAR, base=0,
                                    pattern=[[-1, P]], channel_multiplier=1).then_inc(mask_step, 1)
            pool.wait_ge(v_cut, 1)
            each_head(pool, run)

        @block.scalar
        def _(act):
            def run(h, order, at):
                ring = blocks = products = 0
                for item in order:
                    kind, slot = item[0], (at.slot + ring) % T_RING
                    if kind == "step" and order is not FIRST:
                        act.wait_ge(fin, QG * h.n + item[1] - QG + 1)
                    elif kind == "exp":
                        i = item[1]
                        n = len(tile_parts(i)) - 1
                        act.wait_ge(scored, at.score + last_item(i))
                        row = p[:, i // 4 % 2, i % 4, 0:(i + 1) * P]
                        nc.scalar.activation(row, row, ACT.Exp, scale=-1.0, bias=low[:, i, n:n + 1],
                                             accum_out=total[:, i // 4, i % 4:i % 4 + 1]).then_inc(p_ready, 1)
                    elif kind == "prep":
                        unit_out(act, h.next(), item[1], slot, at.ring + ring)
                        ring += 1
                    elif kind == "block":
                        _, _, g, kb = item
                        j0 = queries(g, kb)
                        act.wait_ge(t_ready, at.ring + ring + 1)
                        if not (order is FIRST and blocks < 4):
                            act.wait_ge(pv_done, at.block + blocks - 3)
                        nc.scalar.copy(pt_hi[:, blocks % 4, j0:], t_ps[slot][:, j0:]).then_inc(t_hi, 1)
                        ring, blocks = ring + 1, blocks + 1
                    elif kind == "product":
                        products += 1
                    elif kind == "copy":
                        act.wait_ge(pv_done, at.product + products)
                        act.wait_ge(t_ready, at.ring + ring)
                        nc.scalar.copy(ot[:], o_ps[:]).then_inc(o_copied, 1)
                    elif kind == "fold":
                        ring += 1

            for u in range(PREP):
                unit_out(act, first_head, u, u % T_RING, u)
            each_head(act, run)

        @block.vector
        def _(dve):
            def run(h, order, at):
                ring = folds = s = 0
                for item in order:
                    kind, slot = item[0], (at.slot + ring) % T_RING
                    if kind == "step":
                        dve.wait_ge(t_ready, at.ring + ring)
                        if item[1] == 0:
                            dve.wait_ge(cb_in[h.slot], 16 * (h.half + 1))
                    elif kind == "score":
                        _, i, part = item
                        at0, w = sum(tile_parts(i)[:part]), tile_parts(i)[part]
                        start = FAR
                        if part:
                            dve.wait_ge(scored, at.score + s)
                            start = low[:, i, part - 1:part]
                        wait_alone(dve, s_ready, at.score + s + 1, passed_dve)
                        nc.vector.tensor_tensor_reduce(out=p[:, i // 4 % 2, i % 4, at0:at0 + w], in0=s_ps[s % S_RING][:, 0:w],
                                                       in1=cb[:, h.slot, at0:at0 + w], scale=1.0, scalar=start,
                                                       op0=ALU.add, op1=ALU.min,
                                                       accum_out=low[:, i, part:part + 1]).then_inc(scored, 1)
                        s += 1
                    elif kind in ("prep", "block"):
                        ring += 1
                    elif kind == "lo":
                        _, g, kb, unit, n = item
                        j0 = queries(g, kb)
                        dve.wait_ge(t_hi, at.block + n + 1)
                        nc.vector.tensor_tensor(pt_lo[:, n % 4, j0:], t_ps[(at.slot + unit) % T_RING][:, j0:],
                                                pt_hi[:, n % 4, j0:].bitcast(F32), ALU.subtract).then_inc(t_lo, 1)
                    elif kind == "fold":
                        _, before, g = item
                        o = owner(h, before)
                        dve.wait_ge(p_ready, KB * o.n + 4 * g + 4)
                        nc.vector.reciprocal(recip[:, g, :], total[:, g, :]).then_inc(recip_done, 1)
                        dve.wait_ge(recip_done, at.fold + folds + 1)
                        dve.wait_ge(t_ready, at.ring + ring + 1)
                        if g == 0:
                            dve.wait_ge(stored[o.slot], 16 * (START + o.half))
                        nc.vector.tensor_tensor(stage[:, o.slot, 4 * g:4 * g + 4, :],
                                                t_ps[slot][:, 0:4 * FD].rearrange("p (j e) -> p j e", e=FD),
                                                recip[:, g, :].unsqueeze(2).broadcast_to([P, 4, FD]), ALU.mult).then_inc(fin, 1)
                        ring, folds = ring + 1, folds + 1

            nc.vector.tensor_copy(ident_r[:], c["ident"][:]).then_inc(consts_done, 1)
            dve.wait_ge(k_in, 16)
            cut_k(dve, nc.vector, hi_done, 1)
            dve.wait_ge(q_in, 16)
            cut_q(dve, nc.vector, hi_done, 2)
            dve.wait_ge(mask_step, 2)
            nc.vector.tensor_copy(beyond_r[:], beyond[:]).then_inc(consts_done, 1)
            nc.vector.tensor_tensor(fold[:], c["ident"][:, 0:FD], c["ident"][:, FD:P], ALU.add).then_inc(consts_done, 1)
            dve.wait_ge(v_in, 16)
            cut_v(dve, nc.vector, first_head, hi_done, 3)
            each_head(dve, run)

        @block.tensor
        def _(pe):
            bank_read = {"block": t_lo, "prep": u_out, "fold": fin}

            def run(h, order, at):
                s = products = folds = blocks = 0
                units = list(at.recent)
                for item in order:
                    kind, slot = item[0], (at.slot + len(units)) % T_RING
                    if kind in bank_read:
                        old = units[-T_RING]
                        count = units[T_RING:].count(old) - units[-T_RING:].count(old) + 1
                        pe.wait_ge(bank_read[old], {"block": at.block, "prep": at.prep, "fold": at.fold}[old] + count)
                        units.append(kind)
                    if kind == "score":
                        _, i, part = item
                        at0, w = sum(tile_parts(i)[:part]), tile_parts(i)[part]
                        if not (order is FIRST and s < S_RING):
                            pe.wait_ge(scored, at.score + s + 1 - S_RING)
                        if s == 0:
                            pe.wait_ge(u_out, at.prep)
                        tile = slice(i * P, (i + 1) * P)
                        out, keys = s_ps[s % S_RING], kst[:, h.slot, at0:at0 + w]
                        nc.tensor.matmul(out[:, 0:w], q1[:, h.slot, tile], keys, start=True, stop=False)
                        if part == len(tile_parts(i)) - 1:
                            nc.tensor.matmul(out[:, w - P:w], ident_r[:], beyond_r[:], start=False, stop=False)
                        nc.tensor.matmul(out[:, 0:w], q2[:, h.slot, tile], keys, start=False, stop=True).then_inc(s_ready, 1)
                        s += 1
                    elif kind == "prep":
                        unit_in(pe, h.next(), item[1], slot)
                    elif kind == "block":
                        _, before, g, kb = item
                        if kb == 0:
                            pe.wait_ge(p_ready, KB * owner(h, before).n + 4 * g + 4)
                        for j in range(max(0, kb - 4 * g), 4):
                            m = nc.tensor.transpose(t_ps[slot][:, j * P:(j + 1) * P],
                                                    p[:, g % 2, j, kb * P:(kb + 1) * P], c["ident"][:])
                        m.then_inc(t_ready, 1)
                        blocks += 1
                    elif kind == "product":
                        _, before, g, kb = item
                        o, j0 = owner(h, before), queries(g, kb)
                        place = (products - (0 if order is FIRST else LAG)) % 4
                        if kb == 0:
                            pe.wait_ge(v_cut, o.n + 1)
                            if not (order is FIRST and g == 0):
                                pe.wait_ge(o_copied, QG * o.n + g)
                        pe.wait_ge(t_lo, at.product + products + 1)
                        for part in (pt_hi, pt_lo):
                            m = nc.tensor.matmul(o_ps[:, j0:], vcat[:, o.slot, kb, :], part[:, place, j0:],
                                                 start=kb == 0 and part is pt_hi, stop=kb == 4 * g + 3 and part is pt_lo)
                        m.then_inc(pv_done, 1)
                        products += 1
                    elif kind == "fold":
                        _, before, g = item
                        pe.wait_ge(o_copied, QG * owner(h, before).n + g + 1)
                        for j in range(4):
                            m = nc.tensor.matmul(t_ps[slot][:, j * FD:(j + 1) * FD], ot[:, j * P:(j + 1) * P], fold[:],
                                                 start=True, stop=True)
                        m.then_inc(t_ready, 1)

            pe.wait_ge(consts_done, 1)
            for u in range(PREP):
                if u >= T_RING:
                    pe.wait_ge(u_out, u + 1 - T_RING)
                unit_in(pe, first_head, u, u % T_RING)
            pe.wait_ge(consts_done, 3)
            each_head(pe, run)


HT = TT // 2
FC = DFF // BANK
FT = BANK // P
CW = DM // BANK


def mix_and_mlp(nc, ctx, c, inp, mix_in, out):
    NRAW = 4
    PIECES = FC * 16
    OUTS = CW * DT
    ADDS = CW * HT * (1 + FC)
    UPS, DOWNS = 8 * FC, CW * HT * FC

    def sem(name):
        return ctx.enter_context(nc.semaphore("m_" + name))

    names = ("w2_in", "out_stored", "w_hi_done", "w_lo_done", "mix_t", "mt_hi_done", "mt_lo_done", "o_ready", "added",
             "squared", "rstd_step", "scaled", "h_t", "ht_hi_done", "ht_lo_done", "up_ready", "relu_done", "sq_done",
             "u_hi_done", "u_lo_done", "down_ready", "w2_scaled", "out_hi_done", "out_lo_done")
    (w2_in, out_stored, w_hi_done, w_lo_done, mix_t, mt_hi_done, mt_lo_done, o_ready, added, squared, rstd_step, scaled,
     h_t, ht_hi_done, ht_lo_done, up_ready, relu_done, sq_done, u_hi_done, u_lo_done, down_ready, w2_scaled, out_hi_done,
     out_lo_done) = (sem(n) for n in names)
    out_in = [sem(f"out_in{k}") for k in range(4)]
    mix_in_done = [sem(f"mix_in{k}") for k in range(2)]
    raw_in = [sem(f"raw_in{k}") for k in range(NRAW)]
    x_in = [sem(f"x_in{k}") for k in range(HT)]
    with ExitStack() as own:
        def sb(name, shape, dt=F32):
            return own.enter_context(nc.sbuf_tensor("m_" + name, shape, dt))

        ht_hi = sb("ht_hi", [P, DT, HT * P], F32R)
        out_raw, = place_under(nc, ["m_out_raw"], [[P, DT, DM]])
        ht_lo = sb("ht_lo", [P, DT, HT * P], F32R)
        w_hi, w_lo = sb("w_hi", [P, 16, BANK], F32R), sb("w_lo", [P, 16, BANK], F32R)
        acc = sb("acc", [P, HT, DM])
        raw = sb("raw", [P, NRAW, BANK])
        u_hi, u_lo = sb("u_hi", [P, FT, HT * P], F32R), sb("u_lo", [P, FT, HT * P], F32R)
        relu = sb("relu", [P, 2, BANK])
        w2 = sb("w2", [P, DM])
        mixr = sb("mixr", [P, 2, DM])
        ss, rstd = sb("ss", [P, 2, 2]), sb("rstd", [P, 2])
        mt_hi = u_hi[:, 0:2, :].rearrange("p s (d t) -> p s d t", t=P)
        mt_lo = u_lo[:, 0:2, :].rearrange("p s (d t) -> p s d t", t=P)
        h2 = sb("h2", [P, DM])
        up_ps = own.enter_context(nc.psum_tensor("m_up", [P, 4, BANK], F32))
        down_ps = own.enter_context(nc.psum_tensor("m_down", [P, 4, BANK], F32))
        mtp = down_ps[:, 0:2, :].rearrange("p b (d t) -> p (b d) t", t=P)
        htp = down_ps[:, 2:4, :].rearrange("p b (d t) -> p (b d) t", t=P)
        w_out = inp["w_out"].rearrange("l (d p) n -> p (l d) n", p=P)
        w_up = inp["w_up"].rearrange("l (d p) n -> p (l d) n", p=P)
        w_down = inp["w_down"].rearrange("l (f p) n -> p (l f) n", p=P)
        x_tiles = inp["x"].rearrange("b (t p) d -> (b t) p d", p=P)
        out_tiles = out.rearrange("b (t p) d -> (b t) p d", p=P)
        block = own.enter_context(nc.Block())

        def each_chunk(eng, body):
            body(0, False)
            with eng.Fori(1, FC - 1) as f:
                body(f, False)
            body(FC - 1, True)

        def out_piece(m):
            return divmod(m, DT)

        def raw_out(m):
            k, d = out_piece(m)
            return out_raw[:, d, k * BANK:(k + 1) * BANK]

        @block.sync
        def _(sp):
            def load_piece(m, src, r):
                if not (isinstance(m, int) and m < NRAW):
                    sp.wait_ge(w_lo_done, m - NRAW + 1)
                sp.dma_start(raw[:, r, :], src).then_inc(raw_in[r], 16)

            def load_w_out(n):
                k, d = n // 2, n % 2 * 4
                sp.dma_start(out_raw[:, d:d + 4, k * BANK:(k + 1) * BANK],
                             w_out[:, d:d + 4, k * BANK:(k + 1) * BANK]).then_inc(out_in[n], 16)

            def load_mix(half, t):
                n = HT * half + t
                if n >= 2:
                    sp.wait_ge(mix_t, n - 1)
                sp.dma_start(mixr[:, t % 2, :], mix_in[n]).then_inc(mix_in_done[t % 2], 16)

            load_mix(0, 0)
            load_w_out(0)
            load_w_out(1)
            load_mix(0, 1)
            sp.dma_start(w2[:], bcast(inp["norm2_w"], DM)).then_inc(w2_in, 16)
            load_w_out(2)
            load_w_out(3)
            for half in range(2):
                base = PIECES * half
                load_mix(half, 2)
                for t in range(HT):
                    if half:
                        sp.wait_ge(out_stored, 16 * HT)
                    sp.dma_start(acc[:, t, :], x_tiles[HT * half + t]).then_inc(x_in[t], 16)
                    if t + 3 < HT:
                        load_mix(half, t + 3)
                for d in range(DT):
                    load_piece(base + d, w_up[:, d, 0:BANK], d % NRAW)

                def chunk(f, last):
                    for k in range(8):
                        src = w_down[:, bass.ds(f * FT + k // 2, 1), k % 2 * BANK:(k % 2 + 1) * BANK]
                        load_piece(base + 8 + 16 * f + k, src.rearrange("p one n -> p (one n)"), k % NRAW)
                    if not last:
                        for d in range(DT):
                            load_piece(base + 16 + 16 * f + d, w_up[:, d, bass.ds(f * BANK + BANK, BANK)], d % NRAW)
                        return
                    if half == 0:
                        sp.wait_ge(up_ready, UPS)
                        for n in range(4):
                            load_w_out(n)
                        load_mix(1, 0)
                        load_mix(1, 1)
                    for t in range(HT):
                        sp.wait_ge(added, ADDS * half + 16 + 16 * f + 2 * t + 2)
                        sp.dma_start(out_tiles[half * HT + t], acc[:, t, :]).then_inc(out_stored, 16)

                each_chunk(sp, chunk)
            sp.wait_ge(out_stored, 16 * TT)

        @block.gpsimd
        def _(pool):
            def cut_lo(m, s, r):
                pool.wait_ge(w_hi_done, m + 1)
                nc.gpsimd.tensor_tensor(w_lo[:, s, :], raw[:, r, :], w_hi[:, s, :].bitcast(F32), ALU.subtract).then_inc(w_lo_done, 1)

            def tile_rstd(n):
                s = slice(n % 2, n % 2 + 1)
                pool.wait_ge(squared, 2 * n + 2)
                nc.gpsimd.tensor_tensor(rstd[:, s], ss[:, n % 2, 0:1], ss[:, n % 2, 1:2], ALU.add).then_inc(rstd_step, 1)
                pool.wait_ge(rstd_step, 3 * n + 1)
                nc.gpsimd.tensor_tensor(rstd[:, s], rstd[:, s], c["eps_dm"][:], ALU.add).then_inc(rstd_step, 1)
                pool.wait_ge(rstd_step, 3 * n + 2)
                nc.gpsimd.tensor_tensor(rstd[:, s], rstd[:, s], c["neg_half"][:, 0:1], ALU.pow).then_inc(rstd_step, 1)

            for half in range(2):
                base = PIECES * half
                for t in range(HT):
                    tile_rstd(HT * half + t)
                pool.wait_ge(w_lo_done, base + DT)

                def chunk(f, last):
                    for k in range(8):
                        pool.wait_ge(relu_done, UPS * half + 8 * f + k + 1)
                        nc.gpsimd.tensor_tensor(relu[:, k % 2, :], relu[:, k % 2, :], relu[:, k % 2, :], ALU.mult).then_inc(sq_done, 1)
                        cut_lo(base + 8 + 16 * f + k, 8 + k, k % NRAW)
                    for d in range(0 if last else DT):
                        cut_lo(base + 16 + 16 * f + d, d, d % NRAW)

                each_chunk(pool, chunk)

        @block.scalar
        def _(act):
            def cut_hi(s, r, uses):
                act.wait_ge(raw_in[r], 16 * uses)
                nc.scalar.copy(w_hi[:, s, :], raw[:, r, :]).then_inc(w_hi_done, 1)

            def cut_out_hi(half, m):
                act.wait_ge(out_in[m // 4], 16 * (half + 1))
                nc.scalar.copy(w_hi[:, m, :], raw_out(m)).then_inc(out_hi_done, 1)

            def square_tile(half, t):
                n = HT * half + t
                act.wait_ge(added, ADDS * half + 2 * t + 2)
                if n >= 2:
                    act.wait_ge(rstd_step, 3 * (n - 2) + 1)
                for k in range(2):
                    act.wait_ge(squared, 2 * n + k)
                    nc.scalar.activation(relu[:, 0, :], acc[:, t, k * BANK:(k + 1) * BANK], ACT.Square,
                                         accum_out=ss[:, t % 2, k:k + 1]).then_inc(squared, 1)

            def mix_hi(half, t):
                n = HT * half + t
                act.wait_ge(mix_t, n + 1)
                if t >= 2:
                    act.wait_ge(o_ready, 2 * (n - 2) + 2)
                nc.scalar.copy(mt_hi[:, t % 2], mtp).then_inc(mt_hi_done, 1)

            def norm_hi(half, t):
                act.wait_ge(h_t, HT * half + t + 1)
                nc.scalar.copy(ht_hi[:, :, t * P:(t + 1) * P], htp).then_inc(ht_hi_done, 1)

            for half in range(2):
                uses = PIECES // NRAW * half
                mix_hi(half, 0)
                if half:
                    act.wait_ge(down_ready, DOWNS)
                for m in range(8 * half, OUTS):
                    if m == OUTS - 4:
                        mix_hi(half, 1)
                    cut_out_hi(half, m)
                for t in range(HT):
                    if 1 <= t < HT - 1:
                        mix_hi(half, t + 1)
                    if t == HT - 1:
                        act.wait_ge(o_ready, 2 * HT * (half + 1) - 1)
                        for d in range(DT // 2):
                            cut_hi(d, d % NRAW, uses + 1)
                    if t >= 1:
                        norm_hi(half, t - 1)
                    if t == HT - 1:
                        for d in range(DT // 2, DT):
                            cut_hi(d, d % NRAW, uses + 2)
                    square_tile(half, t)
                norm_hi(half, HT - 1)
                act.wait_ge(o_ready, 2 * HT * (half + 1))

                def chunk(f, last):
                    for k in range(8):
                        n = UPS * half + 8 * f + k
                        act.wait_ge(up_ready, n + 1)
                        if not (isinstance(n, int) and n < 2):
                            act.wait_ge(u_lo_done, n - 1 if k >= 1 else n)
                        if isinstance(f, int) and f == 0 and k == 0:
                            act.wait_ge(squared, 2 * HT * (half + 1))
                        nc.scalar.activation(relu[:, k % 2, :], up_ps[:, k % 4, :], ACT.Relu).then_inc(relu_done, 1)
                        if k == 0:
                            act.wait_ge(down_ready, DOWNS * half + 16 * f)
                        cut_hi(8 + k, k % NRAW, uses + 2 + 4 * f + k // NRAW + 1)
                        act.wait_ge(sq_done, n + 1)
                        nc.scalar.copy(u_hi[:, k % 4, k // 4 * BANK:(k // 4 + 1) * BANK], relu[:, k % 2, :]).then_inc(u_hi_done, 1)
                    if not (last and half):
                        act.wait_ge(up_ready, UPS * half + 8 * f + 8)
                        for d in range(DT):
                            if last:
                                cut_out_hi(1, d)
                            else:
                                cut_hi(d, d % NRAW, uses + 4 + 4 * f + d // NRAW + 1)

                each_chunk(act, chunk)

        @block.vector
        def _(dve):
            def mix_lo(half, t):
                dve.wait_ge(mt_hi_done, HT * half + t + 1)
                nc.vector.tensor_tensor(mt_lo[:, t % 2], mtp, mt_hi[:, t % 2].bitcast(F32), ALU.subtract).then_inc(mt_lo_done, 1)

            def cut_out_lo(half, m):
                dve.wait_ge(out_hi_done, OUTS * half + m + 1)
                nc.vector.tensor_tensor(w_lo[:, m, :], raw_out(m), w_hi[:, m, :].bitcast(F32), ALU.subtract).then_inc(out_lo_done, 1)

            def cut_up_lo(half, d):
                dve.wait_ge(w_hi_done, PIECES * half + d + 1)
                nc.vector.tensor_tensor(w_lo[:, d, :], raw[:, d % NRAW, :], w_hi[:, d, :].bitcast(F32),
                                        ALU.subtract).then_inc(w_lo_done, 1)

            def norm_lo(half, t):
                dve.wait_ge(ht_hi_done, HT * half + t + 1)
                tok = slice(t * P, (t + 1) * P)
                nc.vector.tensor_tensor(ht_lo[:, :, tok], htp, ht_hi[:, :, tok].bitcast(F32), ALU.subtract).then_inc(ht_lo_done, 1)

            def add(t, k, bank):
                cols = acc[:, t, k * BANK:(k + 1) * BANK]
                nc.vector.tensor_tensor(cols, cols, bank, ALU.add).then_inc(added, 1)

            def scale_tile(half, t):
                n = HT * half + t
                dve.wait_ge(rstd_step, 3 * n + 3)
                dve.wait_ge(h_t, n)
                nc.vector.scalar_tensor_tensor(h2[:], acc[:, t, :], rstd[:, t % 2:t % 2 + 1], w2[:],
                                               ALU.mult, ALU.mult).then_inc(scaled, 1)

            for half in range(2):
                mix_lo(half, 0)
                for m in range(8 * half, OUTS):
                    if m == OUTS - 4:
                        mix_lo(half, 1)
                    cut_out_lo(half, m)
                if half == 0:
                    dve.wait_ge(w2_in, 16)
                    nc.vector.tensor_scalar(w2[:], w2[:], float(DM) ** 0.5, None, ALU.mult).then_inc(w2_scaled, 1)
                    dve.wait_ge(w2_scaled, 1)
                dve.wait_ge(out_lo_done, OUTS * (half + 1))
                for t in range(HT):
                    if 1 <= t < HT - 1:
                        mix_lo(half, t + 1)
                    if t == HT - 1:
                        if half:
                            dve.wait_ge(w_lo_done, PIECES)
                        for d in range(DT // 2):
                            cut_up_lo(half, d)
                    if t >= 1:
                        norm_lo(half, t - 1)
                    dve.wait_ge(x_in[t], 16 * (half + 1))
                    for k in range(2):
                        dve.wait_ge(o_ready, 2 * (HT * half + t) + k + 1)
                        add(t, k, up_ps[:, (2 * t + k) % 4, :])
                    if t == HT - 1:
                        for d in range(DT // 2, DT):
                            cut_up_lo(half, d)
                    scale_tile(half, t)
                norm_lo(half, HT - 1)

                def chunk(f, last):
                    for k in range(8):
                        dve.wait_ge(u_hi_done, UPS * half + 8 * f + k + 1)
                        tok = slice(k // 4 * BANK, (k // 4 + 1) * BANK)
                        nc.vector.tensor_tensor(u_lo[:, k % 4, tok], relu[:, k % 2, :], u_hi[:, k % 4, tok].bitcast(F32),
                                                ALU.subtract).then_inc(u_lo_done, 1)
                    for t in range(HT):
                        for k in range(CW):
                            n = 16 * f + 2 * t + k
                            dve.wait_ge(added, ADDS * half + n + 1)
                            dve.wait_ge(down_ready, DOWNS * half + n + 1)
                            add(t, k, down_ps[:, (2 * t + k) % 4, :])
                        if last and half == 0:
                            cut_out_lo(1, t)

                each_chunk(dve, chunk)

        @block.tensor
        def _(pe):
            def turn(src, dst):
                for d in range(DT):
                    m = nc.tensor.transpose(dst[:, d, :], src[:, d * P:(d + 1) * P], c["ident"][:])
                return m

            def turn_mix(half, t):
                n = HT * half + t
                pe.wait_ge(mix_in_done[t % 2], 16 * (n // 2 + 1))
                pe.wait_ge(mt_lo_done, n)
                turn(mixr[:, t % 2, :], mtp).then_inc(mix_t, 1)

            def turn_norm(half, t):
                n = HT * half + t
                pe.wait_ge(scaled, n + 1)
                pe.wait_ge(ht_lo_done, n)
                turn(h2[:], htp).then_inc(h_t, 1)

            for half in range(2):
                if half:
                    pe.wait_ge(added, ADDS - 2)
                turn_mix(half, 0)
                for t in range(HT):
                    if t + 1 < HT:
                        turn_mix(half, t + 1)
                    pe.wait_ge(mt_lo_done, HT * half + t + 1)
                    for k in range(2):
                        if t >= 2:
                            pe.wait_ge(added, ADDS * half + 2 * t + k - 3)
                        for d in range(DT):
                            s = DT * k + d
                            if t == 0:
                                pe.wait_ge(out_lo_done, OUTS * half + s + 1)
                            m = three_pass(nc, up_ps[:, (2 * t + k) % 4, :], mt_hi[:, t % 2, d, :], mt_lo[:, t % 2, d, :],
                                           w_hi[:, s, :], w_lo[:, s, :], d == 0, d == DT - 1)
                        m.then_inc(o_ready, 1)
                    if t >= 1:
                        turn_norm(half, t - 1)

                def chunk(f, last):
                    first = isinstance(f, int) and f == 0
                    for k in range(8):
                        n = UPS * half + 8 * f + k
                        if first and k < 4:
                            pe.wait_ge(added, ADDS * half + 2 * HT - 3 + k)
                            pe.wait_ge(ht_lo_done, HT * half + 4)
                        else:
                            pe.wait_ge(relu_done, n - 3 if k >= 3 else n - k)
                        if first and k == 2:
                            turn_norm(half, HT - 1)
                        elif first and k == 4:
                            pe.wait_ge(ht_lo_done, HT * (half + 1))
                        tok, hid = slice(k // 4 * BANK, (k // 4 + 1) * BANK), slice(k % 4 * P, k % 4 * P + P)
                        for d in range(DT):
                            if k == 0:
                                pe.wait_ge(w_lo_done, PIECES * half + 16 * f + d + 1)
                            m = three_pass(nc, up_ps[:, k % 4, :], w_hi[:, d, hid], w_lo[:, d, hid], ht_hi[:, d, tok],
                                           ht_lo[:, d, tok], d == 0, d == DT - 1)
                        m.then_inc(up_ready, 1)
                    for t in range(HT):
                        tok = slice(t * P, (t + 1) * P)
                        for k in range(CW):
                            n = 16 * f + 2 * t + k
                            if t % 4 == 0 and k == 0:
                                pe.wait_ge(u_lo_done, UPS * half + 8 * f + t + 4)
                            pe.wait_ge(added, ADDS * half + 16 + n - 3)
                            for i in range(FT):
                                s = 8 + 2 * i + k
                                if t == 0:
                                    pe.wait_ge(w_lo_done, PIECES * half + 16 * f + s + 1)
                                m = three_pass(nc, down_ps[:, (2 * t + k) % 4, :], u_hi[:, i, tok], u_lo[:, i, tok],
                                               w_hi[:, s, :], w_lo[:, s, :], i == 0, i == FT - 1)
                            m.then_inc(down_ready, 1)

                each_chunk(pe, chunk)


def build(nc, inp, out):
    with ExitStack() as ctx:
        c = constants(nc, ctx)
        tok = nc.dram_tensor("tok_major", (NT, TT, P, BANK), F32, kind="Internal").ap()
        chan = nc.dram_tensor("chan_major", (2, HH, P, S), F32, kind="Internal").ap()
        cum = nc.dram_tensor("cum_gates", (FH, S), F32, kind="Internal").ap()
        mix = nc.dram_tensor("mixed", (TT, P, DM), F32, kind="Internal").ap()
        project(nc, ctx, c, inp, tok, chan, cum)
        recurrence(nc, ctx, c, tok, chan, mix)
        attention(nc, ctx, c, tok, cum, mix)
        mix_and_mlp(nc, ctx, c, inp, mix, out)


_INS = ["x", "lower_bounds", "norm1_w", "w_in", "fox_f_bias", "q_norm_w", "k_norm_w", "hgrn_norm_w", "w_out",
        "norm2_w", "w_up", "w_down"]


def kernel(**inputs):
    import numpy as _np
    import concourse.bacc as _bacc
    from concourse.bass_utils import run_bass_kernel_spmd as _run

    nc = _bacc.Bacc("TRN2", target_bir_lowering=False, num_devices=1, dynamic_dma_scratch_size=1024)
    arrays, args = {}, {}
    for name in _INS:
        a = _np.ascontiguousarray(inputs[name])
        arrays[f"in_{name}"] = a
        args[name] = nc.dram_tensor(f"in_{name}", a.shape, mybir.dt.from_np(a.dtype), kind="ExternalInput").ap()
    out = nc.dram_tensor("out_0", (1, S, DM), F32, kind="ExternalOutput").ap()
    build(nc, args, out)
    r = _run(nc, [arrays], core_ids=[0])
    return r.results[0]["out_0"]
```
